# Optimizing a Trainium2 kernel written in Bass

```python
import math
import jax, jax.numpy as jnp
from jax import lax
import numpy as np

D_MODEL = 1024
BATCH = 1
SEQ = 512
DEPTH = 1

HEAD_DIM = 64
N_HEADS = D_MODEL // HEAD_DIM
SB_HEADS = N_HEADS // 4
SWA_HEADS = N_HEADS // 2
SWA_KV_HEADS = SWA_HEADS // 4
MOBA_HEADS = N_HEADS - SB_HEADS - SWA_HEADS
SB_W = SB_HEADS * HEAD_DIM
SWA_W = SWA_HEADS * HEAD_DIM
SWA_KV_W = SWA_KV_HEADS * HEAD_DIM
MOBA_W = MOBA_HEADS * HEAD_DIM
MIX_W = SB_W + SWA_W + MOBA_W
IN_W = 3 * SB_W + SWA_W + 2 * SWA_KV_W + 3 * MOBA_W
Q_BLOCK = 128
WINDOW = 128
MOBA_BLOCK = 256
MOBA_TOPK = 3
NUM_BUCKETS = 32
MAX_DISTANCE = 128
BIAS_HEADS = SWA_HEADS + MOBA_HEADS
N_EXPERTS = 32
TOP_K = 4
D_FF = D_MODEL
SWIGLU_LIMIT = 7.0
SWIGLU_ALPHA = 1.702
MOE_BLOCK = 256
EPS = 1e-6
NEG = -1e30

kernel_name = "hymba_style_sb_swa_moba_moe_trunk"

def rms_norm(x, g):
    xf = x.astype(jnp.float32)
    y = xf * lax.rsqrt(jnp.mean(xf * xf, axis=-1, keepdims=True) + EPS)
    return (y * g.astype(jnp.float32)).astype(x.dtype)

def t5_bucket(dist):
    n = jnp.maximum(dist, 0)
    max_exact = NUM_BUCKETS // 2
    nf = jnp.maximum(n, 1).astype(jnp.float32)
    large = max_exact + (jnp.log(nf / max_exact) / math.log(MAX_DISTANCE / max_exact)
                         * (NUM_BUCKETS - max_exact)).astype(jnp.int32)
    large = jnp.minimum(large, NUM_BUCKETS - 1)
    return jnp.where(n < max_exact, n, large)

def stick_breaking_attention(q, k, v):
    B, H, S, d = q.shape
    nq = S // Q_BLOCK
    scale = d ** -0.5
    qb = q.reshape(B, H, nq, Q_BLOCK, d).transpose(2, 0, 1, 3, 4)
    key_pos = jnp.arange(S)

    def block(args):
        i, qi = args
        t = i * Q_BLOCK + jnp.arange(Q_BLOCK)
        z = jnp.einsum('bhqd,bhkd->bhqk', qi, k, preferred_element_type=jnp.float32) * scale
        strict = key_pos[None, :] < t[:, None]
        log_1m = jnp.where(strict, jax.nn.log_sigmoid(-z), 0.0)
        later = lax.cumsum(log_1m, axis=3, reverse=True) - log_1m
        a = jnp.where(strict, jnp.exp(jax.nn.log_sigmoid(z) + later), 0.0)
        return jnp.einsum('bhqk,bhkd->bhqd', a.astype(v.dtype), v)

    out = lax.map(block, (jnp.arange(nq), qb))
    return out.transpose(1, 0, 3, 2, 4).reshape(B, S, H * d)

def sliding_window_attention(q, k, v, sinks, table):
    B, S, Hq, d = q.shape
    Hkv = k.shape[2]
    G = Hq // Hkv
    nq = S // Q_BLOCK
    scale = d ** -0.5
    qb = q.reshape(B, nq, Q_BLOCK, Hkv, G, d)

    def banded(a):
        ap = jnp.pad(a, ((0, 0), (Q_BLOCK, 0), (0, 0), (0, 0))).reshape(B, nq + 1, Q_BLOCK, Hkv, d)
        return jnp.concatenate([ap[:, :-1], ap[:, 1:]], axis=2)

    kw, vw = banded(k), banded(v)
    i = jnp.arange(Q_BLOCK)[:, None]
    j = jnp.arange(2 * Q_BLOCK)[None, :]
    dist = Q_BLOCK + i - j
    key_pos = (jnp.arange(nq)[:, None, None] - 1) * Q_BLOCK + j
    valid = (dist >= 0) & (dist < WINDOW) & (key_pos >= 0)
    bias = table[t5_bucket(dist)].transpose(2, 0, 1).reshape(Hkv, G, Q_BLOCK, 2 * Q_BLOCK)
    s = jnp.einsum('bnqhgd,bnkhd->bnhgqk', qb, kw, preferred_element_type=jnp.float32) * scale
    s = jnp.where(valid[None, :, None, None], s + bias.astype(jnp.float32), NEG)
    sink = jnp.broadcast_to(sinks.astype(jnp.float32).reshape(1, 1, Hkv, G, 1, 1), s.shape[:-1] + (1,))
    p = jax.nn.softmax(jnp.concatenate([s, sink], axis=-1), axis=-1)[..., :-1]
    out = jnp.einsum('bnhgqk,bnkhd->bnqhgd', p.astype(v.dtype), vw)
    return out.reshape(B, S, Hq * d)

def moba_attention(q, k, v, table):
    B, H, S, d = q.shape
    nq = S // Q_BLOCK
    nb = -(-S // MOBA_BLOCK)
    n_sel = min(MOBA_TOPK, nb)
    scale = d ** -0.5
    padlen = nb * MOBA_BLOCK - S
    kb = jnp.pad(k, ((0, 0), (0, 0), (0, padlen), (0, 0))).reshape(B, H, nb, MOBA_BLOCK, d)
    vb = jnp.pad(v, ((0, 0), (0, 0), (0, padlen), (0, 0))).reshape(B, H, nb, MOBA_BLOCK, d)
    k_mean = jnp.mean(kb.astype(jnp.float32), axis=3).astype(k.dtype)
    qb = q.reshape(B, H, nq, Q_BLOCK, d).transpose(2, 0, 1, 3, 4)
    bi = jnp.arange(B)[:, None, None, None]
    hi = jnp.arange(H)[None, :, None, None]
    table_t = table.T
    j = jnp.arange(MOBA_BLOCK)

    def block(args):
        i, qi = args
        t = i * Q_BLOCK + jnp.arange(Q_BLOCK)
        cur = (i * Q_BLOCK) // MOBA_BLOCK
        gate = jnp.einsum('bhqd,bhnd->bhqn', qi, k_mean, preferred_element_type=jnp.float32)
        gate = jnp.where(jnp.arange(nb) < cur, gate, NEG)
        _, sel = lax.top_k(gate, n_sel)
        sel_ok = sel < cur
        kg = kb[bi, hi, sel]
        vg = vb[bi, hi, sel]
        sg = jnp.einsum('bhqd,bhqnkd->bhqnk', qi, kg, preferred_element_type=jnp.float32) * scale
        dist_g = t[None, None, :, None, None] - (sel[..., None] * MOBA_BLOCK + j)
        sg = sg + table_t[hi[..., None], t5_bucket(dist_g)].astype(jnp.float32)
        sg = jnp.where(sel_ok[..., None], sg, NEG).reshape(B, H, Q_BLOCK, n_sel * MOBA_BLOCK)
        ko = lax.dynamic_index_in_dim(kb, cur, axis=2, keepdims=False)
        vo = lax.dynamic_index_in_dim(vb, cur, axis=2, keepdims=False)
        so = jnp.einsum('bhqd,bhkd->bhqk', qi, ko, preferred_element_type=jnp.float32) * scale
        dist_o = t[:, None] - (cur * MOBA_BLOCK + j)[None, :]
        so = so + table_t[:, t5_bucket(dist_o)].astype(jnp.float32)
        so = jnp.where(dist_o >= 0, so, NEG)
        p = jax.nn.softmax(jnp.concatenate([sg, so], axis=-1), axis=-1)
        pg = p[..., :n_sel * MOBA_BLOCK].reshape(B, H, Q_BLOCK, n_sel, MOBA_BLOCK)
        po = p[..., n_sel * MOBA_BLOCK:]
        return (jnp.einsum('bhqnk,bhqnkd->bhqd', pg.astype(v.dtype), vg)
                + jnp.einsum('bhqk,bhkd->bhqd', po.astype(v.dtype), vo))

    out = lax.map(block, (jnp.arange(nq), qb))
    return out.transpose(1, 0, 3, 2, 4).reshape(B, S, H * d)

def token_mixer(h, w_in, w_out, g_group, sinks, rel_bias):
    B, S, _ = h.shape
    proj = h @ w_in
    widths = [SB_W] * 3 + [SWA_W, SWA_KV_W, SWA_KV_W] + [MOBA_W] * 3
    cuts = [int(c) for c in np.cumsum(widths)[:-1]]
    sb_q, sb_k, sb_v, sw_q, sw_k, sw_v, mb_q, mb_k, mb_v = jnp.split(proj, cuts, axis=-1)

    def heads(a, n):
        return a.reshape(B, S, n, HEAD_DIM).transpose(0, 2, 1, 3)

    o_sb = stick_breaking_attention(heads(sb_q, SB_HEADS), heads(sb_k, SB_HEADS), heads(sb_v, SB_HEADS))
    o_sw = sliding_window_attention(sw_q.reshape(B, S, SWA_HEADS, HEAD_DIM),
                                    sw_k.reshape(B, S, SWA_KV_HEADS, HEAD_DIM),
                                    sw_v.reshape(B, S, SWA_KV_HEADS, HEAD_DIM),
                                    sinks, rel_bias[:, :SWA_HEADS])
    o_mb = moba_attention(heads(mb_q, MOBA_HEADS), heads(mb_k, MOBA_HEADS), heads(mb_v, MOBA_HEADS),
                          rel_bias[:, SWA_HEADS:])
    merged = jnp.concatenate([
        rms_norm(o_sb, g_group[:SB_W]),
        rms_norm(o_sw, g_group[SB_W:SB_W + SWA_W]),
        rms_norm(o_mb, g_group[SB_W + SWA_W:]),
    ], axis=-1)
    return merged @ w_out

def moe_ffn(h, w_router, b_router, w_gate_up, b_gate_up, w_down, b_down):
    B, S, D = h.shape
    n_tok = B * S
    hf = h.reshape(n_tok, D)
    logits = jnp.dot(hf, w_router, preferred_element_type=jnp.float32) + b_router.astype(jnp.float32)
    top_logit, top_e = lax.top_k(logits, TOP_K)
    weights = jax.nn.softmax(top_logit, axis=-1).astype(h.dtype)
    n_assign = n_tok * TOP_K
    flat_e = top_e.reshape(n_assign)
    flat_tok = jnp.arange(n_assign, dtype=jnp.int32) // TOP_K
    order = jnp.argsort(flat_e)
    e_sorted = flat_e[order]
    counts = jnp.bincount(flat_e, length=N_EXPERTS)
    padded = (counts + MOE_BLOCK - 1) // MOE_BLOCK * MOE_BLOCK
    start = jnp.cumsum(counts) - counts
    pad_end = jnp.cumsum(padded)
    pad_start = pad_end - padded
    dest = pad_start[e_sorted] + jnp.arange(n_assign) - start[e_sorted]
    n_rows = (-(-n_assign // MOE_BLOCK) + N_EXPERTS) * MOE_BLOCK
    n_blocks = n_rows // MOE_BLOCK
    row_tok = jnp.zeros((n_rows,), jnp.int32).at[dest].set(flat_tok[order])
    row_w = jnp.zeros((n_rows,), h.dtype).at[dest].set(weights.reshape(n_assign)[order])
    block_e = jnp.minimum(jnp.searchsorted(pad_end, jnp.arange(n_blocks) * MOE_BLOCK, side='right'),
                          N_EXPERTS - 1)
    xs = hf[row_tok].reshape(n_blocks, MOE_BLOCK, D)

    def expert_block(args):
        xb, e = args
        gu = xb @ w_gate_up[e] + b_gate_up[e]
        gate = jnp.minimum(gu[:, :D_FF], SWIGLU_LIMIT)
        up = jnp.clip(gu[:, D_FF:], -SWIGLU_LIMIT, SWIGLU_LIMIT)
        act = (up + 1.0) * gate * jax.nn.sigmoid(SWIGLU_ALPHA * gate)
        return act @ w_down[e] + b_down[e]

    ys = lax.map(expert_block, (xs, block_e)).reshape(n_rows, D)
    out = jnp.zeros((n_tok, D), h.dtype).at[row_tok].add(ys * row_w[:, None])
    return out.reshape(B, S, D)

def setup_inputs(seed: int = 0) -> dict:
    key = jax.random.key(seed)
    ks = jax.random.split(key, 20)
    f32 = jnp.float32
    nrm = lambda k, shape, s: jax.random.normal(k, shape, f32) * s
    return {
        "x": nrm(ks[0], (BATCH, SEQ, D_MODEL), 1.0),
        "c": nrm(ks[1], (BATCH, D_MODEL), 1.0),
        "w_in": nrm(ks[2], (DEPTH, D_MODEL, IN_W), D_MODEL ** -0.5),
        "w_out": nrm(ks[3], (DEPTH, MIX_W, D_MODEL), MIX_W ** -0.5),
        "g_norm_mix": 1.0 + nrm(ks[4], (DEPTH, D_MODEL), 0.1),
        "g_norm_ffn": 1.0 + nrm(ks[5], (DEPTH, D_MODEL), 0.1),
        "g_group": 1.0 + nrm(ks[6], (DEPTH, MIX_W), 0.1),
        "w_mod": nrm(ks[7], (DEPTH, D_MODEL, 6 * D_MODEL), 0.5 * D_MODEL ** -0.5),
        "b_mod": nrm(ks[8], (DEPTH, 6 * D_MODEL), 0.02),
        "swa_sinks": nrm(ks[9], (DEPTH, SWA_HEADS), 1.0),
        "rel_bias": nrm(ks[10], (NUM_BUCKETS, BIAS_HEADS), 0.5),
        "w_router": nrm(ks[11], (DEPTH, D_MODEL, N_EXPERTS), D_MODEL ** -0.5),
        "b_router": nrm(ks[12], (DEPTH, N_EXPERTS), 0.01),
        "w_gate_up": nrm(ks[13], (DEPTH, N_EXPERTS, D_MODEL, 2 * D_FF), D_MODEL ** -0.5),
        "b_gate_up": nrm(ks[14], (DEPTH, N_EXPERTS, 2 * D_FF), 0.02),
        "w_down": nrm(ks[15], (DEPTH, N_EXPERTS, D_FF, D_MODEL), D_FF ** -0.5),
        "b_down": nrm(ks[16], (DEPTH, N_EXPERTS, D_MODEL), 0.02),
        "g_final": 1.0 + nrm(ks[17], (D_MODEL,), 0.1),
    }

def reference(x, c, w_in, w_out, g_norm_mix, g_norm_ffn, g_group, w_mod, b_mod, swa_sinks,
              rel_bias, w_router, b_router, w_gate_up, b_gate_up, w_down, b_down, g_final):
    c_act = jax.nn.silu(c)
    for l in range(DEPTH):
        mod = (c_act @ w_mod[l] + b_mod[l])[:, None, :]
        sh1, sc1, gt1, sh2, sc2, gt2 = jnp.split(mod, 6, axis=-1)
        h = rms_norm(x, g_norm_mix[l]) * (1.0 + sc1) + sh1
        x = x + gt1 * token_mixer(h, w_in[l], w_out[l], g_group[l], swa_sinks[l], rel_bias)
        h = rms_norm(x, g_norm_ffn[l]) * (1.0 + sc2) + sh2
        x = x + gt2 * moe_ffn(h, w_router[l], b_router[l], w_gate_up[l], b_gate_up[l],
                              w_down[l], b_down[l])
    return rms_norm(x, g_final)


_drawn_inputs = setup_inputs


def setup_inputs(seed=0):
    import zlib

    import numpy as np

    out = dict(_drawn_inputs(seed))
    spreads = {}
    factors = {'swa_sinks': 4.415, 'b_router': 5.638, 'b_gate_up': 8.0, 'b_down': 8.0}
    for name, (base, spread) in spreads.items():
        noise = np.random.default_rng([zlib.crc32(name.encode()), seed]).standard_normal(out[name].shape)
        drawn = base * np.exp(spread * noise) if base else spread * noise
        out[name] = __import__('jax').numpy.asarray(drawn.astype(out[name].dtype))
    for name, factor in factors.items():
        out[name] = (out[name] * factor).astype(out[name].dtype)
    return out
```

```python
from contextlib import ExitStack

import numpy as np

import concourse.bass as bass
from concourse import mybir

F32 = mybir.dt.float32
F32R = mybir.dt.float32r
I32 = mybir.dt.int32
U32 = mybir.dt.uint32
ALU = mybir.AluOpType
ACT = mybir.ActivationFunctionType
AX = mybir.AxisListType.X

P = 128
D = 1024
T = 512
NT = T // P
C = D // P
HD = 64
E = 32
TOPK = 4
BUCKETS = 32
EPS = 1e-6
NEG = -1e30
LIMIT = 7.0
ALPHA = 1.702
MAX_TILES = T * TOPK // P + E - 1
BAND = 384

SB_Q, SB_K, SB_V, SW_Q, SW_K, SW_V, MB_Q, MB_K, MB_V, IN_W = 0, 256, 512, 768, 1280, 1408, 1536, 1792, 2048, 2304

Q_COLS = [SB_Q, SB_Q + P, SB_K, SB_K + P, *range(SW_Q, SW_K, P), SW_K, MB_Q, MB_Q + P, MB_K, MB_K + P]
UNITS = [("sb", 0), ("sw", 0), ("mb", 0), ("sw", 1), ("sb", 1), ("sw", 2), ("mb", 1), ("sw", 3),
         ("sb", 2), ("sw", 4), ("mb", 2), ("sw", 5), ("sb", 3), ("sw", 6), ("mb", 3), ("sw", 7)]
SOFT_UNITS = sum(kind != "sb" for kind, _ in UNITS)
ROWS = [("gt1", 2), ("sc2", 4), ("sh2", 3), ("gt2", 5)]
RING = 6
CHUNKS = 12


def dist_tables():
    d = 255 - np.arange(BAND)
    n = np.maximum(d, 0)
    exact = BUCKETS // 2
    nf = np.maximum(n, 1).astype(np.float32)
    large = exact + (np.log(nf / np.float32(exact)) / np.float32(np.log(128 / exact))
                     * np.float32(BUCKETS - exact)).astype(np.int32)
    bucket = np.where(n < exact, n, np.minimum(large, BUCKETS - 1))
    onehot = (bucket[None, :] == np.arange(BUCKETS)[:, None]).astype(np.float32)
    masks = np.zeros((12, BAND), np.float32)
    masks[:, d < 0] = NEG
    masks[:8, d >= 128] = NEG
    return onehot, masks


def build(nc, x, c, w_in, w_out, g_mix, g_ffn, g_group, w_mod, b_mod, sinks, table, w_router, b_router,
          w_gate_up, b_gate_up, w_down, b_down, g_final, onehot, masks, out):
    band_dram = nc.dram_tensor("band_dram", (12, P, BAND), F32, kind="Internal").ap()
    ys = nc.dram_tensor("ys", ((MAX_TILES + 1) * P, D), F32, kind="Internal").ap()

    ctx = ExitStack()
    with ctx:
        BASE = 16896

        def at(name, kb, shape, dt=F32):
            return nc.alloc_sbuf_tensor_at(name, shape, dt, offset=BASE + int(kb * 1024))

        def sem(name):
            return ctx.enter_context(nc.semaphore(name))

        PS = ctx.enter_context(nc.psum_tensor("PS", [P, 8, 512], F32))
        PSF = PS[:].rearrange("p b n -> p (b n)")

        X = at("X", 0, [P, NT, D])
        RINGB = at("RINGB", 16, [P, RING, 2048])
        WIN = at("WIN", 16, [P, C, IN_W])
        WOUT = at("WOUT", 32, [P, C, D])
        MERG = at("MERG", 64, [P, NT, D])
        UB1 = [at("UA1", 176, [P, 2048]), at("UB1", 184, [P, 2048])]
        UB2 = [at("UA2", 80, [P, 2048]), at("UB2", 16, [P, 2048])]
        BROW = at("BROW", 24, [1, 2, 512])
        ROW = {"sc2": at("SC2", 88, [P, D]), "sh2": at("SH2", 92, [P, D]),
               "gt1": at("GT1", 196, [P, D]), "gt2": at("GT2", 200, [P, D])}
        MB = at("MB", 96, [P, 2, C, 512])
        QKT = at("QKT", 128, [P, 13, T])
        KSW = at("KSW", 28, [P, T])
        ZERO = at("ZERO", 30, [P, 512])
        V = at("V", 154, [P, NT, 640])
        HT = at("HT", 164, [P, C, T])
        XN = at("XN", 180, [P, NT, D])
        BT = at("BT", 164, [P, 12, 256])
        CSB = at("CSB", 192, [P, C, P])
        MT = at("MT", 128, [P, C, T])
        MTF = MT[:].rearrange("p c t -> p (c t)").rearrange("p (t d) -> p t d", t=NT)
        XN2 = at("XN2", 64, [P, NT, D])
        H2T = at("H2T", 96, [P, C, T])
        BW = at("BW", 164, [64, 3 * D])
        BHT = at("BHT", 176, [64, 3 * D], F32R)
        BR = at("BR", 144, [64, 3 * D], F32R)
        WH = at("WH", 64, [P, 3, 2048], F32R)
        WL = at("WL", 88, [P, 3, 2048], F32R)
        H2H = at("H2H", 112, [P, NT, D], F32R)
        H2L = at("H2L", 128, [P, NT, D], F32R)
        XH = at("XH", 156, [P, C, P], F32R)
        XL = at("XL", 160, [P, C, P], F32R)
        AH = at("AH", 164, [P, 2, 4, P], F32R)
        AL = at("AL", 168, [P, 2, 4, P], F32R)
        Y = at("Y", 172, [P, D])
        GC = at("GC", 180, [P, 512])
        UC = at("UC", 182, [P, 512])
        SG = at("SG", 184, [P, 512])
        AC = at("AC", 186, [P, 2, 512])
        S = at("S", 190, [P, NT, P], F32R)
        SEL = at("SEL", 192, [64, P], F32R)
        GM = at("GM", 192.5, [P, NT, E])
        IOTA = at("IOTA", 193, [P, P])
        ID2 = at("ID2", 193.5, [64, E])
        WJ = at("WJ", 193.75, [P, NT, 8])
        SI = at("SI", 193.9375, [P, NT, TOPK], U32)
        GMC = at("GMC", 194, [P, NT])
        TILE_P = at("TILE_P", 194.03125, [P, 1])
        TILE0 = at("TILE0", 194.3125, [P, 1])
        GMS = at("GMS", 194.34375, [P, NT])
        TILE_E = at("TILE_E", 194.0625, [1, 48], I32)
        LAST = at("LAST", 194.25, [1, 8], I32)
        WR = at("WR", 194.5, [P, C, E])
        BRT = at("BRT", 195.5, [P, E])
        ID = at("ID", 204, [P, P])
        NTRI = at("NTRI", 204.5, [P, P])
        NONE_ = at("NONE", 205, [P, P])
        ONES = at("ONES", 205.5, [P, P])
        SLT = at("SLT", 206, [P, P])
        SMALL = at("SMALL", 206.5, [P, 216])
        BANDH = at("BANDH", 88, [BUCKETS, BAND])
        BANDM = at("BANDM", 89.5, [12, BAND])
        BANDS = at("BANDS", 91, [12, BAND])
        GFFN = at("GFFN", 96, [P, D])
        TMP = [at("TMP0", 100, [P, D]), at("TMP1", 104, [P, D])]
        RT = at("RT", 156, [P, 32, P])

        def rt(a, b=0, t=NT):
            return RT[:, a, 0:b or P].rearrange("p (t e) -> p t e", t=t)

        L, M8, IF, LM, EXPJ = rt(0), rt(1, 32), rt(3, 32), rt(4, 32), rt(5, 32)
        I8 = RT[:, 2, 0:32].bitcast(U32).rearrange("p (t e) -> p t e", t=NT)
        OH = RT[:, 6:10, :].rearrange("p b (j e) -> p b j e", e=E)
        MK2, MK3, SLOT, MASK = rt(10), rt(11), rt(12), rt(16)
        SUM4 = RT[:, 13, 0:NT]
        CNT, TL, TSTART = RT[:, 13, 32:64], RT[:, 13, 64:96], RT[:, 13, 96:128]
        TEND = [RT[:, 14, 0:32], RT[:, 14, 32:64]]
        SJ = RT[:, 14, 64:80].rearrange("p (t j) -> p t j", t=NT)
        TE = RT[0:1, 14, 80:128]
        IOTAE = RT[:, 15, 0:E]
        IOTA48 = RT[0:1, 15, 64:112]
        TT = RT[0:1, 17:29, :].rearrange("p b n -> p (b n)").rearrange("p (i e) -> p i e", e=E)
        GR = at("GR", 64, [P, 8, D])
        AC2 = at("AC2", 96, [P, NT, D])
        GF = at("GF", 112, [P, D])
        FJ = at("FJ", 116, [P, NT, D])

        _o = [0]

        def small(n):
            _o[0] += n
            return SMALL[:, _o[0] - n:_o[0]]

        cT, cS, gmixc, ggrc, bsc, bsh = (small(C) for _ in range(6))
        G1, SH1 = small(C), small(C)
        ss, rs = small(4), small(4)
        gss, grs = small(12), small(12)
        sinkb = small(8)
        farb = small(4)
        mx = [small(4), small(4)]
        negm = [small(4), small(4)]
        den = [small(4), small(4)]
        esink = [small(4), small(4)]
        rden = [small(4), small(4)]
        sg = small(C)
        BANDT = small(12)[0:BUCKETS]

        consts = sem("consts")
        x_in, c_in, win_in, band_in = sem("x_in"), sem("c_in"), sem("win_in"), sem("band_in")
        swap_in = sem("swap_in")
        wout_in, wr_in, bias_in, misc_in = sem("wout_in"), sem("wr_in"), sem("bias_in"), sem("misc_in")
        mod_in = [sem("mod_in0"), sem("mod_in1")]
        act_step, dve_step, pool_step = sem("act_step"), sem("dve_step"), sem("pool_step")
        mod_used, rows_kept = sem("mod_used"), sem("rows_kept")
        dve_mean, ys_ready, g_ffn_in, iotas, sum_ready = (sem("dve_mean"), sem("ys_ready"), sem("g_ffn_in"),
                                                          sem("iotas"), sem("sum_ready"))
        c_silu, c_wide = sem("c_silu"), sem("c_wide")
        squares, roots, xn_ready = sem("squares"), sem("roots"), sem("xn_ready")
        turned, kept = sem("turned"), sem("kept")
        proj_done, q_kept, v_kept = sem("proj_done"), sem("q_kept"), sem("v_kept")
        band_done, band_kept, band_out = sem("band_done"), sem("band_kept"), sem("band_out")
        scores_done, set_free, pv_done = sem("scores_done"), sem("set_free"), sem("pv_done")
        logs_ready, drop_ready, drop_masked = sem("logs_ready"), sem("drop_ready"), sem("drop_masked")
        sums_done, stick_ready, stick_masked = sem("sums_done"), sem("stick_ready"), sem("stick_masked")
        max_ready, probs_ready, probs_turned, pt_kept = (sem("max_ready"), sem("probs_ready"), sem("probs_turned"),
                                                         sem("pt_kept"))
        wout_done, wout_kept = sem("wout_done"), sem("wout_kept")
        logits_done, mask_ready, ranks_done = sem("logits_done"), sem("mask_ready"), sem("ranks_done")
        routed, h2_split, bias_split = sem("routed"), sem("h2_split"), sem("bias_split")
        ring_in = [sem(f"ring_in{s}") for s in range(RING)]
        hi_done, lo_done, pe_chunk = sem("hi_done"), sem("lo_done"), sem("pe_chunk")
        gu_done, act_turned, gathered, sel_used = sem("gu_done"), sem("act_turned"), sem("gathered"), sem("sel_used")
        gate_ready, up_ready, sig_ready, act_ready = (sem("gate_ready"), sem("up_ready"), sem("sig_ready"),
                                                      sem("act_ready"))
        ah_ready, al_ready, xh_ready, xl_ready = sem("ah_ready"), sem("al_ready"), sem("xh_ready"), sem("xl_ready")
        y_kept, y_stored = sem("y_kept"), sem("y_stored")
        gated_up, zeros, cols_ready = sem("gated_up"), sem("zeros"), sem("cols_ready")
        s_ready, sel_ready, tile_step = sem("s_ready"), sem("sel_ready"), sem("tile_step")
        rows_in = [sem(f"rows_in{s}") for s in range(8)]
        rows_used, final_ready, stored = sem("rows_used"), sem("final_ready"), sem("stored")

        block = ctx.enter_context(nc.Block())

        x_v = x[0].rearrange("(t p) d -> p t d", p=P)
        out_v = out[0].rearrange("(t p) d -> p t d", p=P)
        wmod_v = w_mod[0].rearrange("(p k) (v h n) -> v h p k n", p=P, v=6, h=2)
        bmod_v = b_mod[0].rearrange("(v h a n) -> v h a n", v=6, h=2, a=1)
        gu_v = w_gate_up.rearrange("l e (p k) (g h n) -> (l e) h p (k g) n", p=P, g=2, h=2)
        down_v = w_down.rearrange("l e (h p q r) n -> (l e) h q p (r n)", h=2, p=P, q=2)

        def col8(v):
            return v.rearrange("(p k) -> p k", k=C)

        def rep(v, n):
            return v.rearrange("(a n) -> a n", a=1).broadcast_to([P, n])

        def nth(u, *kinds):
            return sum(k in kinds for k, _ in UNITS[:u + 1])

        def sb_blocks():
            return [(qt, kt) for qt in range(NT) for kt in range(qt + 1)]

        def sw_blocks():
            return [(qt, kt) for qt in range(NT) for kt in ((qt - 1, qt) if qt else (0,))]

        @block.sync
        def _(sp):
            sp.dma_start(cT, col8(c[0])).then_inc(c_in, 16)
            sp.dma_start(gmixc, col8(g_mix[0])).then_inc(c_in, 16)
            sp.dma_start(bsh, col8(b_mod[0, 0:D])).then_inc(c_in, 16)
            sp.dma_start(bsc, col8(b_mod[0, D:2 * D])).then_inc(c_in, 16)
            sp.dma_start(X[:], x_v).then_inc(x_in, 16)

            def mod_chunk(n, v, h, row):
                b = n % 2
                if n >= 2:
                    sp.wait_ge(mod_used, n - 1)
                sp.dma_start(MB[:, b], wmod_v[v, h]).then_inc(mod_in[b], 16)
                if row:
                    sp.dma_start(BROW[0:1, b, :], bmod_v[v, h]).then_inc(mod_in[b], 16)

            n = 0
            for v in (1, 0):
                for h in range(2):
                    mod_chunk(n, v, h, False)
                    n += 1
            sp.dma_start(WIN[:], w_in[0].rearrange("(p k) n -> p k n", p=P)).then_inc(win_in, 16)
            sp.dma_start(ggrc, col8(g_group[0])).then_inc(misc_in, 16)
            sp.dma_start(sinkb, sinks[0:1, :].broadcast_to([P, 8])).then_inc(misc_in, 16)
            sp.dma_start(farb, table[31:32, 8:12].broadcast_to([P, 4])).then_inc(misc_in, 16)
            sp.wait_ge(proj_done, 21)
            sp.wait_ge(q_kept, 9)
            for p0 in (0, 64):
                sp.dma_start(KSW[p0:p0 + 64, :], QKT[64 - p0:128 - p0, 8, :]).then_inc(swap_in, 16)
            for _, v in ROWS:
                for h in range(2):
                    mod_chunk(n, v, h, True)
                    n += 1
            sp.wait_ge(band_out, 16)
            sp.dma_start(BT[:], bass.AP(band_dram.tensor, P - 1, [[BAND - 1, P], [P * BAND, 12], [1, 256]])).then_inc(band_in, 16)
            sp.dma_start(WOUT[:], w_out[0].rearrange("(p k) n -> p k n", p=P)).then_inc(wout_in, 16)
            sp.wait_ge(mod_used, 12)
            sp.dma_start(GFFN[:], rep(g_ffn[0], D)).then_inc(g_ffn_in, 16)
            sp.dma_start(WR[:], w_router[0].rearrange("(p k) e -> p k e", p=P)).then_inc(wr_in, 16)
            sp.dma_start(BRT[:], b_router[0:1, :].broadcast_to([P, E])).then_inc(wr_in, 16)
            sp.wait_ge(set_free, len(UNITS))
            for k in range(2):
                sp.dma_start(BW[32 * k:32 * k + 32, 0:2 * D], b_gate_up[0]).then_inc(bias_in, 16)
                sp.dma_start(BW[32 * k:32 * k + 32, 2 * D:3 * D], b_down[0]).then_inc(bias_in, 16)
            sp.wait_ge(wout_done, NT)
            sp.wait_ge(y_stored, 16)
            sp.wait_ge(routed, 1)
            last_tile = sp.value_load(LAST[0:1, 0:1], min_val=15, max_val=MAX_TILES - 1)

            def load(e, i, k, src):
                if not (isinstance(i, int) and 4 + CHUNKS * i + k < RING):
                    sp.wait_ge(lo_done, i * CHUNKS + (k + 1))
                slot = (4 + k) % RING
                kind, h, q = src
                if kind == "gu":
                    sp.dma_start(RINGB[:, slot, :].rearrange("p (k n) -> p k n", n=512),
                                 gu_v[bass.ds(e, 1), h, :, 4 * q:4 * q + 4, :].rearrange("a p k n -> (a p) k n")
                                 ).then_inc(ring_in[slot], 16)
                else:
                    sp.dma_start(RINGB[:, slot, :],
                                 down_v[bass.ds(e, 1), h, q].rearrange("a p n -> (a p) n")).then_inc(ring_in[slot], 16)

            e0 = sp.value_load(TILE_E[0:1, 0:1], min_val=0, max_val=E - 1)
            for q in range(4):
                load(e0, 0, q - 4, ("gu", 0, q))
            with sp.Fori(0, last_tile) as i:
                e = sp.value_load(TILE_E[0:1, bass.ds(i, 1)], min_val=0, max_val=E - 1)
                en = sp.value_load(TILE_E[0:1, bass.ds(i + 1, 1)], min_val=0, max_val=E - 1)
                for q in range(4):
                    load(e, i, q, ("gu", 1, q))
                for q in range(2):
                    load(e, i, 4 + q, ("dn", 0, q))
                for q in range(4):
                    load(en, i, 6 + q, ("gu", 0, q))
                for q in range(2):
                    load(e, i, 10 + q, ("dn", 1, q))
            i = last_tile
            e = sp.value_load(TILE_E[0:1, bass.ds(i, 1)], min_val=0, max_val=E - 1)
            for q in range(4):
                load(e, i, q, ("gu", 1, q))
            for q in range(2):
                load(e, i, 4 + q, ("dn", 0, q))
            for q in range(2):
                load(e, i, 6 + q, ("dn", 1, q))
            sp.wait_ge(pe_chunk, last_tile * CHUNKS + CHUNKS)
            sp.dma_start(GF[:], rep(g_final, D)).then_inc(misc_in, 16)
            for t in range(NT):
                sp.wait_ge(final_ready, t + 1)
                sp.dma_start(out_v[:, t, :], AC2[:, t, :]).then_inc(stored, 16)
            sp.wait_ge(stored, 16 * NT)

        @block.tensor
        def _(pe):
            pe.wait_ge(consts, 1)
            def turn(src, j, bank):
                for t in range(NT):
                    last = pe.transpose(PS[:, bank, t * P:(t + 1) * P], src[:, t, j:D:C], ID[:])
                last.then_inc(turned, 1)

            pe.wait_ge(xn_ready, NT)
            for j in range(6):
                turn(XN, j, j)
            pe.wait_ge(band_in, 48)
            pe.matmul(PS[0:12, 6, 0:BAND], BANDT, BANDH[:], start=True, stop=True).then_inc(band_done, 1)
            pe.wait_ge(c_silu, 1)
            n = 0
            for v in range(2):
                for h in range(2):
                    b = n % 2
                    pe.wait_ge(mod_in[b], 16 * (n // 2 + 1))
                    for j in range(C):
                        for k in range(C):
                            mm = pe.matmul(PS[64 * h:64 * h + 64, 7, C * v + j:C * v + j + 1],
                                           MB[:, b, k, j:512:C], cS[:, k:k + 1], start=(k == 0), stop=(k == C - 1))
                    mm.then_inc(mod_used, 1)
                    n += 1
            for j in range(6, C):
                pe.wait_ge(kept, j - 5)
                turn(XN, j, j % 6)
            pe.wait_ge(win_in, 16)
            pe.wait_ge(kept, C)

            def bank_free(n):
                if n >= 19:
                    pe.wait_ge(v_kept, n - 18)
                elif n >= 6:
                    pe.wait_ge(q_kept, n - 5)

            n = 0
            for blk in range(13):
                bank_free(n)
                for k in range(C):
                    lhs = WIN[:, k, Q_COLS[blk]:Q_COLS[blk] + P]
                    mm = pe.matmul(PS[:, n % 6, :], lhs, HT[:, k, :], start=(k == 0), stop=(k == C - 1))
                mm.then_inc(proj_done, 1)
                n += 1
            for t in range(NT):
                bank_free(n)
                for col, width, o in ((SB_V, 256, 0), (SW_V, P, 256)):
                    for k in range(C):
                        mm = pe.matmul(PS[:, n % 6, o:o + width], HT[:, k, t * P:(t + 1) * P],
                                       WIN[:, k, col:col + width], start=(k == 0), stop=(k == C - 1))
                mm.then_inc(proj_done, 1)
                n += 1
                bank_free(n)
                for k in range(C):
                    mm = pe.matmul(PS[:, n % 6, 0:256], HT[:, k, t * P:(t + 1) * P],
                                   WIN[:, k, MB_V:MB_V + 256], start=(k == 0), stop=(k == C - 1))
                mm.then_inc(proj_done, 1)
                n += 1
            pe.wait_ge(c_wide, 1)
            n = 4
            for r in range(len(ROWS)):
                for h in range(2):
                    b = n % 2
                    pe.wait_ge(mod_in[b], 32 + 32 * ((n - 4) // 2 + 1))
                    if n >= 6:
                        pe.wait_ge(rows_kept, n - 5)
                    for k in range(C):
                        mm = pe.matmul(PS[:, 6 + b, :], CSB[:, k, :], MB[:, b, k, :], start=(k == 0), stop=False)
                    mm = pe.matmul(PS[:, 6 + b, :], ONES[0:1, :], BROW[0:1, b, :], start=False, stop=True)
                    mm.then_inc(mod_used, 1)
                    n += 1
            pe.wait_ge(q_kept, 13)
            pe.wait_ge(v_kept, 8)
            pe.wait_ge(swap_in, 32)
            pe.wait_ge(rows_kept, 8)

            def q_k(kind, h):
                p0 = 64 * (h % 2)
                if kind == "sb":
                    return QKT[p0:p0 + 64, h // 2, :], QKT[p0:p0 + 64, 2 + h // 2, :]
                if kind == "mb":
                    return QKT[p0:p0 + 64, 9 + h // 2, :], QKT[p0:p0 + 64, 11 + h // 2, :]
                k = QKT[p0:p0 + 64, 8, :] if h // 4 == h % 2 else KSW[p0:p0 + 64, :]
                return QKT[p0:p0 + 64, 4 + h // 2, :], k

            def scores(u):
                kind, h = UNITS[u]
                q, k = q_k(kind, h)
                s0 = 4 * (u % 2)
                if u >= 2:
                    pe.wait_ge(set_free, u - 1)
                for t in range(NT):
                    if kind == "sb":
                        mm = pe.matmul(PS[:, s0 + t, t * P:T], k[:, t * P:(t + 1) * P], q[:, t * P:T],
                                       start=True, stop=True)
                    elif kind == "sw":
                        lo = max(t - 1, 0) * P
                        o = 256 * (t % 2) + (0 if t else P)
                        mm = pe.matmul(PS[:, s0 + t // 2, o:256 * (t % 2) + 256], q[:, t * P:(t + 1) * P],
                                       k[:, lo:(t + 1) * P], start=True, stop=True)
                    else:
                        mm = pe.matmul(PS[:, s0 + t, 0:(t + 1) * P], q[:, t * P:(t + 1) * P], k[:, 0:(t + 1) * P],
                                       start=True, stop=True)
                mm.then_inc(scores_done, 1)

            def middle(u):
                kind, h = UNITS[u]
                s0 = 4 * (u % 2)
                if kind == "sb":
                    pe.wait_ge(drop_masked, nth(u, "sb"))
                    drop = UB2[u % 2][:].rearrange("p (t n) -> p t n", t=NT)
                    for kt in range(NT):
                        for jt in range(kt, NT):
                            mm = pe.matmul(PS[:, s0 + kt, jt * P:T], (NTRI if jt == kt else NONE_)[:],
                                           drop[:, jt, jt * P:T], start=False, stop=(jt == NT - 1),
                                           skip_group_check=True)
                    mm.then_inc(sums_done, 1)
                else:
                    pe.wait_ge(probs_ready, nth(u, "sw", "mb"))
                    wide = 256 if kind == "sw" else T
                    probs = UB1[u % 2][:, 0:NT * wide].rearrange("p (t n) -> p t n", t=NT)
                    bls = sw_blocks() if kind == "sw" else sb_blocks()
                    b0 = s0 + (2 if kind == "sw" else 0)
                    for n, (qt, kt) in enumerate(bls):
                        o = (kt - qt + 1) * P if kind == "sw" else kt * P
                        mm = pe.transpose(PS[:, b0 + n // 4, (n % 4) * P:(n % 4 + 1) * P], probs[:, qt, o:o + P], ID[:])
                    mm.then_inc(probs_turned, 1)

            def values(u):
                kind, h = UNITS[u]
                s0 = 4 * (u % 2)
                vo = {"sb": h * HD, "sw": 256 + (h // 4) * HD, "mb": 384 + h * HD}[kind]
                ob = s0 + (3 if kind == "mb" else 0)
                if kind == "sb":
                    pe.wait_ge(stick_masked, nth(u, "sb"))
                else:
                    pe.wait_ge(pt_kept, nth(u, "sw", "mb"))
                bls = sw_blocks() if kind == "sw" else sb_blocks()
                for n, (qt, kt) in enumerate(bls):
                    lhs = (UB1[u % 2][:, kt * T + qt * P:kt * T + (qt + 1) * P] if kind == "sb"
                           else UB2[u % 2][:, n * P:(n + 1) * P])
                    first = kt == (max(qt - 1, 0) if kind == "sw" else 0)
                    mm = pe.matmul(PS[:, ob, qt * HD:(qt + 1) * HD], lhs, V[:, kt, vo:vo + HD],
                                   start=first, stop=(kt == qt))
                mm.then_inc(pv_done, 1)

            scores(0)
            for u in range(len(UNITS)):
                if u + 1 < len(UNITS):
                    scores(u + 1)
                middle(u)
                values(u)
            pe.wait_ge(xn_ready, 2 * NT)
            for j in range(C):
                if j >= 6:
                    pe.wait_ge(kept, C + j - 5)
                turn(MERG, j, j % 6)
            pe.wait_ge(wout_in, 16)
            pe.wait_ge(kept, 2 * C)
            for t in range(NT):
                if t >= 3:
                    pe.wait_ge(wout_kept, t - 2)
                for h in range(2):
                    for k in range(C):
                        mm = pe.matmul(PS[:, 2 * (t % 3) + h, :], MT[:, k, t * P:(t + 1) * P],
                                       WOUT[:, k, h * 512:(h + 1) * 512], start=(k == 0), stop=(k == C - 1))
                mm.then_inc(wout_done, 1)
            pe.wait_ge(xn_ready, 3 * NT)
            pe.wait_ge(wout_kept, NT)
            for j in range(C):
                if j >= 6:
                    pe.wait_ge(kept, 2 * C + j - 5)
                turn(XN2, j, j % 6)
            pe.wait_ge(wr_in, 32)
            pe.wait_ge(kept, 3 * C)
            for t in range(NT):
                for k in range(C):
                    mm = pe.matmul(PS[:, 6, t * E:(t + 1) * E], H2T[:, k, t * P:(t + 1) * P], WR[:, k, :],
                                   start=(k == 0), stop=(k == C - 1))
            mm.then_inc(logits_done, 1)
            pe.wait_ge(mask_ready, 1)
            for t in range(NT):
                for s in range(t + 1):
                    mm = pe.matmul(PS[:, 7, t * E:(t + 1) * E], (SLT if s == t else ONES)[:], MASK[:, s, :],
                                   start=(s == 0), stop=(s == t))
            for s in range(NT):
                mm = pe.matmul(PS[:, 7, P:P + E], ONES[:], MASK[:, s, :], start=(s == 0), stop=(s == NT - 1))
            mm.then_inc(ranks_done, 1)

            def gather(i_next):
                pe.wait_ge(s_ready, i_next)
                for j in range(C):
                    for t in range(NT):
                        for part, h2 in enumerate((H2H, H2L)):
                            mm = pe.matmul(PS[:, j // 4, (j % 4) * P:(j % 4 + 1) * P], h2[:, t, j:D:C], S[:, t, :],
                                           start=(t == 0 and part == 0), stop=(t == NT - 1 and part == 1))
                mm.then_inc(gathered, 1)

            def chunk(i, k, xh, xl, banks, js, first, last):
                pe.wait_ge(lo_done, i * CHUNKS + (k + 7))
                b = (4 + k) % 3
                for a, j in enumerate(js):
                    for g in range(2):
                        o = (2 * a + g) * 512
                        for n, (xs, ws) in enumerate(((xh, WH), (xl, WH), (xh, WL))):
                            mm = pe.matmul(PS[:, banks + g, :], xs[:, j, :], ws[:, b, o:o + 512],
                                           start=(first and a == 0 and n == 0),
                                           stop=(last and a == 1 and n == 2), skip_group_check=True)
                mm.then_inc(pe_chunk, 1)

            def gate_up(i, k0, h, n):
                for q in range(4):
                    chunk(i, k0 + q, XH, XL, 2 + 2 * h, (2 * q, 2 * q + 1), q == 0, False)
                for g in range(2):
                    o = g * D + h * 512
                    mm = pe.matmul(PS[:, 2 + 2 * h + g, :], SEL[:], BR[:, o:o + 512], start=False, stop=True,
                                   skip_group_check=True)
                mm.then_inc(gu_done, 1)

            def turn_act(h, n):
                pe.wait_ge(act_ready, n)
                for r in range(4):
                    mm = pe.transpose(PS[:, 2 + 2 * h, r * P:(r + 1) * P], AC[:, h, r:512:4], ID[:])
                mm.then_inc(act_turned, 1)

            def down(i, k0, h):
                pe.wait_ge(al_ready, i * 2 + (h + 1))
                if h == 0:
                    pe.wait_ge(y_kept, i + 1)
                    for g in range(2):
                        o = 2 * D + g * 512
                        mm = pe.matmul(PS[:, 6 + g, :], SEL[:], BR[:, o:o + 512], start=True, stop=False,
                                       skip_group_check=True)
                    mm.then_inc(sel_used, 1)
                for q in range(2):
                    chunk(i, k0 + q, AH[:, h], AL[:, h], 6, (2 * q, 2 * q + 1), False, h == 1 and q == 1)

            pe.wait_ge(h2_split, 1)
            pe.wait_ge(bias_split, 1)
            last_tile = pe.value_load(LAST[0:1, 0:1], min_val=15, max_val=MAX_TILES - 1)
            gather(1)
            pe.wait_ge(xl_ready, 1)
            pe.wait_ge(sel_ready, 1)
            gate_up(0, -4, 0, 1)
            with pe.Fori(0, last_tile) as i:
                gate_up(i, 0, 1, i * 2 + 2)
                turn_act(0, i * 2 + 1)
                gather(i + 2)
                down(i, 4, 0)
                turn_act(1, i * 2 + 2)
                pe.wait_ge(xl_ready, i + 2)
                pe.wait_ge(sel_ready, i + 2)
                gate_up(i, 6, 0, i * 2 + 3)
                down(i, 10, 1)
            i = last_tile
            gate_up(i, 0, 1, i * 2 + 2)
            turn_act(0, i * 2 + 1)
            down(i, 4, 0)
            turn_act(1, i * 2 + 2)
            down(i, 6, 1)

        @block.scalar
        def _(act):
            done = [0]

            def step(ins):
                done[0] += 1
                ins.then_inc(act_step, 1)
                act.wait_ge(act_step, done[0])

            act.dma_start(BANDH[:], onehot).then_inc(band_in, 16)
            act.dma_start(BANDT, table).then_inc(band_in, 16)
            act.dma_start(BANDM[:], masks).then_inc(band_in, 16)
            act.wait_ge(c_in, 64)
            act.activation(sg, cT, ACT.Sigmoid).then_inc(roots, 1)

            def norm_sums(src, n, junk):
                for t in range(NT):
                    last = act.activation(junk[:, t, :], src[:, t, :], ACT.Square, accum_out=ss[:, t:t + 1])
                last.then_inc(squares, 1)
                act.wait_ge(dve_mean, n)
                act.activation(rs, rs, ACT.Sqrt).then_inc(roots, 1)

            act.wait_ge(x_in, 16)
            norm_sums(X, 1, XN)
            act.wait_ge(band_kept, 1)
            act.dma_start(band_dram, BANDS[:].unsqueeze(1).broadcast_to([12, P, BAND])).then_inc(band_out, 16)
            for n in range(13, 21):
                act.wait_ge(proj_done, n + 1)
                t, part = divmod(n - 13, 2)
                if part == 0:
                    act.activation(V[:, t, 0:384], PS[:, n % 6, 0:384], ACT.Copy).then_inc(v_kept, 1)
                else:
                    act.activation(V[:, t, 384:640], PS[:, n % 6, 0:256], ACT.Copy).then_inc(v_kept, 1)
            act.wait_ge(zeros, 1)
            act.dma_start(ys[16 * P:(MAX_TILES + 1) * P, :].rearrange("(p r) (h n) -> p (r h) n", p=P, h=2),
                          ZERO[:].unsqueeze(1).broadcast_to([P, 64, 512])).then_inc(y_stored, 16)
            act.wait_ge(misc_in, 48)

            def first(u):
                kind, h = UNITS[u]
                s = u % 2
                s0 = 4 * s
                a, b = UB1[s], UB2[s]
                if kind == "sb":
                    act.wait_ge(scores_done, u + 1)
                    av = a[:].rearrange("p (t n) -> p t n", t=NT)
                    for t in range(NT):
                        last = act.activation(av[:, t, t * P:T], PS[:, s0 + t, t * P:T], ACT.Abs)
                    step(last)
                    for t in range(NT):
                        last = act.activation(av[:, t, t * P:T], av[:, t, t * P:T], ACT.Exp, scale=-1.0)
                    step(last)
                    for t in range(NT):
                        last = act.activation(av[:, t, t * P:T], av[:, t, t * P:T], ACT.Ln, bias=1.0)
                    last.then_inc(logs_ready, 1)
                else:
                    act.wait_ge(max_ready, nth(u, "sw", "mb"))
                    wide = 256 if kind == "sw" else T
                    av = a[:, 0:NT * wide].rearrange("p (t n) -> p t n", t=NT)
                    for t in range(NT):
                        lo, hi = ((0 if t else P), 256) if kind == "sw" else (0, (t + 1) * P)
                        last = act.activation(av[:, t, lo:hi], av[:, t, lo:hi], ACT.Exp, bias=negm[s][:, t:t + 1],
                                              accum_out=den[s][:, t:t + 1])
                    if kind == "sw":
                        last = act.activation(esink[s], negm[s], ACT.Exp, bias=sinkb[:, h:h + 1])
                    last.then_inc(probs_ready, 1)

            def second(u):
                kind, h = UNITS[u]
                s = u % 2
                s0 = 4 * s
                a, b = UB1[s], UB2[s]
                if kind == "sb":
                    act.wait_ge(sums_done, nth(u, "sb"))
                    av = a[:].rearrange("p (t n) -> p t n", t=NT)
                    for t in range(NT):
                        last = act.activation(av[:, t, t * P:T], PS[:, s0 + t, t * P:T], ACT.Exp)
                    last.then_inc(stick_ready, 1)
                else:
                    act.wait_ge(probs_turned, nth(u, "sw", "mb"))
                    b0, n = (s0 + 2, 7) if kind == "sw" else (s0, 10)
                    act.activation(b[:, 0:n * P], PSF[:, b0 * 512:b0 * 512 + n * P], ACT.Copy).then_inc(pt_kept, 1)

            first(0)
            for u in range(len(UNITS)):
                if u + 1 < len(UNITS):
                    first(u + 1)
                second(u)
            act.wait_ge(set_free, len(UNITS))
            for g, (o, w) in enumerate(((0, 256), (256, 512), (768, 256))):
                for t in range(NT):
                    last = act.activation(MTF[:, t, o:o + w], MERG[:, t, o:o + w], ACT.Square,
                                          accum_out=gss[:, 4 * g + t:4 * g + t + 1])
            last.then_inc(squares, 1)
            act.wait_ge(dve_mean, 2)
            act.activation(grs, grs, ACT.Sqrt).then_inc(roots, 1)
            act.wait_ge(wout_kept, NT)
            norm_sums(X, 3, XN2)
            act.wait_ge(max_ready, SOFT_UNITS + 1)
            act.activation(EXPJ, LM, ACT.Exp).then_inc(probs_ready, 1)

            act.wait_ge(routed, 1)
            last_tile = act.value_load(LAST[0:1, 0:1], min_val=15, max_val=MAX_TILES - 1)
            act.wait_ge(h2_split, 1)
            act.sem_inc(y_kept, 1)

            def hi(i, k):
                slot, b = (4 + k) % RING, (4 + k) % 3
                act.wait_ge(ring_in[slot], i * 32 + 16 * ((4 + k) // RING + 1))
                if not (isinstance(i, int) and 4 + CHUNKS * i + k < 3):
                    act.wait_ge(pe_chunk, i * CHUNKS + (k + 2))
                act.activation(WH[:, b, :], RINGB[:, slot, :], ACT.Copy).then_inc(hi_done, 1)

            def sig(n):
                act.wait_ge(gate_ready, n)
                act.activation(SG[:], GC[:], ACT.Sigmoid, scale=ALPHA).then_inc(sig_ready, 1)

            def keep_turned(h, n):
                act.wait_ge(act_turned, n)
                act.activation(AH[:, h].rearrange("p r m -> p (r m)"), PS[:, 2 + 2 * h, :], ACT.Copy
                               ).then_inc(ah_ready, 1)

            def keep_gathered(n):
                act.wait_ge(gathered, n)
                act.activation(XH[:].rearrange("p j m -> p (j m)"), PSF[:, 0:D], ACT.Copy).then_inc(xh_ready, 1)

            def keep_y(i, k):
                act.wait_ge(pe_chunk, i * CHUNKS + (k + 5))
                act.wait_ge(y_stored, i * 16 + 16)
                act.activation(Y[:], PSF[:, 6 * 512:8 * 512], ACT.Copy).then_inc(y_kept, 1)
                act.wait_ge(y_kept, i + 2)
                act.dma_start(ys[bass.ds(i * P, P), :], Y[:]).then_inc(y_stored, 16)

            for k in range(-4, -1):
                hi(0, k)
            keep_gathered(1)
            for k in range(-1, 1):
                hi(0, k)
            sig(1)
            for k in range(1, 3):
                hi(0, k)
            with act.Fori(0, last_tile) as i:
                hi(i, 3)
                hi(i, 4)
                hi(i, 5)
                sig(i * 2 + 2)
                keep_turned(0, i * 2 + 1)
                hi(i, 6)
                keep_gathered(i + 2)
                hi(i, 7)
                hi(i, 8)
                keep_turned(1, i * 2 + 2)
                hi(i, 9)
                hi(i, 10)
                hi(i, 11)
                sig(i * 2 + 3)
                hi(i, 12)
                hi(i, 13)
                keep_y(i, 11)
                hi(i, 14)
            i = last_tile
            hi(i, 3)
            hi(i, 4)
            hi(i, 5)
            sig(i * 2 + 2)
            keep_turned(0, i * 2 + 1)
            hi(i, 6)
            keep_turned(1, i * 2 + 2)
            hi(i, 7)
            keep_y(i, 7)
            act.wait_ge(y_stored, last_tile * 16 + 32)
            act.activation(sg, sg, ACT.Copy).then_inc(ys_ready, 1)
            for t in range(NT):
                act.wait_ge(sum_ready, t + 1)
                act.activation(FJ[:, t, :], AC2[:, t, :], ACT.Square,
                               accum_out=ss[:, t:t + 1]).then_inc(squares, 1)
                act.wait_ge(dve_mean, 4 + t)
                act.activation(rs[:, t:t + 1], rs[:, t:t + 1], ACT.Sqrt).then_inc(roots, 1)

        @block.vector
        def _(v):
            done = [0]

            def step(ins):
                done[0] += 1
                ins.then_inc(dve_step, 1)
                v.wait_ge(dve_step, done[0])

            v.wait_ge(roots, 1)
            v.tensor_tensor(cS, cT, sg, ALU.mult).then_inc(c_silu, 1)

            def rows_normed(n_sq, n_mean, n_root, src, dst):
                v.wait_ge(squares, n_sq)
                v.tensor_scalar(rs, ss, 1.0 / D, EPS, ALU.mult, ALU.add).then_inc(dve_mean, 1)
                v.wait_ge(roots, n_root)
                step(v.reciprocal(rs, rs))
                for t in range(NT):
                    v.tensor_scalar(dst[:, t, :], src[:, t, :], rs[:, t:t + 1], None, ALU.mult).then_inc(xn_ready, 1)

            rows_normed(1, 1, 2, X, XN)
            v.wait_ge(mod_used, 4)
            step(v.tensor_tensor(G1, PS[:, 7, 0:C], bsc, ALU.add))
            v.tensor_tensor(SH1, PS[:, 7, C:2 * C], bsh, ALU.add)
            step(v.scalar_tensor_tensor(out=G1, in0=G1, scalar=1.0, in1=gmixc, op0=ALU.add, op1=ALU.mult))
            for j in range(C):
                v.wait_ge(turned, j + 1)
                v.tensor_scalar(HT[:, j, :], PS[:, j % 6, :], G1[:, j:j + 1], SH1[:, j:j + 1], ALU.mult, ALU.add
                                ).then_inc(kept, 1)
            v.wait_ge(band_done, 1)
            v.wait_ge(band_in, 48)
            v.tensor_tensor(BANDS[:], PS[0:12, 6, 0:BAND], BANDM[:], ALU.add).then_inc(band_kept, 1)
            for n in range(13):
                v.wait_ge(proj_done, n + 1)
                q = n in (0, 1, 4, 5, 6, 7, 9, 10)
                v.tensor_scalar(QKT[:, n, :], PS[:, n % 6, :], HD ** -0.5 if q else 1.0, None, ALU.mult
                                ).then_inc(q_kept, 1)
            v.wait_ge(proj_done, 13)
            v.wait_ge(band_out, 16)
            v.tensor_copy(CSB[:], cS.unsqueeze(2).broadcast_to([P, C, P])).then_inc(c_wide, 1)
            for n, (name, _) in enumerate(ROWS):
                for h in range(2):
                    v.wait_ge(mod_used, 4 + 2 * n + h + 1)
                    v.tensor_scalar(ROW[name][:, h * 512:(h + 1) * 512], PS[:, 6 + h, :],
                                    1.0 if name == "sc2" else 0.0, None, ALU.add).then_inc(rows_kept, 1)
            v.wait_ge(band_in, 64)
            v.wait_ge(misc_in, 48)

            def first(u):
                kind, h = UNITS[u]
                s = u % 2
                s0 = 4 * s
                a, b = UB1[s], UB2[s]
                if kind == "sb":
                    v.wait_ge(logs_ready, nth(u, "sb"))
                    av = a[:].rearrange("p (t n) -> p t n", t=NT)
                    bv = b[:].rearrange("p (t n) -> p t n", t=NT)
                    for t in range(NT):
                        last = v.scalar_tensor_tensor(out=bv[:, t, t * P:T], in0=PS[:, s0 + t, t * P:T], scalar=0.0,
                                                      in1=av[:, t, t * P:T], op0=ALU.max, op1=ALU.add)
                    last.then_inc(drop_ready, 1)
                    return
                v.wait_ge(scores_done, u + 1)
                if kind == "sw":
                    av = a[:, 0:NT * 256].rearrange("p (t n) -> p t n", t=NT)
                    pv = PSF[:, s0 * 512:s0 * 512 + NT * 256].rearrange("p (t n) -> p t n", t=NT)
                    v.tensor_tensor(av[:, 0, P:256], pv[:, 0, P:256], BT[:, h, P:256], ALU.add)
                    step(v.tensor_tensor(av[:, 1:NT, :], pv[:, 1:NT, :],
                                         BT[:, h, :].unsqueeze(1).broadcast_to([P, NT - 1, 256]), ALU.add))
                    v.tensor_reduce(mx[s][:, 0:1], av[:, 0, P:256], AX, ALU.max)
                    step(v.tensor_reduce(mx[s][:, 1:NT], av[:, 1:NT, :], AX, ALU.max))
                    v.tensor_scalar(negm[s], mx[s], sinkb[:, h:h + 1], -1.0, ALU.max, ALU.mult).then_inc(max_ready, 1)
                else:
                    av = a[:].rearrange("p (t n) -> p t n", t=NT)
                    for t in range(NT):
                        lo = max(t - 1, 0) * P
                        last = v.tensor_tensor(av[:, t, lo:(t + 1) * P], PS[:, s0 + t, lo:(t + 1) * P],
                                               BT[:, 8 + h, (0 if t else P):256], ALU.add)
                        if t >= 2:
                            last = v.tensor_scalar(av[:, t, 0:lo], PS[:, s0 + t, 0:lo], farb[:, h:h + 1], None, ALU.add)
                    step(last)
                    for t in range(NT):
                        last = v.tensor_reduce(mx[s][:, t:t + 1], av[:, t, 0:(t + 1) * P], AX, ALU.max)
                    step(last)
                    v.tensor_scalar(negm[s], mx[s], -1.0, None, ALU.mult).then_inc(max_ready, 1)

            def last_of(u):
                kind, h = UNITS[u]
                s = u % 2
                s0 = 4 * s
                if kind != "sb":
                    v.wait_ge(probs_ready, nth(u, "sw", "mb"))
                    if kind == "sw":
                        step(v.tensor_tensor(den[s], den[s], esink[s], ALU.add))
                    step(v.reciprocal(rden[s], den[s]))
                v.wait_ge(pv_done, u + 1)
                ob = s0 + (3 if kind == "mb" else 0)
                o = {"sb": 0, "sw": 256, "mb": 768}[kind] + h * HD
                src = PS[:, ob, 0:NT * HD].rearrange("p (t n) -> p t n", t=NT)
                if kind == "sb":
                    v.tensor_copy(MERG[:, :, o:o + HD], src).then_inc(set_free, 1)
                else:
                    v.tensor_tensor(MERG[:, :, o:o + HD], src, rden[s].unsqueeze(2).broadcast_to([P, NT, HD]),
                                    ALU.mult).then_inc(set_free, 1)

            first(0)
            for u in range(len(UNITS)):
                if u + 1 < len(UNITS):
                    first(u + 1)
                last_of(u)
            v.wait_ge(squares, 2)
            for g, w in enumerate((256, 512, 256)):
                last = v.tensor_scalar(grs[:, 4 * g:4 * g + 4], gss[:, 4 * g:4 * g + 4], 1.0 / w, EPS, ALU.mult, ALU.add)
            last.then_inc(dve_mean, 1)
            v.wait_ge(roots, 3)
            step(v.reciprocal(grs, grs))
            for t in range(NT):
                for g, (o, w) in enumerate(((0, 256), (256, 512), (768, 256))):
                    last = v.tensor_scalar(MERG[:, t, o:o + w], MERG[:, t, o:o + w],
                                           grs[:, 4 * g + t:4 * g + t + 1], None, ALU.mult)
                last.then_inc(xn_ready, 1)
            for j in range(C):
                v.wait_ge(turned, C + j + 1)
                v.tensor_scalar(MT[:, j, :], PS[:, j % 6, :], ggrc[:, j:j + 1], None, ALU.mult).then_inc(kept, 1)
            for t in range(NT):
                v.wait_ge(wout_done, t + 1)
                b0 = 2 * (t % 3)
                step(v.tensor_tensor(TMP[t % 2][:], PSF[:, b0 * 512:b0 * 512 + D], ROW["gt1"][:], ALU.mult))
                v.tensor_tensor(X[:, t, :], X[:, t, :], TMP[t % 2][:], ALU.add).then_inc(wout_kept, 1)
            v.wait_ge(bias_in, 64)
            step(v.tensor_scalar(BW[:, D:2 * D], BW[:, D:2 * D], 1.0, None, ALU.add))
            v.tensor_copy(BR[0:32, :], BW[0:32, :])
            step(v.tensor_copy(BHT[32:64, :], BW[32:64, :]))
            v.tensor_tensor(BR[32:64, :], BW[32:64, :], BHT[32:64, :].bitcast(F32), ALU.subtract).then_inc(bias_split, 1)
            v.wait_ge(g_ffn_in, 16)
            step(v.tensor_tensor(ROW["sc2"][:], ROW["sc2"][:], GFFN[:], ALU.mult))
            v.wait_ge(squares, 3)
            v.tensor_scalar(rs, ss, 1.0 / D, EPS, ALU.mult, ALU.add).then_inc(dve_mean, 1)
            v.wait_ge(roots, 4)
            step(v.reciprocal(rs, rs))
            for t in range(NT):
                step(v.scalar_tensor_tensor(out=XN2[:, t, :], in0=X[:, t, :], scalar=rs[:, t:t + 1],
                                            in1=ROW["sc2"][:], op0=ALU.mult, op1=ALU.mult))
                v.tensor_tensor(XN2[:, t, :], XN2[:, t, :], ROW["sh2"][:], ALU.add).then_inc(xn_ready, 1)
            for j in range(C):
                v.wait_ge(turned, 2 * C + j + 1)
                v.tensor_copy(H2T[:, j, :], PS[:, j % 6, :]).then_inc(kept, 1)
            v.wait_ge(logits_done, 1)
            step(v.tensor_tensor(L, PS[:, 6, 0:P].rearrange("p (t e) -> p t e", t=NT),
                                 BRT[:].unsqueeze(1).broadcast_to([P, NT, E]), ALU.add))
            for t in range(NT):
                last = v.max(M8[:, t, :], L[:, t, :])
            step(last)
            for t in range(NT):
                last = v.max_index(I8[:, t, :], M8[:, t, :], L[:, t, :])
            step(last)
            v.tensor_tensor(LM, M8, M8[:, :, 0:1].broadcast_to([P, NT, 8]), ALU.subtract).then_inc(max_ready, 1)
            step(v.tensor_copy(IF, I8))
            v.wait_ge(iotas, 1)
            step(v.tensor_tensor(OH, IF[:, :, 0:TOPK].unsqueeze(3).broadcast_to([P, NT, TOPK, E]),
                                 IOTAE.unsqueeze(1).unsqueeze(1).broadcast_to([P, NT, TOPK, E]), ALU.is_equal))
            step(v.tensor_tensor(MK2, OH[:, :, 0, :], OH[:, :, 1, :], ALU.add))
            step(v.tensor_tensor(MK3, OH[:, :, 2, :], OH[:, :, 3, :], ALU.add))
            v.tensor_tensor(MASK, MK2, MK3, ALU.add).then_inc(mask_ready, 1)
            v.wait_ge(probs_ready, SOFT_UNITS + 1)
            step(v.tensor_reduce(SUM4, EXPJ[:, :, 0:TOPK], AX, ALU.add))
            step(v.reciprocal(SUM4, SUM4))
            v.tensor_tensor(WJ[:], EXPJ, SUM4.unsqueeze(2).broadcast_to([P, NT, 8]), ALU.mult)
            v.wait_ge(ranks_done, 1)
            step(v.tensor_copy(CNT, PS[:, 7, P:P + E]))
            step(v.tensor_scalar(TL, CNT, 0.0, None, ALU.is_gt))
            for full in range(1, NT):
                step(v.scalar_tensor_tensor(out=TL, in0=CNT, scalar=float(full * P), in1=TL, op0=ALU.is_gt, op1=ALU.add))
            step(v.tensor_copy(TEND[0], TL))
            k, n = 0, 1
            while n < E:
                v.tensor_copy(TEND[1 - k][:, 0:n], TEND[k][:, 0:n])
                step(v.tensor_tensor(TEND[1 - k][:, n:E], TEND[k][:, n:E], TEND[k][:, 0:E - n], ALU.add))
                k, n = 1 - k, 2 * n
            tend = TEND[k]
            step(v.tensor_tensor(TSTART, tend, TL, ALU.subtract))
            step(v.scalar_tensor_tensor(out=SLOT, in0=TSTART.unsqueeze(1).broadcast_to([P, NT, E]), scalar=float(P),
                                        in1=PS[:, 7, 0:P].rearrange("p (t e) -> p t e", t=NT),
                                        op0=ALU.mult, op1=ALU.add))
            step(v.scalar_tensor_tensor(out=GM[:], in0=SLOT, scalar=1.0, in1=MASK, op0=ALU.add, op1=ALU.mult))
            v.tensor_scalar(GM[:], GM[:], -1.0, None, ALU.add)
            step(v.tensor_tensor(OH, OH, SLOT.unsqueeze(2).broadcast_to([P, NT, TOPK, E]), ALU.mult))
            step(v.tensor_reduce(SJ, OH, AX, ALU.add))
            v.tensor_copy(SI[:], SJ)
            step(v.tensor_tensor(TT, IOTA48.unsqueeze(2).broadcast_to([1, 48, E]), tend[0:1].unsqueeze(1).broadcast_to([1, 48, E]), ALU.is_ge))
            step(v.tensor_reduce(TE, TT, AX, ALU.add))
            v.tensor_scalar(TILE_E[:], TE, float(E - 1), None, ALU.min)
            v.tensor_scalar(LAST[0:1, 0:1], tend[0:1, E - 1:E], -1.0, None, ALU.add).then_inc(routed, 1)
            for t in range(NT):
                last = v.tensor_copy(H2H[:, t, :], XN2[:, t, :])
            step(last)
            for t in range(NT):
                last = v.tensor_tensor(H2L[:, t, :], XN2[:, t, :], H2H[:, t, :].bitcast(F32), ALU.subtract)
            last.then_inc(h2_split, 1)

            last_tile = v.value_load(LAST[0:1, 0:1], min_val=15, max_val=MAX_TILES - 1)
            v.sem_inc(lo_done, 2)

            def place(n):
                v.wait_ge(cols_ready, n)
                v.tensor_tensor(S[:], IOTA[:].unsqueeze(1).broadcast_to([P, NT, P]),
                                GMS[:].unsqueeze(2).broadcast_to([P, NT, P]), ALU.is_equal).then_inc(s_ready, 1)

            def lo(i, k):
                slot, b = (4 + k) % RING, (4 + k) % 3
                v.wait_ge(hi_done, i * CHUNKS + (4 + k + 1))
                v.tensor_tensor(WL[:, b, :], RINGB[:, slot, :], WH[:, b, :].bitcast(F32), ALU.subtract
                                ).then_inc(lo_done, 1)

            def clip(h, n, first_=False):
                v.wait_ge(gu_done, n)
                if not first_:
                    v.wait_ge(act_ready, n - 1)
                b = 2 + 2 * h
                v.tensor_scalar(GC[:], PS[:, b, :], LIMIT, None, ALU.min).then_inc(gate_ready, 1)
                v.tensor_scalar(UC[:], PS[:, b + 1, :], LIMIT + 1.0, 1.0 - LIMIT, ALU.min, ALU.max).then_inc(up_ready, 1)

            def keep_turned(h, n):
                v.wait_ge(ah_ready, n)
                v.tensor_tensor(AL[:, h].rearrange("p r m -> p (r m)"), PS[:, 2 + 2 * h, :],
                                AH[:, h].rearrange("p r m -> p (r m)").bitcast(F32), ALU.subtract).then_inc(al_ready, 1)

            def keep_gathered(n):
                v.wait_ge(xh_ready, n)
                v.tensor_tensor(XL[:].rearrange("p j m -> p (j m)"), PSF[:, 0:D],
                                XH[:].rearrange("p j m -> p (j m)").bitcast(F32), ALU.subtract).then_inc(xl_ready, 1)

            place(1)
            for k in range(-4, -1):
                lo(0, k)
            keep_gathered(1)
            for k in range(-1, 1):
                lo(0, k)
            clip(0, 1, True)
            for k in range(1, 3):
                lo(0, k)
            with v.Fori(0, last_tile) as i:
                v.wait_ge(gathered, i + 1)
                place(i + 2)
                lo(i, 3)
                lo(i, 4)
                lo(i, 5)
                clip(1, i * 2 + 2)
                keep_turned(0, i * 2 + 1)
                lo(i, 6)
                keep_gathered(i + 2)
                lo(i, 7)
                lo(i, 8)
                keep_turned(1, i * 2 + 2)
                lo(i, 9)
                lo(i, 10)
                lo(i, 11)
                clip(0, i * 2 + 3)
                lo(i, 12)
                lo(i, 13)
                lo(i, 14)
            i = last_tile
            lo(i, 3)
            lo(i, 4)
            lo(i, 5)
            clip(1, i * 2 + 2)
            keep_turned(0, i * 2 + 1)
            lo(i, 6)
            keep_turned(1, i * 2 + 2)
            lo(i, 7)
            v.wait_ge(misc_in, 64)
            for t in range(NT):
                for j in range(TOPK):
                    n = TOPK * t + j
                    v.wait_ge(rows_in[n % 8], 16 * (n // 8 + 1))
                    if j == 0:
                        last = v.tensor_scalar(AC2[:, t, :], GR[:, n % 8, :], WJ[:, t, 0:1], None, ALU.mult)
                    else:
                        last = v.scalar_tensor_tensor(out=AC2[:, t, :], in0=GR[:, n % 8, :], scalar=WJ[:, t, j:j + 1],
                                                      in1=AC2[:, t, :], op0=ALU.mult, op1=ALU.add)
                    last.then_inc(rows_used, 1)
                    v.wait_ge(rows_used, n + 1)
                step(v.tensor_tensor(AC2[:, t, :], AC2[:, t, :], ROW["gt2"][:], ALU.mult))
                v.tensor_tensor(AC2[:, t, :], AC2[:, t, :], X[:, t, :], ALU.add).then_inc(sum_ready, 1)
                v.wait_ge(squares, 4 + t)
                v.tensor_scalar(rs[:, t:t + 1], ss[:, t:t + 1], 1.0 / D, EPS, ALU.mult, ALU.add).then_inc(dve_mean, 1)
                v.wait_ge(roots, 5 + t)
                step(v.reciprocal(rs[:, t:t + 1], rs[:, t:t + 1]))
                v.scalar_tensor_tensor(out=AC2[:, t, :], in0=AC2[:, t, :], scalar=rs[:, t:t + 1], in1=GF[:],
                                       op0=ALU.mult, op1=ALU.mult).then_inc(final_ready, 1)

        @block.gpsimd
        def _(g):
            done = [0]

            def step(ins):
                done[0] += 1
                ins.then_inc(pool_step, 1)
                g.wait_ge(pool_step, done[0])

            for m, val in ((ID, 0.0), (NTRI, -1.0), (NONE_, -1.0), (ONES, 1.0), (SLT, 1.0)):
                last = g.memset(m[:], val)
            step(last)
            g.affine_select(out=ID[:], in_=ID[:], compare_op=ALU.not_equal, fill=1.0, base=0,
                            pattern=[[-1, P]], channel_multiplier=1)
            g.affine_select(out=NTRI[:], in_=NTRI[:], compare_op=ALU.is_ge, fill=0.0, base=0,
                            pattern=[[-1, P]], channel_multiplier=1)
            g.affine_select(out=SLT[:], in_=SLT[:], compare_op=ALU.is_gt, fill=0.0, base=0,
                            pattern=[[1, P]], channel_multiplier=-1).then_inc(consts, 1)

            g.wait_ge(proj_done, 21)
            g.memset(ZERO[:], 0.0).then_inc(zeros, 1)
            def keep_past(buf):
                ap = bass.AP(buf[:].tensor, 0, [[2048, P], [T + P, NT], [1, P]])
                return g.affine_select(out=ap, in_=ap, compare_op=ALU.is_gt, fill=0.0, base=0,
                                       pattern=[[0, NT], [1, P]], channel_multiplier=-1)

            def first(u):
                if UNITS[u][0] == "sb":
                    g.wait_ge(drop_ready, nth(u, "sb"))
                    keep_past(UB2[u % 2]).then_inc(drop_masked, 1)

            def second(u):
                if UNITS[u][0] == "sb":
                    g.wait_ge(stick_ready, nth(u, "sb"))
                    keep_past(UB1[u % 2]).then_inc(stick_masked, 1)

            first(0)
            for u in range(len(UNITS)):
                if u + 1 < len(UNITS):
                    first(u + 1)
                second(u)
            g.wait_ge(set_free, len(UNITS))
            g.wait_ge(mod_used, 12)
            g.iota(IOTAE, pattern=[[1, E]], base=0, channel_multiplier=0, allow_small_or_imprecise_dtypes=True)
            g.iota(IOTA48, pattern=[[1, 48]], base=0, channel_multiplier=0, allow_small_or_imprecise_dtypes=True)
            g.iota(IOTA[:], pattern=[[1, P]], base=0, channel_multiplier=0, allow_small_or_imprecise_dtypes=True)
            step(g.memset(ID2[:], 0.0))
            for half in range(2):
                step(g.affine_select(out=ID2[:], in_=ID2[:], compare_op=ALU.not_equal, fill=1.0, base=-32 * half,
                                     pattern=[[-1, E]], channel_multiplier=1))
            g.memset(TILE0[:], 0.0)
            g.memset(TILE_P[:], float(P)).then_inc(iotas, 1)
            g.wait_ge(iotas, 1)
            g.wait_ge(routed, 1)
            last_tile = g.value_load(LAST[0:1, 0:1], min_val=15, max_val=MAX_TILES - 1)

            def slots(e, i_next):
                g.tensor_copy(GMC[:], GM[:, :, bass.ds(e, 1)].rearrange("p t e -> p (t e)")).then_inc(tile_step, 1)
                g.wait_ge(tile_step, i_next * 2 - 1)
                g.tensor_tensor(GMS[:], GMC[:], TILE0[:].broadcast_to([P, NT]), ALU.subtract).then_inc(cols_ready, 1)
                g.wait_ge(cols_ready, i_next * 1)
                g.tensor_tensor(TILE0[:], TILE0[:], TILE_P[:], ALU.add).then_inc(tile_step, 1)
                g.wait_ge(tile_step, i_next * 2)

            def selector(e):
                g.tensor_copy(SEL[:], ID2[:, bass.ds(e, 1)].broadcast_to([64, P])).then_inc(sel_ready, 1)

            def gated(h, n):
                g.wait_ge(up_ready, n)
                g.wait_ge(gate_ready, n)
                g.tensor_tensor(UC[:], UC[:], GC[:], ALU.mult).then_inc(gated_up, 1)
                g.wait_ge(gated_up, n)
                g.wait_ge(sig_ready, n)
                g.tensor_tensor(AC[:, h], UC[:], SG[:], ALU.mult).then_inc(act_ready, 1)

            e = g.value_load(TILE_E[0:1, 0:1], min_val=0, max_val=E - 1)
            slots(e, 1)
            selector(e)
            with g.Fori(0, last_tile) as i:
                gated(0, i * 2 + 1)
                e = g.value_load(TILE_E[0:1, bass.ds(i + 1, 1)], min_val=0, max_val=E - 1)
                g.wait_ge(s_ready, i + 1)
                slots(e, i + 2)
                gated(1, i * 2 + 2)
                g.wait_ge(sel_used, i + 1)
                selector(e)
            i = last_tile
            gated(0, i * 2 + 1)
            gated(1, i * 2 + 2)
            g.wait_ge(ys_ready, 1)
            for n in range(NT * TOPK):
                if n >= 8:
                    g.wait_ge(rows_used, n - 7)
                g.indirect_dma_start(GR[:, n % 8, :], None, ys,
                                     bass.IndirectOffsetOnAxis(ap=SI[:, n // TOPK, n % TOPK:n % TOPK + 1], axis=0)
                                     ).then_inc(rows_in[n % 8], 16)
    return nc


_INS = ["x", "c", "w_in", "w_out", "g_norm_mix", "g_norm_ffn", "g_group", "w_mod", "b_mod", "swa_sinks", "rel_bias",
        "w_router", "b_router", "w_gate_up", "b_gate_up", "w_down", "b_down", "g_final"]


def kernel(**inputs):
    import concourse.bacc as bacc
    from concourse.bass_utils import run_bass_kernel_spmd

    onehot, masks = dist_tables()
    nc = bacc.Bacc("TRN2", target_bir_lowering=False, num_devices=1)
    arrays, args = {}, []
    given = {n: inputs[n] for n in _INS}
    given["onehot"], given["masks"] = onehot, masks
    for name, a in given.items():
        a = np.ascontiguousarray(a)
        arrays[f"in_{name}"] = a
        args.append(nc.dram_tensor(f"in_{name}", a.shape, mybir.dt.from_np(a.dtype), kind="ExternalInput").ap())
    out = nc.dram_tensor("out_dram", (1, T, D), F32, kind="ExternalOutput").ap()
    build(nc, *args, out)
    r = run_bass_kernel_spmd(nc, [arrays], core_ids=[0])
    return r.results[0]["out_dram"]
```

```python
from contextlib import ExitStack

import numpy as np

import concourse.bass as bass
from concourse import mybir

F32 = mybir.dt.float32
F32R = mybir.dt.float32r
I32 = mybir.dt.int32
U32 = mybir.dt.uint32
ALU = mybir.AluOpType
ACT = mybir.ActivationFunctionType
AX = mybir.AxisListType.X

P = 128
D = 1024
T = 512
NT = T // P
C = D // P
HD = 64
E = 32
TOPK = 4
BUCKETS = 32
EPS = 1e-6
NEG = -1e30
LIMIT = 7.0
ALPHA = 1.702
MAX_TILES = T * TOPK // P + E - 1
BAND = 384

SB_Q, SB_K, SB_V, SW_Q, SW_K, SW_V, MB_Q, MB_K, MB_V, IN_W = 0, 256, 512, 768, 1280, 1408, 1536, 1792, 2048, 2304

Q_COLS = [SB_Q, SB_Q + P, SB_K, SB_K + P, *range(SW_Q, SW_K, P), SW_K, MB_Q, MB_Q + P, MB_K, MB_K + P]
UNITS = [("sb", 0), ("sw", 0), ("mb", 0), ("sw", 1), ("sb", 1), ("sw", 2), ("mb", 1), ("sw", 3),
         ("sb", 2), ("sw", 4), ("mb", 2), ("sw", 5), ("sb", 3), ("sw", 6), ("mb", 3), ("sw", 7)]
SOFT_UNITS = sum(kind != "sb" for kind, _ in UNITS)
ROWS = [("gt1", 2), ("sc2", 4), ("sh2", 3), ("gt2", 5)]
RING = 6
CHUNKS = 12


def dist_tables():
    d = 255 - np.arange(BAND)
    n = np.maximum(d, 0)
    exact = BUCKETS // 2
    nf = np.maximum(n, 1).astype(np.float32)
    large = exact + (np.log(nf / np.float32(exact)) / np.float32(np.log(128 / exact))
                     * np.float32(BUCKETS - exact)).astype(np.int32)
    bucket = np.where(n < exact, n, np.minimum(large, BUCKETS - 1))
    onehot = (bucket[None, :] == np.arange(BUCKETS)[:, None]).astype(np.float32)
    masks = np.zeros((12, BAND), np.float32)
    masks[:, d < 0] = NEG
    masks[:8, d >= 128] = NEG
    return onehot, masks


def build(nc, x, c, w_in, w_out, g_mix, g_ffn, g_group, w_mod, b_mod, sinks, table, w_router, b_router,
          w_gate_up, b_gate_up, w_down, b_down, g_final, onehot, masks, out):
    band_dram = nc.dram_tensor("band_dram", (12, P, BAND), F32, kind="Internal").ap()
    h2_dram = nc.dram_tensor("h2_dram", (T, D), F32, kind="Internal").ap()
    ys = nc.dram_tensor("ys", (T * TOPK, D), F32, kind="Internal").ap()

    ctx = ExitStack()
    with ctx:
        BASE = 16896

        def at(name, kb, shape, dt=F32):
            return nc.alloc_sbuf_tensor_at(name, shape, dt, offset=BASE + int(kb * 1024))

        def sem(name):
            return ctx.enter_context(nc.semaphore(name))

        PS = ctx.enter_context(nc.psum_tensor("PS", [P, 8, 512], F32))
        PSF = PS[:].rearrange("p b n -> p (b n)")

        X = at("X", 0, [P, NT, D])
        RINGB = at("RINGB", 16, [P, RING, 2048])
        WIN = at("WIN", 16, [P, C, IN_W])
        WOUT = at("WOUT", 32, [P, C, D])
        MERG = at("MERG", 64, [P, NT, D])
        UB1 = [at("UA1", 176, [P, 2048]), at("UB1", 184, [P, 2048])]
        UB2 = [at("UA2", 80, [P, 2048]), at("UB2", 16, [P, 2048])]
        ROW = {"sc2": at("SC2", 88, [P, D]), "sh2": at("SH2", 92, [P, D]),
               "gt1": at("GT1", 196, [P, D]), "gt2": at("GT2", 200, [P, D])}
        MB = at("MB", 96, [P, 2, C, 512])
        QKT = at("QKT", 128, [P, 13, T])
        KSW = at("KSW", 192, [P, T])
        V = at("V", 154, [P, NT, 640])
        HT = at("HT", 164, [P, C, T])
        XN = at("XN", 180, [P, NT, D])
        BT = at("BT", 164, [P, 12, 256])
        COL = [at("COL_SC", 164, [P, D]), at("COL_SH", 168, [P, D])]
        MT = at("MT", 128, [P, C, T])
        MTF = MT[:].rearrange("p c t -> p (c t)").rearrange("p (t d) -> p t d", t=NT)
        XN2 = at("XN2", 64, [P, NT, D])
        H2T = at("H2T", 96, [P, C, T])
        BW = at("BW", 164, [64, 3 * D])
        BHT = at("BHT", 176, [64, 3 * D], F32R)
        BR = at("BR", 144, [64, 3 * D], F32R)
        WH = at("WH", 64, [P, 3, 2048], F32R)
        WL = at("WL", 88, [P, 3, 2048], F32R)
        XG = at("XG", 176, [P, D])
        XH = at("XH", 156, [P, C, P], F32R)
        XL = at("XL", 160, [P, C, P], F32R)
        AH = at("AH", 164, [P, 2, 4, P], F32R)
        AL = at("AL", 168, [P, 2, 4, P], F32R)
        Y = at("Y", 172, [P, D])
        GC = at("GC", 180, [P, 512])
        UC = at("UC", 182, [P, 512])
        SG = at("SG", 184, [P, 512])
        AC = at("AC", 186, [P, 2, 512])
        TOKF = at("TOKF", 190, [P, 2, 48])
        TOKC = at("TOKC", 190.5, [P, 2], I32)
        ROWC = at("ROWC", 190.53125, [P, 2], I32)
        SEL = at("SEL", 192, [64, P], F32R)
        TOKV = at("TOKV", 192.5, [P, NT * TOPK])
        ROWV = at("ROWV", 192.5625, [P, NT * TOPK])
        TILEV = at("TILEV", 192.625, [P, 48])
        IOTA = at("IOTA", 193, [P, P])
        ID2 = at("ID2", 193.5, [64, E])
        WJ = at("WJ", 193.75, [P, NT, 8])
        TILE_E = at("TILE_E", 194.0625, [1, 48], I32)
        LAST = at("LAST", 194.25, [1, 8], I32)
        WR = at("WR", 194.5, [P, C, E])
        BRT = at("BRT", 195.5, [P, E])
        ID = at("ID", 204, [P, P])
        NTRI = at("NTRI", 204.5, [P, P])
        NONE_ = at("NONE", 205, [P, P])
        ONES = at("ONES", 205.5, [P, P])
        SLT = at("SLT", 206, [P, P])
        SMALL = at("SMALL", 206.5, [P, 216])
        BANDH = at("BANDH", 172, [BUCKETS, BAND])
        BANDM = at("BANDM", 173.5, [12, BAND])
        BANDS = at("BANDS", 175, [12, BAND])
        GFFN = at("GFFN", 96, [P, D])
        TMP = [at("TMP0", 100, [P, D]), at("TMP1", 104, [P, D])]
        RT = at("RT", 156, [P, 32, P])

        def rt(a, b=0, t=NT):
            return RT[:, a, 0:b or P].rearrange("p (t e) -> p t e", t=t)

        L, M8, IF, LM, EXPJ = rt(0), rt(1, 32), rt(3, 32), rt(4, 32), rt(5, 32)
        I8 = RT[:, 2, 0:32].bitcast(U32).rearrange("p (t e) -> p t e", t=NT)
        OH = RT[:, 6:10, :].rearrange("p b (j e) -> p b j e", e=E)
        MK2, MK3, SLOT, MASK = rt(10), rt(11), rt(12), rt(16)
        SUM4 = RT[:, 13, 0:NT]
        CNT, TL, TSTART = RT[:, 13, 32:64], RT[:, 13, 64:96], RT[:, 13, 96:128]
        TEND = [RT[:, 14, 0:32], RT[:, 14, 32:64]]
        SJ = RT[:, 14, 64:80].rearrange("p (t j) -> p t j", t=NT)
        TE = RT[0:1, 14, 80:128]
        IOTAE = RT[:, 15, 0:E]
        IOTA48 = RT[0:1, 15, 64:112]
        TT = RT[0:1, 17:29, :].rearrange("p b n -> p (b n)").rearrange("p (i e) -> p i e", e=E)
        GR = at("GR", 16, [P, NT, TOPK, D])
        PAST = at("PAST", 112, [P, NT * TOPK, 48])
        INT = at("INT", 115, [P, NT * TOPK, 48])
        WHO = at("WHO", 118, [P, NT * TOPK, 2, 48])
        SLOTS = at("SLOTS", 124, [P, NT * TOPK, P])
        TA = at("TA", 132, [P, NT * TOPK])
        MA = at("MA", 132.0625, [P, NT * TOPK])
        EMPTY = at("EMPTY", 132.125, [P, 48])
        AC2 = at("AC2", 96, [P, NT, D])
        GF = at("GF", 112, [P, D])
        FJ = at("FJ", 116, [P, NT, D])

        _o = [0]

        def small(n):
            _o[0] += n
            return SMALL[:, _o[0] - n:_o[0]]

        cT, cS, gmixc, ggrc = (small(C) for _ in range(4))
        G1, SH1 = small(C), small(C)
        ss, rs = small(4), small(4)
        gss, grs = small(12), small(12)
        sinkb = small(8)
        farb = small(4)
        mx = [small(4), small(4)]
        negm = [small(4), small(4)]
        den = [small(4), small(4)]
        esink = [small(4), small(4)]
        rden = [small(4), small(4)]
        sg = small(C)
        BANDT = small(12)[0:BUCKETS]

        consts = sem("consts")
        x_in, c_in, band_in = sem("x_in"), sem("c_in"), sem("band_in")
        win_in = [sem(f"win_in{s}") for s in range(3)]
        swap_in = sem("swap_in")
        wout_in, wr_in, bias_in, misc_in = sem("wout_in"), sem("wr_in"), sem("bias_in"), sem("misc_in")
        mod_in = [sem("mod_in0"), sem("mod_in1")]
        act_step, dve_step, pool_step = sem("act_step"), sem("dve_step"), sem("pool_step")
        mod_used, rows_kept = sem("mod_used"), sem("rows_kept")
        dve_mean, slots_ready, g_ffn_in, iotas, sum_ready = (sem("dve_mean"), sem("slots_ready"), sem("g_ffn_in"),
                                                          sem("iotas"), sem("sum_ready"))
        c_silu, zeroed, mod_bias = sem("c_silu"), sem("zeroed"), sem("mod_bias")
        summed, totals = sem("summed"), sem("totals")
        squares, roots, xn_ready = sem("squares"), sem("roots"), sem("xn_ready")
        turned, kept = sem("turned"), sem("kept")
        proj_done, q_kept, v_kept = sem("proj_done"), sem("q_kept"), sem("v_kept")
        band_done, band_kept, band_out = sem("band_done"), sem("band_kept"), sem("band_out")
        scores_done, set_free, pv_done = sem("scores_done"), sem("set_free"), sem("pv_done")
        logs_ready, drop_ready, drop_masked = sem("logs_ready"), sem("drop_ready"), sem("drop_masked")
        sums_done, stick_ready, stick_masked = sem("sums_done"), sem("stick_ready"), sem("stick_masked")
        max_ready, probs_ready, probs_turned, pt_kept = (sem("max_ready"), sem("probs_ready"), sem("probs_turned"),
                                                         sem("pt_kept"))
        wout_done, wout_kept = sem("wout_done"), sem("wout_kept")
        logits_done, mask_ready, ranks_done = sem("logits_done"), sem("mask_ready"), sem("ranks_done")
        routed, h2_out, bias_split = sem("routed"), sem("h2_out"), sem("bias_split")
        slots_placed, tables_ready, idx_step = sem("slots_placed"), sem("tables_ready"), sem("idx_step")
        row_step = sem("row_step")
        ring_in = [sem(f"ring_in{s}") for s in range(RING)]
        hi_done, lo_done, pe_chunk = sem("hi_done"), sem("lo_done"), sem("pe_chunk")
        gu_done, act_turned, gathered, sel_used = sem("gu_done"), sem("act_turned"), sem("gathered"), sem("sel_used")
        rows_turned = sem("rows_turned")
        gate_ready, up_ready, sig_ready, act_ready = (sem("gate_ready"), sem("up_ready"), sem("sig_ready"),
                                                      sem("act_ready"))
        ah_ready, al_ready, xh_ready, xl_ready = sem("ah_ready"), sem("al_ready"), sem("xh_ready"), sem("xl_ready")
        y_kept, y_free, y_stored = sem("y_kept"), sem("y_free"), sem("y_stored")
        gated_up, sel_ready = sem("gated_up"), sem("sel_ready")
        rows_in = [sem(f"rows_in{t}") for t in range(NT)]
        rows_used, final_ready, stored = sem("rows_used"), sem("final_ready"), sem("stored")

        block = ctx.enter_context(nc.Block())

        x_v = x[0].rearrange("(t p) d -> p t d", p=P)
        out_v = out[0].rearrange("(t p) d -> p t d", p=P)
        wmod_v = w_mod[0].rearrange("(p k) (v h n) -> v h p k n", p=P, v=6, h=2)
        bmod_v = b_mod[0].rearrange("(v a n) -> v a n", v=6, a=1)
        gu_v = w_gate_up.rearrange("l e (p k) (g h n) -> (l e) h p (k g) n", p=P, g=2, h=2)
        down_v = w_down.rearrange("l e (h p q r) n -> (l e) h q p (r n)", h=2, p=P, q=2)

        def col8(v):
            return v.rearrange("(p k) -> p k", k=C)

        def rep(v, n):
            return v.rearrange("(a n) -> a n", a=1).broadcast_to([P, n])

        SUMS = [(1, COL[0]), (0, COL[1])] + [(v, ROW[name]) for name, v in ROWS]

        def nth(u, *kinds):
            return sum(k in kinds for k, _ in UNITS[:u + 1])

        def sb_blocks():
            return [(qt, kt) for qt in range(NT) for kt in range(qt + 1)]

        def sw_blocks():
            return [(qt, kt) for qt in range(NT) for kt in ((qt - 1, qt) if qt else (0,))]

        @block.sync
        def _(sp):
            sp.dma_start(cT, col8(c[0])).then_inc(c_in, 16)
            sp.dma_start(gmixc, col8(g_mix[0])).then_inc(c_in, 16)
            sp.dma_start(X[:], x_v).then_inc(x_in, 16)
            sp.wait_ge(zeroed, 1)
            for v, buf in SUMS:
                sp.dma_start(buf[0:1, :], bmod_v[v]).then_inc(mod_bias, 16)

            def mod_chunk(n):
                b = n % 2
                if n >= 2:
                    sp.wait_ge(mod_used, n - 1)
                sp.dma_start(MB[:, b], wmod_v[SUMS[n // 2][0], n % 2]).then_inc(mod_in[b], 16)

            for n in range(4):
                mod_chunk(n)
            for part in range(3):
                sp.dma_start(WIN[:, :, part * 768:(part + 1) * 768],
                             w_in[0].rearrange("(p k) n -> p k n", p=P)[:, :, part * 768:(part + 1) * 768]
                             ).then_inc(win_in[part], 16)
            sp.dma_start(ggrc, col8(g_group[0])).then_inc(misc_in, 16)
            sp.dma_start(sinkb, sinks[0:1, :].broadcast_to([P, 8])).then_inc(misc_in, 16)
            sp.dma_start(farb, table[31:32, 8:12].broadcast_to([P, 4])).then_inc(misc_in, 16)
            for n in range(4, 12):
                mod_chunk(n)
            sp.wait_ge(q_kept, 9)
            for p0 in (0, 64):
                sp.dma_start(KSW[p0:p0 + 64, :], QKT[64 - p0:128 - p0, 8, :]).then_inc(swap_in, 16)
            sp.wait_ge(band_out, 16)
            sp.wait_ge(proj_done, 21)
            sp.dma_start(BT[:], bass.AP(band_dram.tensor, P - 1, [[BAND - 1, P], [P * BAND, 12], [1, 256]])).then_inc(band_in, 16)
            sp.dma_start(WOUT[:], w_out[0].rearrange("(p k) n -> p k n", p=P)).then_inc(wout_in, 16)
            sp.wait_ge(mod_used, 12)
            sp.dma_start(GFFN[:], rep(g_ffn[0], D)).then_inc(g_ffn_in, 16)
            sp.dma_start(WR[:], w_router[0].rearrange("(p k) e -> p k e", p=P)).then_inc(wr_in, 16)
            sp.dma_start(BRT[:], b_router[0:1, :].broadcast_to([P, E])).then_inc(wr_in, 16)
            sp.wait_ge(set_free, len(UNITS))
            for k in range(2):
                sp.dma_start(BW[32 * k:32 * k + 32, 0:2 * D], b_gate_up[0]).then_inc(bias_in, 16)
                sp.dma_start(BW[32 * k:32 * k + 32, 2 * D:3 * D], b_down[0]).then_inc(bias_in, 16)
            for t in range(NT):
                sp.wait_ge(xn_ready, 2 * NT + t + 1)
                sp.dma_start(h2_dram[t * P:(t + 1) * P, :], XN2[:, t, :]).then_inc(h2_out, 16)
            sp.wait_ge(wout_done, NT)
            sp.wait_ge(routed, 1)
            last_tile = sp.value_load(LAST[0:1, 0:1], min_val=15, max_val=MAX_TILES - 1)

            def load(e, i, k, src):
                if not (isinstance(i, int) and 4 + CHUNKS * i + k < RING):
                    sp.wait_ge(lo_done, i * CHUNKS + (k + 1))
                slot = (4 + k) % RING
                kind, h, q = src
                if kind == "gu":
                    sp.dma_start(RINGB[:, slot, :].rearrange("p (k n) -> p k n", n=512),
                                 gu_v[bass.ds(e, 1), h, :, 4 * q:4 * q + 4, :].rearrange("a p k n -> (a p) k n")
                                 ).then_inc(ring_in[slot], 16)
                else:
                    sp.dma_start(RINGB[:, slot, :],
                                 down_v[bass.ds(e, 1), h, q].rearrange("a p n -> (a p) n")).then_inc(ring_in[slot], 16)

            e0 = sp.value_load(TILE_E[0:1, 0:1], min_val=0, max_val=E - 1)
            for q in range(4):
                load(e0, 0, q - 4, ("gu", 0, q))
            with sp.Fori(0, last_tile) as i:
                e = sp.value_load(TILE_E[0:1, bass.ds(i, 1)], min_val=0, max_val=E - 1)
                en = sp.value_load(TILE_E[0:1, bass.ds(i + 1, 1)], min_val=0, max_val=E - 1)
                for q in range(4):
                    load(e, i, q, ("gu", 1, q))
                for q in range(2):
                    load(e, i, 4 + q, ("dn", 0, q))
                for q in range(4):
                    load(en, i, 6 + q, ("gu", 0, q))
                for q in range(2):
                    load(e, i, 10 + q, ("dn", 1, q))
            i = last_tile
            e = sp.value_load(TILE_E[0:1, bass.ds(i, 1)], min_val=0, max_val=E - 1)
            for q in range(4):
                load(e, i, q, ("gu", 1, q))
            for q in range(2):
                load(e, i, 4 + q, ("dn", 0, q))
            for q in range(2):
                load(e, i, 6 + q, ("dn", 1, q))
            sp.wait_ge(pe_chunk, last_tile * CHUNKS + CHUNKS)
            sp.dma_start(GF[:], rep(g_final, D)).then_inc(misc_in, 16)
            sp.wait_ge(y_stored, last_tile * 16 + 16)
            for t in range(NT):
                sp.dma_start(GR[:, t], ys[t * P * TOPK:(t + 1) * P * TOPK, :].rearrange("(p j) d -> p j d", j=TOPK)
                             ).then_inc(rows_in[t], 16)
            for t in range(NT):
                sp.wait_ge(final_ready, t + 1)
                sp.dma_start(out_v[:, t, :], AC2[:, t, :]).then_inc(stored, 16)
            sp.wait_ge(stored, 16 * NT)

        @block.tensor
        def _(pe):
            pe.wait_ge(consts, 1)
            pe.wait_ge(band_in, 48)
            pe.matmul(PS[0:12, 6, 0:BAND], BANDT, BANDH[:], start=True, stop=True).then_inc(band_done, 1)
            def turn(src, j, bank):
                for t in range(NT):
                    last = pe.transpose(PS[:, bank, t * P:(t + 1) * P], src[:, t, j:D:C], ID[:])
                last.then_inc(turned, 1)

            pe.wait_ge(xn_ready, NT)
            for j in range(6):
                turn(XN, j, j)
            for v in range(2):
                pe.wait_ge(summed, v + 1)
                for j in range(C):
                    mm = pe.matmul(PS[:, 7, C * v + j:C * v + j + 1], COL[v][:, j:D:C], ONES[:, 0:1],
                                   start=True, stop=True)
            mm.then_inc(totals, 1)
            for j in range(6, C):
                pe.wait_ge(kept, j - 5)
                turn(XN, j, j % 6)
            pe.wait_ge(kept, C)

            def bank_free(n):
                if n >= 19:
                    pe.wait_ge(v_kept, n - 18)
                elif n >= 6:
                    pe.wait_ge(q_kept, n - 5)

            n = 0
            for blk in range(13):
                if blk in (0, 4, 9):
                    pe.wait_ge(win_in[(0, 4, 9).index(blk)], 16)
                bank_free(n)
                for k in range(C):
                    lhs = WIN[:, k, Q_COLS[blk]:Q_COLS[blk] + P]
                    mm = pe.matmul(PS[:, n % 6, :], lhs, HT[:, k, :], start=(k == 0), stop=(k == C - 1))
                mm.then_inc(proj_done, 1)
                n += 1
            for t in range(NT):
                bank_free(n)
                for col, width, o in ((SB_V, 256, 0), (SW_V, P, 256)):
                    for k in range(C):
                        mm = pe.matmul(PS[:, n % 6, o:o + width], HT[:, k, t * P:(t + 1) * P],
                                       WIN[:, k, col:col + width], start=(k == 0), stop=(k == C - 1))
                mm.then_inc(proj_done, 1)
                n += 1
                bank_free(n)
                for k in range(C):
                    mm = pe.matmul(PS[:, n % 6, 0:256], HT[:, k, t * P:(t + 1) * P],
                                   WIN[:, k, MB_V:MB_V + 256], start=(k == 0), stop=(k == C - 1))
                mm.then_inc(proj_done, 1)
                n += 1
            for r, (name, _) in enumerate(ROWS):
                pe.wait_ge(summed, r + 3)
                if r >= 1:
                    pe.wait_ge(rows_kept, r)
                for h in range(2):
                    mm = pe.matmul(PS[:, 6 + h, :], ONES[:], ROW[name][:, h * 512:(h + 1) * 512], start=True, stop=True)
                mm.then_inc(totals, 1)
            pe.wait_ge(q_kept, 13)
            pe.wait_ge(v_kept, 8)
            pe.wait_ge(swap_in, 32)
            pe.wait_ge(rows_kept, 4)

            def q_k(kind, h):
                p0 = 64 * (h % 2)
                if kind == "sb":
                    return QKT[p0:p0 + 64, h // 2, :], QKT[p0:p0 + 64, 2 + h // 2, :]
                if kind == "mb":
                    return QKT[p0:p0 + 64, 9 + h // 2, :], QKT[p0:p0 + 64, 11 + h // 2, :]
                k = QKT[p0:p0 + 64, 8, :] if h // 4 == h % 2 else KSW[p0:p0 + 64, :]
                return QKT[p0:p0 + 64, 4 + h // 2, :], k

            def scores(u):
                kind, h = UNITS[u]
                q, k = q_k(kind, h)
                s0 = 4 * (u % 2)
                if u >= 2:
                    pe.wait_ge(set_free, u - 1)
                for t in range(NT):
                    if kind == "sb":
                        mm = pe.matmul(PS[:, s0 + t, t * P:T], k[:, t * P:(t + 1) * P], q[:, t * P:T],
                                       start=True, stop=True)
                    elif kind == "sw":
                        lo = max(t - 1, 0) * P
                        o = 256 * (t % 2) + (0 if t else P)
                        mm = pe.matmul(PS[:, s0 + t // 2, o:256 * (t % 2) + 256], q[:, t * P:(t + 1) * P],
                                       k[:, lo:(t + 1) * P], start=True, stop=True)
                    else:
                        mm = pe.matmul(PS[:, s0 + t, 0:(t + 1) * P], q[:, t * P:(t + 1) * P], k[:, 0:(t + 1) * P],
                                       start=True, stop=True)
                mm.then_inc(scores_done, 1)

            def middle(u):
                kind, h = UNITS[u]
                s0 = 4 * (u % 2)
                if kind == "sb":
                    pe.wait_ge(drop_masked, nth(u, "sb"))
                    drop = UB2[u % 2][:].rearrange("p (t n) -> p t n", t=NT)
                    for kt in range(NT):
                        for jt in range(kt, NT):
                            mm = pe.matmul(PS[:, s0 + kt, jt * P:T], (NTRI if jt == kt else NONE_)[:],
                                           drop[:, jt, jt * P:T], start=False, stop=(jt == NT - 1),
                                           skip_group_check=True)
                    mm.then_inc(sums_done, 1)
                else:
                    pe.wait_ge(probs_ready, nth(u, "sw", "mb"))
                    wide = 256 if kind == "sw" else T
                    probs = UB1[u % 2][:, 0:NT * wide].rearrange("p (t n) -> p t n", t=NT)
                    bls = sw_blocks() if kind == "sw" else sb_blocks()
                    b0 = s0 + (2 if kind == "sw" else 0)
                    for n, (qt, kt) in enumerate(bls):
                        o = (kt - qt + 1) * P if kind == "sw" else kt * P
                        mm = pe.transpose(PS[:, b0 + n // 4, (n % 4) * P:(n % 4 + 1) * P], probs[:, qt, o:o + P], ID[:])
                    mm.then_inc(probs_turned, 1)

            def values(u):
                kind, h = UNITS[u]
                s0 = 4 * (u % 2)
                vo = {"sb": h * HD, "sw": 256 + (h // 4) * HD, "mb": 384 + h * HD}[kind]
                ob = s0 + (3 if kind == "mb" else 0)
                if kind == "sb":
                    pe.wait_ge(stick_masked, nth(u, "sb"))
                else:
                    pe.wait_ge(pt_kept, nth(u, "sw", "mb"))
                bls = sw_blocks() if kind == "sw" else sb_blocks()
                for n, (qt, kt) in enumerate(bls):
                    lhs = (UB1[u % 2][:, kt * T + qt * P:kt * T + (qt + 1) * P] if kind == "sb"
                           else UB2[u % 2][:, n * P:(n + 1) * P])
                    first = kt == (max(qt - 1, 0) if kind == "sw" else 0)
                    mm = pe.matmul(PS[:, ob, qt * HD:(qt + 1) * HD], lhs, V[:, kt, vo:vo + HD],
                                   start=first, stop=(kt == qt))
                mm.then_inc(pv_done, 1)

            scores(0)
            for u in range(len(UNITS)):
                if u + 1 < len(UNITS):
                    scores(u + 1)
                middle(u)
                values(u)
            pe.wait_ge(xn_ready, 2 * NT)
            for j in range(C):
                if j >= 6:
                    pe.wait_ge(kept, C + j - 5)
                turn(MERG, j, j % 6)
            pe.wait_ge(wout_in, 16)
            pe.wait_ge(kept, 2 * C)
            for t in range(NT):
                if t >= 3:
                    pe.wait_ge(wout_kept, t - 2)
                for h in range(2):
                    for k in range(C):
                        mm = pe.matmul(PS[:, 2 * (t % 3) + h, :], MT[:, k, t * P:(t + 1) * P],
                                       WOUT[:, k, h * 512:(h + 1) * 512], start=(k == 0), stop=(k == C - 1))
                mm.then_inc(wout_done, 1)
            pe.wait_ge(xn_ready, 3 * NT)
            pe.wait_ge(wout_kept, NT)
            for j in range(C):
                if j >= 6:
                    pe.wait_ge(kept, 2 * C + j - 5)
                turn(XN2, j, j % 6)
            pe.wait_ge(wr_in, 32)
            pe.wait_ge(kept, 3 * C)
            for t in range(NT):
                for k in range(C):
                    mm = pe.matmul(PS[:, 6, t * E:(t + 1) * E], H2T[:, k, t * P:(t + 1) * P], WR[:, k, :],
                                   start=(k == 0), stop=(k == C - 1))
            mm.then_inc(logits_done, 1)
            pe.wait_ge(mask_ready, 1)
            for t in range(NT):
                for s in range(t + 1):
                    mm = pe.matmul(PS[:, 7, t * E:(t + 1) * E], (SLT if s == t else ONES)[:], MASK[:, s, :],
                                   start=(s == 0), stop=(s == t))
            for s in range(NT):
                mm = pe.matmul(PS[:, 7, P:P + E], ONES[:], MASK[:, s, :], start=(s == 0), stop=(s == NT - 1))
            mm.then_inc(ranks_done, 1)

            pe.wait_ge(slots_placed, 1)
            for n in range(NT * TOPK):
                mm = pe.matmul(PS[:, 6, 0:96], SLOTS[:, n, :], WHO[:, n].rearrange("p a i -> p (a i)"),
                               start=(n == 0), stop=(n == NT * TOPK - 1))
            mm.then_inc(slots_ready, 1)

            def turn_rows(n):
                pe.wait_ge(gathered, n * 16)
                for j in range(C):
                    mm = pe.transpose(PS[:, j // 4, (j % 4) * P:(j % 4 + 1) * P], XG[:, j:D:C], ID[:])
                mm.then_inc(rows_turned, 1)

            def chunk(i, k, xh, xl, banks, js, first, last):
                pe.wait_ge(lo_done, i * CHUNKS + (k + 7))
                b = (4 + k) % 3
                for a, j in enumerate(js):
                    for g in range(2):
                        o = (2 * a + g) * 512
                        for n, (xs, ws) in enumerate(((xh, WH), (xl, WH), (xh, WL))):
                            mm = pe.matmul(PS[:, banks + g, :], xs[:, j, :], ws[:, b, o:o + 512],
                                           start=(first and a == 0 and n == 0),
                                           stop=(last and a == 1 and n == 2), skip_group_check=True)
                mm.then_inc(pe_chunk, 1)

            def turn_act(h, n):
                pe.wait_ge(act_ready, n)
                for r in range(4):
                    mm = pe.transpose(PS[:, 2 + 2 * h, r * P:(r + 1) * P], AC[:, h, r:512:4], ID[:])
                mm.then_inc(act_turned, 1)

            def gate_up(i, k0, h, n, turned_half=None):
                for q in range(4):
                    if q == 3 and turned_half is not None:
                        turn_act(*turned_half)
                    chunk(i, k0 + q, XH, XL, 2 + 2 * h, (2 * q, 2 * q + 1), q == 0, False)
                for g in range(2):
                    o = g * D + h * 512
                    mm = pe.matmul(PS[:, 2 + 2 * h + g, :], SEL[:], BR[:, o:o + 512], start=False, stop=True,
                                   skip_group_check=True)
                mm.then_inc(gu_done, 1)

            def down(i, k0, h):
                pe.wait_ge(al_ready, i * 2 + (h + 1))
                if h == 0:
                    pe.wait_ge(y_kept, i + 1)
                    for g in range(2):
                        o = 2 * D + g * 512
                        mm = pe.matmul(PS[:, 6 + g, :], SEL[:], BR[:, o:o + 512], start=True, stop=False,
                                       skip_group_check=True)
                    mm.then_inc(sel_used, 1)
                for q in range(2):
                    chunk(i, k0 + q, AH[:, h], AL[:, h], 6, (2 * q, 2 * q + 1), False, h == 1 and q == 1)

            pe.wait_ge(bias_split, 1)
            pe.wait_ge(tables_ready, 1)
            last_tile = pe.value_load(LAST[0:1, 0:1], min_val=15, max_val=MAX_TILES - 1)
            turn_rows(1)
            pe.wait_ge(xl_ready, 1)
            pe.wait_ge(sel_ready, 1)
            gate_up(0, -4, 0, 1)
            with pe.Fori(0, last_tile) as i:
                gate_up(i, 0, 1, i * 2 + 2, (0, i * 2 + 1))
                turn_rows(i + 2)
                down(i, 4, 0)
                turn_act(1, i * 2 + 2)
                pe.wait_ge(xl_ready, i + 2)
                pe.wait_ge(sel_ready, i + 2)
                gate_up(i, 6, 0, i * 2 + 3)
                down(i, 10, 1)
            i = last_tile
            gate_up(i, 0, 1, i * 2 + 2, (0, i * 2 + 1))
            down(i, 4, 0)
            turn_act(1, i * 2 + 2)
            down(i, 6, 1)

        @block.scalar
        def _(act):
            done = [0]

            def step(ins):
                done[0] += 1
                ins.then_inc(act_step, 1)
                act.wait_ge(act_step, done[0])

            act.dma_start(BANDH[:], onehot).then_inc(band_in, 16)
            act.dma_start(BANDT, table).then_inc(band_in, 16)
            act.dma_start(BANDM[:], masks).then_inc(band_in, 16)
            act.wait_ge(c_in, 32)
            act.activation(sg, cT, ACT.Sigmoid).then_inc(roots, 1)

            def norm_sums(src, n, junk):
                for t in range(NT):
                    last = act.activation(junk[:, t, :], src[:, t, :], ACT.Square, accum_out=ss[:, t:t + 1])
                last.then_inc(squares, 1)
                act.wait_ge(dve_mean, n)
                act.activation(rs, rs, ACT.Sqrt).then_inc(roots, 1)

            act.wait_ge(x_in, 16)
            norm_sums(X, 1, XN)
            act.wait_ge(band_kept, 1)
            act.dma_start(band_dram, BANDS[:].unsqueeze(1).broadcast_to([12, P, BAND])).then_inc(band_out, 16)
            for n in range(13, 21):
                act.wait_ge(proj_done, n + 1)
                t, part = divmod(n - 13, 2)
                if part == 0:
                    act.activation(V[:, t, 0:384], PS[:, n % 6, 0:384], ACT.Copy).then_inc(v_kept, 1)
                else:
                    act.activation(V[:, t, 384:640], PS[:, n % 6, 0:256], ACT.Copy).then_inc(v_kept, 1)
            act.wait_ge(misc_in, 48)

            def first(u):
                kind, h = UNITS[u]
                s = u % 2
                s0 = 4 * s
                a, b = UB1[s], UB2[s]
                if kind == "sb":
                    act.wait_ge(scores_done, u + 1)
                    av = a[:].rearrange("p (t n) -> p t n", t=NT)
                    for t in range(NT):
                        last = act.activation(av[:, t, t * P:T], PS[:, s0 + t, t * P:T], ACT.Abs)
                    step(last)
                    for t in range(NT):
                        last = act.activation(av[:, t, t * P:T], av[:, t, t * P:T], ACT.Exp, scale=-1.0)
                    step(last)
                    for t in range(NT):
                        last = act.activation(av[:, t, t * P:T], av[:, t, t * P:T], ACT.Ln, bias=1.0)
                    last.then_inc(logs_ready, 1)
                else:
                    act.wait_ge(max_ready, nth(u, "sw", "mb"))
                    wide = 256 if kind == "sw" else T
                    av = a[:, 0:NT * wide].rearrange("p (t n) -> p t n", t=NT)
                    for t in range(NT):
                        lo, hi = ((0 if t else P), 256) if kind == "sw" else (0, (t + 1) * P)
                        last = act.activation(av[:, t, lo:hi], av[:, t, lo:hi], ACT.Exp, bias=negm[s][:, t:t + 1],
                                              accum_out=den[s][:, t:t + 1])
                    if kind == "sw":
                        last = act.activation(esink[s], negm[s], ACT.Exp, bias=sinkb[:, h:h + 1])
                    last.then_inc(probs_ready, 1)

            def second(u):
                kind, h = UNITS[u]
                s = u % 2
                s0 = 4 * s
                a, b = UB1[s], UB2[s]
                if kind == "sb":
                    act.wait_ge(sums_done, nth(u, "sb"))
                    av = a[:].rearrange("p (t n) -> p t n", t=NT)
                    for t in range(NT):
                        last = act.activation(av[:, t, t * P:T], PS[:, s0 + t, t * P:T], ACT.Exp)
                    last.then_inc(stick_ready, 1)
                else:
                    act.wait_ge(probs_turned, nth(u, "sw", "mb"))
                    b0, n = (s0 + 2, 7) if kind == "sw" else (s0, 10)
                    act.activation(b[:, 0:n * P], PSF[:, b0 * 512:b0 * 512 + n * P], ACT.Copy).then_inc(pt_kept, 1)

            first(0)
            for u in range(len(UNITS)):
                if u + 1 < len(UNITS):
                    first(u + 1)
                second(u)
            act.wait_ge(set_free, len(UNITS))
            for g, (o, w) in enumerate(((0, 256), (256, 512), (768, 256))):
                for t in range(NT):
                    last = act.activation(MTF[:, t, o:o + w], MERG[:, t, o:o + w], ACT.Square,
                                          accum_out=gss[:, 4 * g + t:4 * g + t + 1])
            last.then_inc(squares, 1)
            act.wait_ge(dve_mean, 2)
            act.activation(grs, grs, ACT.Sqrt).then_inc(roots, 1)
            act.wait_ge(wout_kept, NT)
            norm_sums(X, 3, XN2)
            act.wait_ge(max_ready, SOFT_UNITS + 1)
            act.activation(EXPJ, LM, ACT.Exp).then_inc(probs_ready, 1)

            act.wait_ge(routed, 1)
            last_tile = act.value_load(LAST[0:1, 0:1], min_val=15, max_val=MAX_TILES - 1)
            act.wait_ge(h2_out, 16 * NT)

            act.sem_inc(y_kept, 1)
            act.sem_inc(y_free, 1)

            def hi(i, k):
                slot, b = (4 + k) % RING, (4 + k) % 3
                act.wait_ge(ring_in[slot], i * 32 + 16 * ((4 + k) // RING + 1))
                if not (isinstance(i, int) and 4 + CHUNKS * i + k < 3):
                    act.wait_ge(pe_chunk, i * CHUNKS + (k + 2))
                act.activation(WH[:, b, :], RINGB[:, slot, :], ACT.Copy).then_inc(hi_done, 1)

            def sig(n):
                act.wait_ge(gate_ready, n)
                act.activation(SG[:], GC[:], ACT.Sigmoid, scale=ALPHA).then_inc(sig_ready, 1)

            def keep_turned(h, n):
                act.wait_ge(act_turned, n)
                act.activation(AH[:, h].rearrange("p r m -> p (r m)"), PS[:, 2 + 2 * h, :], ACT.Copy
                               ).then_inc(ah_ready, 1)

            def keep_gathered(n):
                act.wait_ge(rows_turned, n)
                act.activation(XH[:].rearrange("p j m -> p (j m)"), PSF[:, 0:D], ACT.Copy).then_inc(xh_ready, 1)

            def keep_y(i, k):
                act.wait_ge(pe_chunk, i * CHUNKS + (k + 5))
                act.wait_ge(y_free, i + 1)
                act.activation(Y[:], PSF[:, 6 * 512:8 * 512], ACT.Copy).then_inc(y_kept, 1)

            for k in range(-4, -1):
                hi(0, k)
            keep_gathered(1)
            for k in range(-1, 1):
                hi(0, k)
            sig(1)
            for k in range(1, 3):
                hi(0, k)
            with act.Fori(0, last_tile) as i:
                hi(i, 3)
                hi(i, 4)
                hi(i, 5)
                keep_turned(0, i * 2 + 1)
                sig(i * 2 + 2)
                hi(i, 6)
                keep_gathered(i + 2)
                hi(i, 7)
                hi(i, 8)
                keep_turned(1, i * 2 + 2)
                hi(i, 9)
                hi(i, 10)
                hi(i, 11)
                sig(i * 2 + 3)
                hi(i, 12)
                hi(i, 13)
                hi(i, 14)
                keep_y(i, 11)
            i = last_tile
            hi(i, 3)
            hi(i, 4)
            hi(i, 5)
            keep_turned(0, i * 2 + 1)
            sig(i * 2 + 2)
            hi(i, 6)
            keep_turned(1, i * 2 + 2)
            hi(i, 7)
            keep_y(i, 7)
            for t in range(NT):
                act.wait_ge(sum_ready, t + 1)
                act.activation(FJ[:, t, :], AC2[:, t, :], ACT.Square,
                               accum_out=ss[:, t:t + 1]).then_inc(squares, 1)
                act.wait_ge(dve_mean, 4 + t)
                act.activation(rs[:, t:t + 1], rs[:, t:t + 1], ACT.Sqrt).then_inc(roots, 1)

        @block.vector
        def _(v):
            done = [0]

            def step(ins):
                done[0] += 1
                ins.then_inc(dve_step, 1)
                v.wait_ge(dve_step, done[0])

            v.wait_ge(roots, 1)
            v.tensor_tensor(cS, cT, sg, ALU.mult).then_inc(c_silu, 1)

            v.wait_ge(band_done, 1)
            v.wait_ge(band_in, 48)
            v.tensor_tensor(BANDS[:], PS[0:12, 6, 0:BAND], BANDM[:], ALU.add).then_inc(band_kept, 1)
            def rows_normed(n_sq, n_mean, n_root, src, dst):
                v.wait_ge(squares, n_sq)
                v.tensor_scalar(rs, ss, 1.0 / D, EPS, ALU.mult, ALU.add).then_inc(dve_mean, 1)
                v.wait_ge(roots, n_root)
                step(v.reciprocal(rs, rs))
                for t in range(NT):
                    v.tensor_scalar(dst[:, t, :], src[:, t, :], rs[:, t:t + 1], None, ALU.mult).then_inc(xn_ready, 1)

            rows_normed(1, 1, 2, X, XN)

            def add_chunk(n):
                buf = SUMS[n // 2][1][:, n % 2 * 512:(n % 2 + 1) * 512]
                v.wait_ge(mod_in[n % 2], 16 * (n // 2 + 1))
                if n % 2 == 0:
                    v.wait_ge(mod_bias, 16 * len(SUMS))
                for k in range(C):
                    last = v.scalar_tensor_tensor(out=buf, in0=MB[:, n % 2, k, :], scalar=cS[:, k:k + 1], in1=buf,
                                                  op0=ALU.mult, op1=ALU.add)
                    if k < C - 1:
                        step(last)
                last.then_inc(mod_used, 1)
                if n % 2:
                    v.wait_ge(mod_used, n + 1)
                    v.sem_inc(summed, 1)

            for n in range(4):
                add_chunk(n)
            v.wait_ge(totals, 1)
            v.tensor_copy(SH1, PS[:, 7, C:2 * C])
            step(v.scalar_tensor_tensor(out=G1, in0=PS[:, 7, 0:C], scalar=1.0, in1=gmixc, op0=ALU.add, op1=ALU.mult))
            v.wait_ge(band_out, 16)
            for j in range(C):
                v.wait_ge(turned, j + 1)
                v.tensor_scalar(HT[:, j, :], PS[:, j % 6, :], G1[:, j:j + 1], SH1[:, j:j + 1], ALU.mult, ALU.add
                                ).then_inc(kept, 1)
            for n in range(13):
                v.wait_ge(proj_done, n + 1)
                q = n in (0, 1, 4, 5, 6, 7, 9, 10)
                v.tensor_scalar(QKT[:, n, :], PS[:, n % 6, :], HD ** -0.5 if q else 1.0, None, ALU.mult
                                ).then_inc(q_kept, 1)
                if n >= 1 and n <= 8:
                    add_chunk(n + 3)
            for n, (name, _) in enumerate(ROWS):
                v.wait_ge(totals, n + 2)
                v.tensor_scalar(ROW[name][:], PSF[:, 6 * 512:8 * 512], 1.0 if name == "sc2" else 0.0, None, ALU.add
                                ).then_inc(rows_kept, 1)
            v.wait_ge(band_in, 64)
            v.wait_ge(misc_in, 48)

            def first(u):
                kind, h = UNITS[u]
                s = u % 2
                s0 = 4 * s
                a, b = UB1[s], UB2[s]
                if kind == "sb":
                    v.wait_ge(logs_ready, nth(u, "sb"))
                    av = a[:].rearrange("p (t n) -> p t n", t=NT)
                    bv = b[:].rearrange("p (t n) -> p t n", t=NT)
                    for t in range(NT):
                        last = v.scalar_tensor_tensor(out=bv[:, t, t * P:T], in0=PS[:, s0 + t, t * P:T], scalar=0.0,
                                                      in1=av[:, t, t * P:T], op0=ALU.max, op1=ALU.add)
                    last.then_inc(drop_ready, 1)
                    return
                v.wait_ge(scores_done, u + 1)
                if kind == "sw":
                    av = a[:, 0:NT * 256].rearrange("p (t n) -> p t n", t=NT)
                    pv = PSF[:, s0 * 512:s0 * 512 + NT * 256].rearrange("p (t n) -> p t n", t=NT)
                    v.tensor_tensor(av[:, 0, P:256], pv[:, 0, P:256], BT[:, h, P:256], ALU.add)
                    step(v.tensor_tensor(av[:, 1:NT, :], pv[:, 1:NT, :],
                                         BT[:, h, :].unsqueeze(1).broadcast_to([P, NT - 1, 256]), ALU.add))
                    v.tensor_reduce(mx[s][:, 0:1], av[:, 0, P:256], AX, ALU.max)
                    step(v.tensor_reduce(mx[s][:, 1:NT], av[:, 1:NT, :], AX, ALU.max))
                    v.tensor_scalar(negm[s], mx[s], sinkb[:, h:h + 1], -1.0, ALU.max, ALU.mult).then_inc(max_ready, 1)
                else:
                    av = a[:].rearrange("p (t n) -> p t n", t=NT)
                    for t in range(NT):
                        lo = max(t - 1, 0) * P
                        last = v.tensor_tensor(av[:, t, lo:(t + 1) * P], PS[:, s0 + t, lo:(t + 1) * P],
                                               BT[:, 8 + h, (0 if t else P):256], ALU.add)
                        if t >= 2:
                            last = v.tensor_scalar(av[:, t, 0:lo], PS[:, s0 + t, 0:lo], farb[:, h:h + 1], None, ALU.add)
                    step(last)
                    for t in range(NT):
                        last = v.tensor_reduce(mx[s][:, t:t + 1], av[:, t, 0:(t + 1) * P], AX, ALU.max)
                    step(last)
                    v.tensor_scalar(negm[s], mx[s], -1.0, None, ALU.mult).then_inc(max_ready, 1)

            def last_of(u):
                kind, h = UNITS[u]
                s = u % 2
                s0 = 4 * s
                if kind != "sb":
                    v.wait_ge(probs_ready, nth(u, "sw", "mb"))
                    if kind == "sw":
                        step(v.tensor_tensor(den[s], den[s], esink[s], ALU.add))
                    step(v.reciprocal(rden[s], den[s]))
                v.wait_ge(pv_done, u + 1)
                ob = s0 + (3 if kind == "mb" else 0)
                o = {"sb": 0, "sw": 256, "mb": 768}[kind] + h * HD
                src = PS[:, ob, 0:NT * HD].rearrange("p (t n) -> p t n", t=NT)
                if kind == "sb":
                    v.tensor_copy(MERG[:, :, o:o + HD], src).then_inc(set_free, 1)
                else:
                    v.tensor_tensor(MERG[:, :, o:o + HD], src, rden[s].unsqueeze(2).broadcast_to([P, NT, HD]),
                                    ALU.mult).then_inc(set_free, 1)

            first(0)
            for u in range(len(UNITS)):
                if u + 1 < len(UNITS):
                    first(u + 1)
                last_of(u)
            v.wait_ge(squares, 2)
            for g, w in enumerate((256, 512, 256)):
                last = v.tensor_scalar(grs[:, 4 * g:4 * g + 4], gss[:, 4 * g:4 * g + 4], 1.0 / w, EPS, ALU.mult, ALU.add)
            last.then_inc(dve_mean, 1)
            v.wait_ge(roots, 3)
            step(v.reciprocal(grs, grs))
            for t in range(NT):
                for g, (o, w) in enumerate(((0, 256), (256, 512), (768, 256))):
                    last = v.tensor_scalar(MERG[:, t, o:o + w], MERG[:, t, o:o + w],
                                           grs[:, 4 * g + t:4 * g + t + 1], None, ALU.mult)
                last.then_inc(xn_ready, 1)
            for j in range(C):
                v.wait_ge(turned, C + j + 1)
                v.tensor_scalar(MT[:, j, :], PS[:, j % 6, :], ggrc[:, j:j + 1], None, ALU.mult).then_inc(kept, 1)
            for t in range(NT):
                v.wait_ge(wout_done, t + 1)
                b0 = 2 * (t % 3)
                step(v.tensor_tensor(TMP[t % 2][:], PSF[:, b0 * 512:b0 * 512 + D], ROW["gt1"][:], ALU.mult))
                v.tensor_tensor(X[:, t, :], X[:, t, :], TMP[t % 2][:], ALU.add).then_inc(wout_kept, 1)
            v.wait_ge(bias_in, 64)
            step(v.tensor_scalar(BW[:, D:2 * D], BW[:, D:2 * D], 1.0, None, ALU.add))
            v.tensor_copy(BR[0:32, :], BW[0:32, :])
            step(v.tensor_copy(BHT[32:64, :], BW[32:64, :]))
            v.tensor_tensor(BR[32:64, :], BW[32:64, :], BHT[32:64, :].bitcast(F32), ALU.subtract).then_inc(bias_split, 1)
            v.wait_ge(g_ffn_in, 16)
            step(v.tensor_tensor(ROW["sc2"][:], ROW["sc2"][:], GFFN[:], ALU.mult))
            v.wait_ge(squares, 3)
            v.tensor_scalar(rs, ss, 1.0 / D, EPS, ALU.mult, ALU.add).then_inc(dve_mean, 1)
            v.wait_ge(roots, 4)
            step(v.reciprocal(rs, rs))
            for t in range(NT):
                step(v.scalar_tensor_tensor(out=XN2[:, t, :], in0=X[:, t, :], scalar=rs[:, t:t + 1],
                                            in1=ROW["sc2"][:], op0=ALU.mult, op1=ALU.mult))
                v.tensor_tensor(XN2[:, t, :], XN2[:, t, :], ROW["sh2"][:], ALU.add).then_inc(xn_ready, 1)
            for j in range(C):
                v.wait_ge(turned, 2 * C + j + 1)
                v.tensor_copy(H2T[:, j, :], PS[:, j % 6, :]).then_inc(kept, 1)
            v.wait_ge(logits_done, 1)
            step(v.tensor_tensor(L, PS[:, 6, 0:P].rearrange("p (t e) -> p t e", t=NT),
                                 BRT[:].unsqueeze(1).broadcast_to([P, NT, E]), ALU.add))
            for t in range(NT):
                last = v.max(M8[:, t, :], L[:, t, :])
            step(last)
            for t in range(NT):
                last = v.max_index(I8[:, t, :], M8[:, t, :], L[:, t, :])
            step(last)
            v.tensor_tensor(LM, M8, M8[:, :, 0:1].broadcast_to([P, NT, 8]), ALU.subtract).then_inc(max_ready, 1)
            step(v.tensor_copy(IF, I8))
            v.wait_ge(iotas, 1)
            step(v.tensor_tensor(OH, IF[:, :, 0:TOPK].unsqueeze(3).broadcast_to([P, NT, TOPK, E]),
                                 IOTAE.unsqueeze(1).unsqueeze(1).broadcast_to([P, NT, TOPK, E]), ALU.is_equal))
            step(v.tensor_tensor(MK2, OH[:, :, 0, :], OH[:, :, 1, :], ALU.add))
            step(v.tensor_tensor(MK3, OH[:, :, 2, :], OH[:, :, 3, :], ALU.add))
            v.tensor_tensor(MASK, MK2, MK3, ALU.add).then_inc(mask_ready, 1)
            v.wait_ge(probs_ready, SOFT_UNITS + 1)
            step(v.tensor_reduce(SUM4, EXPJ[:, :, 0:TOPK], AX, ALU.add))
            step(v.reciprocal(SUM4, SUM4))
            v.tensor_tensor(WJ[:], EXPJ, SUM4.unsqueeze(2).broadcast_to([P, NT, 8]), ALU.mult)
            v.wait_ge(ranks_done, 1)
            step(v.tensor_copy(CNT, PS[:, 7, P:P + E]))
            step(v.tensor_scalar(TL, CNT, 0.0, None, ALU.is_gt))
            for full in range(1, NT):
                step(v.scalar_tensor_tensor(out=TL, in0=CNT, scalar=float(full * P), in1=TL, op0=ALU.is_gt, op1=ALU.add))
            step(v.tensor_copy(TEND[0], TL))
            k, n = 0, 1
            while n < E:
                v.tensor_copy(TEND[1 - k][:, 0:n], TEND[k][:, 0:n])
                step(v.tensor_tensor(TEND[1 - k][:, n:E], TEND[k][:, n:E], TEND[k][:, 0:E - n], ALU.add))
                k, n = 1 - k, 2 * n
            tend = TEND[k]
            step(v.tensor_tensor(TSTART, tend, TL, ALU.subtract))
            step(v.scalar_tensor_tensor(out=SLOT, in0=TSTART.unsqueeze(1).broadcast_to([P, NT, E]), scalar=float(P),
                                        in1=PS[:, 7, 0:P].rearrange("p (t e) -> p t e", t=NT),
                                        op0=ALU.mult, op1=ALU.add))
            step(v.tensor_tensor(OH, OH, SLOT.unsqueeze(2).broadcast_to([P, NT, TOPK, E]), ALU.mult))
            step(v.tensor_reduce(SJ, OH, AX, ALU.add))
            step(v.tensor_tensor(TT, IOTA48.unsqueeze(2).broadcast_to([1, 48, E]), tend[0:1].unsqueeze(1).broadcast_to([1, 48, E]), ALU.is_ge))
            step(v.tensor_reduce(TE, TT, AX, ALU.add))
            v.tensor_scalar(TILE_E[:], TE, float(E - 1), None, ALU.min)
            v.tensor_scalar(LAST[0:1, 0:1], tend[0:1, E - 1:E], -1.0, None, ALU.add).then_inc(routed, 1)
            NC = NT * TOPK
            sjf = SJ.rearrange("p t j -> p (t j)")
            step(v.tensor_tensor(PAST[:], sjf.unsqueeze(2).broadcast_to([P, NC, 48]),
                                 TILEV[:].unsqueeze(1).broadcast_to([P, NC, 48]), ALU.is_ge))
            step(v.tensor_reduce(TA[:], PAST[:], AX, ALU.add))
            step(v.scalar_tensor_tensor(out=MA[:], in0=TA[:], scalar=float(-P), in1=sjf, op0=ALU.mult, op1=ALU.add))
            v.tensor_tensor(INT[:], TA[:].unsqueeze(2).broadcast_to([P, NC, 48]),
                            IOTA[:, 0:48].unsqueeze(1).broadcast_to([P, NC, 48]), ALU.is_equal)
            for n in range(NC):
                last = v.tensor_scalar(SLOTS[:, n, :], IOTA[:], MA[:, n:n + 1], None, ALU.is_equal)
            step(last)
            v.tensor_tensor(WHO[:, :, 0, :], INT[:], TOKV[:].unsqueeze(2).broadcast_to([P, NC, 48]), ALU.mult)
            v.tensor_tensor(WHO[:, :, 1, :], INT[:], ROWV[:].unsqueeze(2).broadcast_to([P, NC, 48]), ALU.mult
                            ).then_inc(slots_placed, 1)
            v.wait_ge(slots_ready, 1)
            v.tensor_copy(TOKF[:, 0, :], PS[:, 6, 0:48])
            step(v.tensor_scalar(EMPTY[:], PS[:, 6, 48:96], 0.0, float(2 * T * TOPK), ALU.is_equal, ALU.mult))
            v.scalar_tensor_tensor(out=TOKF[:, 1, :], in0=PS[:, 6, 48:96], scalar=-1.0, in1=EMPTY[:],
                                   op0=ALU.add, op1=ALU.add).then_inc(tables_ready, 1)

            last_tile = v.value_load(LAST[0:1, 0:1], min_val=15, max_val=MAX_TILES - 1)
            v.sem_inc(lo_done, 2)

            def lo(i, k):
                slot, b = (4 + k) % RING, (4 + k) % 3
                v.wait_ge(hi_done, i * CHUNKS + (4 + k + 1))
                v.tensor_tensor(WL[:, b, :], RINGB[:, slot, :], WH[:, b, :].bitcast(F32), ALU.subtract
                                ).then_inc(lo_done, 1)

            def clip(h, n, first_=False):
                v.wait_ge(gu_done, n)
                if not first_:
                    v.wait_ge(act_ready, n - 1)
                b = 2 + 2 * h
                v.tensor_scalar(GC[:], PS[:, b, :], LIMIT, None, ALU.min).then_inc(gate_ready, 1)
                v.tensor_scalar(UC[:], PS[:, b + 1, :], LIMIT + 1.0, 1.0 - LIMIT, ALU.min, ALU.max).then_inc(up_ready, 1)

            def keep_turned(h, n):
                v.wait_ge(ah_ready, n)
                v.tensor_tensor(AL[:, h].rearrange("p r m -> p (r m)"), PS[:, 2 + 2 * h, :],
                                AH[:, h].rearrange("p r m -> p (r m)").bitcast(F32), ALU.subtract).then_inc(al_ready, 1)

            def keep_gathered(n):
                v.wait_ge(xh_ready, n)
                v.tensor_tensor(XL[:].rearrange("p j m -> p (j m)"), PSF[:, 0:D],
                                XH[:].rearrange("p j m -> p (j m)").bitcast(F32), ALU.subtract).then_inc(xl_ready, 1)

            for k in range(-4, -1):
                lo(0, k)
            keep_gathered(1)
            for k in range(-1, 1):
                lo(0, k)
            clip(0, 1, True)
            for k in range(1, 3):
                lo(0, k)
            with v.Fori(0, last_tile) as i:
                lo(i, 3)
                lo(i, 4)
                lo(i, 5)
                keep_turned(0, i * 2 + 1)
                clip(1, i * 2 + 2)
                lo(i, 6)
                keep_gathered(i + 2)
                lo(i, 7)
                lo(i, 8)
                keep_turned(1, i * 2 + 2)
                lo(i, 9)
                lo(i, 10)
                lo(i, 11)
                clip(0, i * 2 + 3)
                lo(i, 12)
                lo(i, 13)
                lo(i, 14)
            i = last_tile
            lo(i, 3)
            lo(i, 4)
            lo(i, 5)
            keep_turned(0, i * 2 + 1)
            clip(1, i * 2 + 2)
            lo(i, 6)
            keep_turned(1, i * 2 + 2)
            lo(i, 7)
            v.wait_ge(misc_in, 64)
            for t in range(NT):
                v.wait_ge(rows_in[t], 16)
                step(v.tensor_scalar(AC2[:, t, :], GR[:, t, 0, :], WJ[:, t, 0:1], None, ALU.mult))
                for j in range(1, TOPK):
                    step(v.scalar_tensor_tensor(out=AC2[:, t, :], in0=GR[:, t, j, :], scalar=WJ[:, t, j:j + 1],
                                                in1=AC2[:, t, :], op0=ALU.mult, op1=ALU.add))
                step(v.tensor_tensor(AC2[:, t, :], AC2[:, t, :], ROW["gt2"][:], ALU.mult))
                v.tensor_tensor(AC2[:, t, :], AC2[:, t, :], X[:, t, :], ALU.add).then_inc(sum_ready, 1)
                v.wait_ge(squares, 4 + t)
                v.tensor_scalar(rs[:, t:t + 1], ss[:, t:t + 1], 1.0 / D, EPS, ALU.mult, ALU.add).then_inc(dve_mean, 1)
                v.wait_ge(roots, 5 + t)
                step(v.reciprocal(rs[:, t:t + 1], rs[:, t:t + 1]))
                v.scalar_tensor_tensor(out=AC2[:, t, :], in0=AC2[:, t, :], scalar=rs[:, t:t + 1], in1=GF[:],
                                       op0=ALU.mult, op1=ALU.mult).then_inc(final_ready, 1)

        @block.gpsimd
        def _(g):
            done = [0]

            def step(ins):
                done[0] += 1
                ins.then_inc(pool_step, 1)
                g.wait_ge(pool_step, done[0])

            for _, buf in SUMS:
                last = g.memset(buf[:], 0.0)
            last.then_inc(zeroed, 1)
            for m, val in ((ID, 0.0), (NTRI, -1.0), (NONE_, -1.0), (ONES, 1.0), (SLT, 1.0)):
                last = g.memset(m[:], val)
            step(last)
            g.affine_select(out=ID[:], in_=ID[:], compare_op=ALU.not_equal, fill=1.0, base=0,
                            pattern=[[-1, P]], channel_multiplier=1)
            g.affine_select(out=NTRI[:], in_=NTRI[:], compare_op=ALU.is_ge, fill=0.0, base=0,
                            pattern=[[-1, P]], channel_multiplier=1)
            g.affine_select(out=SLT[:], in_=SLT[:], compare_op=ALU.is_gt, fill=0.0, base=0,
                            pattern=[[1, P]], channel_multiplier=-1).then_inc(consts, 1)

            def keep_past(buf):
                ap = bass.AP(buf[:].tensor, 0, [[2048, P], [T + P, NT], [1, P]])
                return g.affine_select(out=ap, in_=ap, compare_op=ALU.is_gt, fill=0.0, base=0,
                                       pattern=[[0, NT], [1, P]], channel_multiplier=-1)

            def first(u):
                if UNITS[u][0] == "sb":
                    g.wait_ge(drop_ready, nth(u, "sb"))
                    keep_past(UB2[u % 2]).then_inc(drop_masked, 1)

            def second(u):
                if UNITS[u][0] == "sb":
                    g.wait_ge(stick_ready, nth(u, "sb"))
                    keep_past(UB1[u % 2]).then_inc(stick_masked, 1)

            first(0)
            for u in range(len(UNITS)):
                if u + 1 < len(UNITS):
                    first(u + 1)
                second(u)
            g.wait_ge(set_free, len(UNITS))
            g.wait_ge(mod_used, 12)
            g.iota(IOTAE, pattern=[[1, E]], base=0, channel_multiplier=0, allow_small_or_imprecise_dtypes=True)
            g.iota(IOTA48, pattern=[[1, 48]], base=0, channel_multiplier=0, allow_small_or_imprecise_dtypes=True)
            g.iota(IOTA[:], pattern=[[1, P]], base=0, channel_multiplier=0, allow_small_or_imprecise_dtypes=True)
            step(g.memset(ID2[:], 0.0))
            for half in range(2):
                step(g.affine_select(out=ID2[:], in_=ID2[:], compare_op=ALU.not_equal, fill=1.0, base=-32 * half,
                                     pattern=[[-1, E]], channel_multiplier=1))
            g.iota(TOKV[:], pattern=[[P, NT], [0, TOPK]], base=0, channel_multiplier=1,
                   allow_small_or_imprecise_dtypes=True)
            g.iota(ROWV[:], pattern=[[P * TOPK, NT], [1, TOPK]], base=1, channel_multiplier=TOPK,
                   allow_small_or_imprecise_dtypes=True)
            g.iota(TILEV[:], pattern=[[P, 48]], base=P, channel_multiplier=0,
                   allow_small_or_imprecise_dtypes=True).then_inc(iotas, 1)
            g.wait_ge(routed, 1)
            last_tile = g.value_load(LAST[0:1, 0:1], min_val=15, max_val=MAX_TILES - 1)

            def gather(i, n):
                if n is not None:
                    g.tensor_copy(TOKC[:, 0:1], TOKF[:, 0, bass.ds(i, 1)]).then_inc(idx_step, 1)
                    g.wait_ge(h2_out, 16 * NT)
                    g.wait_ge(idx_step, n)
                g.indirect_dma_start(XG[:], None, h2_dram,
                                     bass.IndirectOffsetOnAxis(ap=TOKC[:, 0:1], axis=0),
                                     bounds_check=T - 1, oob_is_err=False).then_inc(gathered, 16)

            def scatter(i):
                g.wait_ge(y_kept, i + 2)
                g.tensor_copy(ROWC[:, 0:1], TOKF[:, 1, bass.ds(i, 1)]).then_inc(row_step, 1)
                g.wait_ge(h2_out, 16 * NT)
                g.wait_ge(row_step, i + 2)
                g.indirect_dma_start(ys, bass.IndirectOffsetOnAxis(ap=ROWC[:, 0:1], axis=0), Y[:], None,
                                     bounds_check=T * TOPK - 1, oob_is_err=False).then_inc(y_stored, 16)

            def selector(e):
                g.tensor_copy(SEL[:], ID2[:, bass.ds(e, 1)].broadcast_to([64, P])).then_inc(sel_ready, 1)

            def gated(h, n):
                g.wait_ge(up_ready, n)
                g.wait_ge(gate_ready, n)
                g.tensor_tensor(UC[:], UC[:], GC[:], ALU.mult).then_inc(gated_up, 1)
                g.wait_ge(gated_up, n)
                g.wait_ge(sig_ready, n)
                g.tensor_tensor(AC[:, h], UC[:], SG[:], ALU.mult).then_inc(act_ready, 1)

            e = g.value_load(TILE_E[0:1, 0:1], min_val=0, max_val=E - 1)
            selector(e)
            g.wait_ge(tables_ready, 1)
            g.sem_inc(row_step, 1)
            step(g.tensor_copy(TOKC[:, 0:1], TOKF[:, 0, 0:1]))
            g.wait_ge(h2_out, 16 * NT)
            gather(0, None)
            g.wait_ge(rows_turned, 1)
            gather(1, 1)
            gated(0, 1)
            with g.Fori(0, last_tile) as i:
                e = g.value_load(TILE_E[0:1, bass.ds(i + 1, 1)], min_val=0, max_val=E - 1)
                g.wait_ge(sel_used, i + 1)
                selector(e)
                g.wait_ge(rows_turned, i + 2)
                gather(i + 2, i + 2)
                gated(1, i * 2 + 2)
                gated(0, i * 2 + 3)
                scatter(i)
                g.wait_ge(y_stored, i * 16 + 16)
                g.sem_inc(y_free, 1)
            i = last_tile
            gated(1, i * 2 + 2)
            scatter(i)
            g.wait_ge(gathered, last_tile * 16 + 32)
    return nc


_INS = ["x", "c", "w_in", "w_out", "g_norm_mix", "g_norm_ffn", "g_group", "w_mod", "b_mod", "swa_sinks", "rel_bias",
        "w_router", "b_router", "w_gate_up", "b_gate_up", "w_down", "b_down", "g_final"]


def kernel(**inputs):
    import concourse.bacc as bacc
    from concourse.bass_utils import run_bass_kernel_spmd

    onehot, masks = dist_tables()
    nc = bacc.Bacc("TRN2", target_bir_lowering=False, num_devices=1)
    arrays, args = {}, []
    given = {n: inputs[n] for n in _INS}
    given["onehot"], given["masks"] = onehot, masks
    for name, a in given.items():
        a = np.ascontiguousarray(a)
        arrays[f"in_{name}"] = a
        args.append(nc.dram_tensor(f"in_{name}", a.shape, mybir.dt.from_np(a.dtype), kind="ExternalInput").ap())
    out = nc.dram_tensor("out_dram", (1, T, D), F32, kind="ExternalOutput").ap()
    build(nc, *args, out)
    r = run_bass_kernel_spmd(nc, [arrays], core_ids=[0])
    return r.results[0]["out_dram"]
```

```python
from contextlib import ExitStack

import numpy as np

import concourse.bass as bass
from concourse import mybir

F32 = mybir.dt.float32
F32R = mybir.dt.float32r
I32 = mybir.dt.int32
U32 = mybir.dt.uint32
ALU = mybir.AluOpType
ACT = mybir.ActivationFunctionType
AX = mybir.AxisListType.X

P = 128
D = 1024
T = 512
NT = T // P
C = D // P
HD = 64
E = 32
TOPK = 4
BUCKETS = 32
EPS = 1e-6
NEG = -1e30
LIMIT = 7.0
ALPHA = 1.702
MAX_TILES = T * TOPK // P + E - 1
BAND = 384

SB_Q, SB_K, SB_V, SW_Q, SW_K, SW_V, MB_Q, MB_K, MB_V, IN_W = 0, 256, 512, 768, 1280, 1408, 1536, 1792, 2048, 2304

Q_COLS = [SB_Q, SB_Q + P, SB_K, SB_K + P, *range(SW_Q, SW_K, P), SW_K, MB_Q, MB_Q + P, MB_K, MB_K + P]
UNITS = [("sb", 0), ("sb", 1), ("sw", 0), ("sw", 1), ("sb", 2), ("sw", 2), ("sb", 3), ("sw", 3),
         ("mb", 0), ("sw", 4), ("mb", 1), ("sw", 5), ("mb", 2), ("sw", 6), ("mb", 3), ("sw", 7)]
V_SB = [("v", (SB_V, 256, 0, t, 2)) for t in (0, 2)]
V_SW = ("v", (SW_V, 128, 256, 0, 4))
V_MB = [("v", (MB_V, 256, 384, t, 2)) for t in (0, 2)]
FIRST_JOBS = [*V_SB, ("qk", 0), ("qk", 2)]
UNIT_JOBS = [[("qk", 8), ("qk", 4)], [V_SW, ("qk", 1)], [("qk", 3)], [("qk", 5)], [V_MB[0], ("qk", 9)], [("qk", 11)],
             [("qk", 6)], [V_MB[1]], [("qk", 10)], [("qk", 12)], [("qk", 7)], [], [], [], [], []]
JOBS = FIRST_JOBS + [job for jobs in UNIT_JOBS for job in jobs]
PIECE = 768
SOFT_UNITS = sum(kind != "sb" for kind, _ in UNITS)
ROWS = [("gt1", 2), ("sc2", 4), ("sh2", 3), ("gt2", 5)]
RING = 6
CHUNKS = 12


def dist_tables():
    d = 255 - np.arange(BAND)
    n = np.maximum(d, 0)
    exact = BUCKETS // 2
    nf = np.maximum(n, 1).astype(np.float32)
    large = exact + (np.log(nf / np.float32(exact)) / np.float32(np.log(128 / exact))
                     * np.float32(BUCKETS - exact)).astype(np.int32)
    bucket = np.where(n < exact, n, np.minimum(large, BUCKETS - 1))
    onehot = (bucket[None, :] == np.arange(BUCKETS)[:, None]).astype(np.float32)
    masks = np.zeros((12, BAND), np.float32)
    masks[:, d < 0] = NEG
    masks[:8, d >= 128] = NEG
    return onehot, masks


def build(nc, x, c, w_in, w_out, g_mix, g_ffn, g_group, w_mod, b_mod, sinks, table, w_router, b_router,
          w_gate_up, b_gate_up, w_down, b_down, g_final, onehot, masks, out):
    band_dram = nc.dram_tensor("band_dram", (12, P, BAND), F32, kind="Internal").ap()
    h2_dram = nc.dram_tensor("h2_dram", (T, D), F32, kind="Internal").ap()
    ys = nc.dram_tensor("ys", (T * TOPK, D), F32, kind="Internal").ap()

    ctx = ExitStack()
    with ctx:
        BASE = 16896

        def at(name, kb, shape, dt=F32):
            return nc.alloc_sbuf_tensor_at(name, shape, dt, offset=BASE + int(kb * 1024))

        def sem(name):
            return ctx.enter_context(nc.semaphore(name))

        PS = ctx.enter_context(nc.psum_tensor("PS", [P, 8, 512], F32))
        PSF = PS[:].rearrange("p b n -> p (b n)")

        X = at("X", 0, [P, NT, D])
        RINGB = at("RINGB", 16, [P, RING, 2048])
        WIN = [at(f"WIN{s}", 16 + 24 * s, [P, C, PIECE]) for s in range(3)]
        MB2 = at("MB2", 16, [P, 2, C, 256])
        WOUT = at("WOUT", 32, [P, C, D])
        MT = at("MT", 0, [P, C, T])
        SQ = at("SQ", 64, [P, C, T])
        RSG = at("RSG", 80, [P, 3, T])
        XB = at("XB", 128, [P, NT, D])
        UB1 = [at("UA1", 96, [P, 2048]), at("UB1", 104, [P, 2048])]
        UB2 = [at("UA2", 112, [P, 2048]), at("UB2", 120, [P, 2048])]
        ROW = {"sc2": at("SC2", 88, [P, D]), "sh2": at("SH2", 92, [P, D]),
               "gt1": at("GT1", 196, [P, D]), "gt2": at("GT2", 200, [P, D])}
        MB = at("MB", 96, [P, 2, C, 512])
        QKT = at("QKT", 128, [P, 13, T])
        KSW = at("KSW", 192, [P, T])
        V = at("V", 154, [P, NT, 640])
        HT = at("HT", 164, [P, C, T])
        XN = at("XN", 180, [P, NT, D])
        BT = at("BT", 180, [P, 12, 256])
        COL = [at("COL_SC", 164, [P, D]), at("COL_SH", 168, [P, D])]
        XN2 = at("XN2", 64, [P, NT, D])
        H2T = at("H2T", 96, [P, C, T])
        BW = at("BW", 164, [64, 3 * D])
        BHT = at("BHT", 176, [64, 3 * D], F32R)
        BR = at("BR", 144, [64, 3 * D], F32R)
        WH = at("WH", 64, [P, 3, 2048], F32R)
        WL = at("WL", 88, [P, 3, 2048], F32R)
        XG = at("XG", 176, [P, D])
        XH = at("XH", 156, [P, C, P], F32R)
        XL = at("XL", 160, [P, C, P], F32R)
        AH = at("AH", 164, [P, 2, 4, P], F32R)
        AL = at("AL", 168, [P, 2, 4, P], F32R)
        Y = at("Y", 172, [P, D])
        GC = at("GC", 180, [P, 512])
        UC = at("UC", 182, [P, 512])
        SG = at("SG", 184, [P, 512])
        AC = at("AC", 186, [P, 2, 512])
        TOKF = at("TOKF", 190, [P, 2, 48])
        TOKC = at("TOKC", 190.5, [P, 2], I32)
        ROWC = at("ROWC", 190.53125, [P, 2], I32)
        SEL = at("SEL", 192, [64, P], F32R)
        TOKV = at("TOKV", 192.5, [P, NT * TOPK])
        ROWV = at("ROWV", 192.5625, [P, NT * TOPK])
        TILEV = at("TILEV", 192.625, [P, 48])
        IOTA = at("IOTA", 193, [P, P])
        ID2 = at("ID2", 193.5, [64, E])
        WJ = at("WJ", 193.75, [P, NT, 8])
        TILE_E = at("TILE_E", 194.0625, [1, 48], I32)
        LAST = at("LAST", 194.25, [1, 8], I32)
        WR = at("WR", 194.5, [P, C, E])
        BRT = at("BRT", 195.5, [P, E])
        ID = at("ID", 204, [P, P])
        NTRI = at("NTRI", 204.5, [P, P])
        NONE_ = at("NONE", 205, [P, P])
        ONES = at("ONES", 205.5, [P, P])
        SLT = at("SLT", 206, [P, P])
        SMALL = at("SMALL", 206.5, [P, 216])
        BANDH = at("BANDH", 172, [BUCKETS, BAND])
        BANDM = at("BANDM", 173.5, [12, BAND])
        BANDS = at("BANDS", 175, [12, BAND])
        GFFN = at("GFFN", 112, [P, D])
        TMP = [at("TMP0", 116, [P, D]), at("TMP1", 120, [P, D])]
        RT = at("RT", 156, [P, 32, P])

        def rt(a, b=0, t=NT):
            return RT[:, a, 0:b or P].rearrange("p (t e) -> p t e", t=t)

        L, M8, IF, LM, EXPJ = rt(0), rt(1, 32), rt(3, 32), rt(4, 32), rt(5, 32)
        I8 = RT[:, 2, 0:32].bitcast(U32).rearrange("p (t e) -> p t e", t=NT)
        OH = RT[:, 6:10, :].rearrange("p b (j e) -> p b j e", e=E)
        MK2, MK3, SLOT = rt(10), rt(11), rt(12)
        MASK = at("MASK", 164, [P, NT, E], F32R)
        SLTR = at("SLTR", 170.5, [P, P], F32R)
        ONESR = at("ONESR", 171, [P, P], F32R)
        SUM4 = RT[:, 13, 0:NT]
        CNT, TL, TSTART = RT[:, 13, 32:64], RT[:, 13, 64:96], RT[:, 13, 96:128]
        TEND = [RT[:, 14, 0:32], RT[:, 14, 32:64]]
        SJ = RT[:, 14, 64:80].rearrange("p (t j) -> p t j", t=NT)
        TE = RT[0:1, 14, 80:128]
        IOTAE = RT[:, 15, 0:E]
        IOTA48 = RT[0:1, 15, 64:112]
        TT = RT[0:1, 17:29, :].rearrange("p b n -> p (b n)").rearrange("p (i e) -> p i e", e=E)
        GR = at("GR", 16, [P, NT, TOPK, D])
        PAST = at("PAST", 0, [P, NT * TOPK, 48])
        INT = at("INT", 3, [P, NT * TOPK, 48])
        WHO = at("WHO", 6, [P, NT * TOPK, 2, 48], F32R)
        SLOTS = at("SLOTS", 112, [P, NT * TOPK, P], F32R)
        TA = at("TA", 12, [P, NT * TOPK])
        MA = at("MA", 12.0625, [P, NT * TOPK])
        EMPTY = at("EMPTY", 12.125, [P, 48])
        AC2 = at("AC2", 96, [P, NT, D])
        GF = at("GF", 112, [P, D])
        FJ = at("FJ", 144, [P, NT, D])

        _o = [0]

        def small(n):
            _o[0] += n
            return SMALL[:, _o[0] - n:_o[0]]

        cT, cS, gmixc, ggrc = (small(C) for _ in range(4))
        G1, SH1 = small(C), small(C)
        ss, rs = small(4), small(4)
        sinkb = small(8)
        farb = small(4)
        mx = [small(4), small(4)]
        negm = [small(4), small(4)]
        den = [small(4), small(4)]
        esink = [small(4), small(4)]
        rden = [small(4), small(4)]
        sg = small(C)
        BANDT = small(12)[0:BUCKETS]

        consts = sem("consts")
        x_in, c_in, band_in = sem("x_in"), sem("c_in"), sem("band_in")
        win_in = [sem(f"win_in{s}") for s in range(3)]
        swap_in = sem("swap_in")
        wout_in, wr_in, bias_in, misc_in = sem("wout_in"), sem("wr_in"), sem("bias_in"), sem("misc_in")
        mod_in, row_in = [sem("mod_in0"), sem("mod_in1")], [sem("row_in0"), sem("row_in1")]
        ones_kept = sem("ones_kept")
        x_back, group_sq, group_sums = sem("x_back"), sem("group_sq"), sem("group_sums")
        group_mean, group_roots, probs_scaled = sem("group_mean"), sem("group_roots"), sem("probs_scaled")
        act_step, dve_step, pool_step = sem("act_step"), sem("dve_step"), sem("pool_step")
        mod_used, rows_kept = sem("mod_used"), sem("rows_kept")
        dve_mean, slots_ready, g_ffn_in, iotas, sum_ready = (sem("dve_mean"), sem("slots_ready"), sem("g_ffn_in"),
                                                          sem("iotas"), sem("sum_ready"))
        c_silu, zeroed, mod_bias = sem("c_silu"), sem("zeroed"), sem("mod_bias")
        summed, totals = sem("summed"), sem("totals")
        squares, roots, xn_ready = sem("squares"), sem("roots"), sem("xn_ready")
        turned, kept = sem("turned"), sem("kept")
        proj_done, q_kept, v_kept = sem("proj_done"), sem("q_kept"), sem("v_kept")
        band_done, band_kept, band_out = sem("band_done"), sem("band_kept"), sem("band_out")
        scores_done, set_free, pv_done = sem("scores_done"), sem("set_free"), sem("pv_done")
        logs_ready, drop_ready, drop_masked = sem("logs_ready"), sem("drop_ready"), sem("drop_masked")
        sums_done, stick_ready, stick_masked = sem("sums_done"), sem("stick_ready"), sem("stick_masked")
        max_ready, probs_ready, probs_turned, pt_kept = (sem("max_ready"), sem("probs_ready"), sem("probs_turned"),
                                                         sem("pt_kept"))
        wout_done, wout_kept = sem("wout_done"), sem("wout_kept")
        logits_done, mask_ready, ranks_done = sem("logits_done"), sem("mask_ready"), sem("ranks_done")
        routed, h2_out, bias_split = sem("routed"), sem("h2_out"), sem("bias_split")
        slots_placed, tables_ready, idx_step = sem("slots_placed"), sem("tables_ready"), sem("idx_step")
        row_step = sem("row_step")
        ring_in = [sem(f"ring_in{s}") for s in range(RING)]
        hi_done, lo_done, pe_chunk = sem("hi_done"), sem("lo_done"), sem("pe_chunk")
        gu_done, act_turned, gathered, sel_used = sem("gu_done"), sem("act_turned"), sem("gathered"), sem("sel_used")
        rows_turned = sem("rows_turned")
        gate_ready, up_ready, sig_ready, act_ready = (sem("gate_ready"), sem("up_ready"), sem("sig_ready"),
                                                      sem("act_ready"))
        ah_ready, al_ready, xh_ready, xl_ready = sem("ah_ready"), sem("al_ready"), sem("xh_ready"), sem("xl_ready")
        y_kept, y_free, y_stored = sem("y_kept"), sem("y_free"), sem("y_stored")
        gated_up, sel_ready = sem("gated_up"), sem("sel_ready")
        rows_in = [sem(f"rows_in{t}") for t in range(NT)]
        gated_sum = sem("gated_sum")
        first_ready, final_ready, stored = sem("first_ready"), sem("final_ready"), sem("stored")

        block = ctx.enter_context(nc.Block())

        x_v = x[0].rearrange("(t p) d -> p t d", p=P)
        out_v = out[0].rearrange("(t p) d -> p t d", p=P)
        wmod_v = w_mod[0].rearrange("(p k) (v h n) -> v h p k n", p=P, v=6, h=2)
        wquarter_v = w_mod[0].rearrange("(p k) (v q n) -> v q p k n", p=P, v=6, q=4)
        bmod_v = b_mod[0].rearrange("(v a n) -> v a n", v=6, a=1)
        gu_v = w_gate_up.rearrange("l e (p k) (g h n) -> (l e) h p (k g) n", p=P, g=2, h=2)
        down_v = w_down.rearrange("l e (h p q r) n -> (l e) h q p (r n)", h=2, p=P, q=2)

        def col8(v):
            return v.rearrange("(p k) -> p k", k=C)

        def rep(v, n):
            return v.rearrange("(a n) -> a n", a=1).broadcast_to([P, n])

        SUMS = [(1, COL[0]), (0, COL[1])] + [(v, ROW[name]) for name, v in ROWS]

        def nth(u, *kinds):
            return sum(k in kinds for k, _ in UNITS[:u + 1])

        GROUPS = [((0, 1), 256), ((6, 7), 256), ((2, 3, 4, 5), 512)]
        SQUARED = {12: (0, 1), 13: (2, 3), 14: (4, 6), 15: (7,)}
        SQUARES = [ch for chs in SQUARED.values() for ch in chs] + [5]

        def kept_by(job):
            return sum(k == job[0] for k, _ in JOBS[:JOBS.index(job) + 1])

        BANKS = 3 * 512
        SB_AT, SW_AT, MB_AT = (0, 512, 1024, 896), (1024, 0, 256, 512), (896, 1024, 512, 0)

        def stick(u, t, c=None):
            o = BANKS * (u % 2) + SB_AT[t]
            return PSF[:, o + ((c or t) - t) * P:o + T - t * P]

        def queries(kind, kt):
            return range(kt, min(kt + 2, NT) if kind == "sw" else NT)

        def turned_at(kind, kt):
            return sum(len(queries(kind, j)) for j in range(kt)) * P

        def chunk_of(kind, h):
            return {"sb": 0, "sw": 2, "mb": 6}[kind] + h // 2

        @block.sync
        def _(sp):
            sp.dma_start(cT, col8(c[0])).then_inc(c_in, 16)
            sp.dma_start(gmixc, col8(g_mix[0])).then_inc(c_in, 16)
            sp.dma_start(X[:], x_v).then_inc(x_in, 16)
            sp.wait_ge(zeroed, 1)
            for v, buf in SUMS:
                sp.dma_start(buf[0:1, :], bmod_v[v]).then_inc(mod_bias, 16)

            def mod_chunk(n):
                b = n % 2
                if n >= 2:
                    sp.wait_ge(mod_used, n - 1)
                sp.dma_start(MB[:, b], wmod_v[SUMS[n // 2][0], n % 2]).then_inc(mod_in[b], 16)

            for n in range(4):
                mod_chunk(n)
            for part in range(3):
                sp.dma_start(WIN[part][:], w_in[0].rearrange("(p k) n -> p k n", p=P)[:, :, part * PIECE:(part + 1) * PIECE]
                             ).then_inc(win_in[part], 16)
            sp.dma_start(ggrc, g_group[0].rearrange("(k p) -> p k", p=P), allow_slow_non_contiguous=True).then_inc(misc_in, 16)
            sp.dma_start(sinkb, sinks[0:1, :].broadcast_to([P, 8])).then_inc(misc_in, 16)
            sp.dma_start(farb, table[31:32, 8:12].broadcast_to([P, 4])).then_inc(misc_in, 16)
            sp.wait_ge(band_out, 16)
            sp.wait_ge(turned, C)
            sp.dma_start(BT[:], bass.AP(band_dram.tensor, P - 1, [[BAND - 1, P], [P * BAND, 12], [1, 256]])).then_inc(band_in, 16)
            sp.wait_ge(q_kept, kept_by(("qk", 8)))
            for p0 in (0, 64):
                sp.dma_start(KSW[p0:p0 + 64, :], QKT[64 - p0:128 - p0, 8, :]).then_inc(swap_in, 16)
            sp.wait_ge(proj_done, JOBS.index(("qk", 3)) + 1)
            for n in range(16):
                if n >= 2:
                    sp.wait_ge(mod_used, 4 + n - 1)
                sp.dma_start(MB2[:, n % 2], wquarter_v[SUMS[2 + n // 4][0], n % 4]).then_inc(row_in[n % 2], 16)
            sp.wait_ge(proj_done, len(JOBS))
            sp.dma_start(WOUT[:], w_out[0].rearrange("(k p) n -> p k n", p=P)).then_inc(wout_in, 16)
            sp.dma_start(WR[:], w_router[0].rearrange("(p k) e -> p k e", p=P)).then_inc(wr_in, 16)
            sp.dma_start(BRT[:], b_router[0:1, :].broadcast_to([P, E])).then_inc(wr_in, 16)
            sp.wait_ge(set_free, len(UNITS))
            sp.dma_start(GFFN[:], rep(g_ffn[0], D)).then_inc(g_ffn_in, 16)
            for k in range(2):
                sp.dma_start(BW[32 * k:32 * k + 32, 0:2 * D], b_gate_up[0]).then_inc(bias_in, 16)
                sp.dma_start(BW[32 * k:32 * k + 32, 2 * D:3 * D], b_down[0]).then_inc(bias_in, 16)

            def load(e, i, k, src):
                if not (isinstance(i, int) and 4 + CHUNKS * i + k < RING):
                    sp.wait_ge(lo_done, i * CHUNKS + (k + 1))
                slot = (4 + k) % RING
                kind, h, q = src
                if kind == "gu":
                    sp.dma_start(RINGB[:, slot, :].rearrange("p (k n) -> p k n", n=512),
                                 gu_v[bass.ds(e, 1), h, :, 4 * q:4 * q + 4, :].rearrange("a p k n -> (a p) k n")
                                 ).then_inc(ring_in[slot], 16)
                else:
                    sp.dma_start(RINGB[:, slot, :],
                                 down_v[bass.ds(e, 1), h, q].rearrange("a p n -> (a p) n")).then_inc(ring_in[slot], 16)

            sp.dma_start(XB[:], x_v).then_inc(x_back, 16)
            for t in range(NT):
                if t == NT - 1:
                    sp.wait_ge(wout_done, NT)
                    for q in range(4):
                        load(0, 0, q - 4, ("gu", 0, q))
                    for q in range(2):
                        load(0, 0, q, ("gu", 1, q))
                sp.wait_ge(xn_ready, NT + t + 1)
                sp.dma_start(h2_dram[t * P:(t + 1) * P, :], XN2[:, t, :]).then_inc(h2_out, 16)
            sp.wait_ge(routed, 1)
            last_tile = sp.value_load(LAST[0:1, 0:1], min_val=15, max_val=MAX_TILES - 1)
            with sp.Fori(0, last_tile) as i:
                e = sp.value_load(TILE_E[0:1, bass.ds(i, 1)], min_val=0, max_val=E - 1)
                en = sp.value_load(TILE_E[0:1, bass.ds(i + 1, 1)], min_val=0, max_val=E - 1)
                for q in range(2, 4):
                    load(e, i, q, ("gu", 1, q))
                for q in range(2):
                    load(e, i, 4 + q, ("dn", 0, q))
                for q in range(4):
                    load(en, i, 6 + q, ("gu", 0, q))
                for q in range(2):
                    load(e, i, 10 + q, ("dn", 1, q))
                for q in range(2):
                    load(en, i, 12 + q, ("gu", 1, q))
            i = last_tile
            e = sp.value_load(TILE_E[0:1, bass.ds(i, 1)], min_val=0, max_val=E - 1)
            for q in range(2, 4):
                load(e, i, q, ("gu", 1, q))
            for q in range(2):
                load(e, i, 4 + q, ("dn", 0, q))
            for q in range(2):
                load(e, i, 6 + q, ("dn", 1, q))
            sp.wait_ge(pe_chunk, last_tile * CHUNKS + CHUNKS)
            sp.dma_start(GF[:], rep(g_final, D)).then_inc(misc_in, 16)
            sp.wait_ge(y_stored, last_tile * 16 + 16)
            for t in range(NT):
                sp.dma_start(GR[:, t], ys[t * P * TOPK:(t + 1) * P * TOPK, :].rearrange("(p j) d -> p j d", j=TOPK)
                             ).then_inc(rows_in[t], 16)
            for t in range(NT):
                sp.wait_ge(final_ready, t + 1)
                sp.dma_start(out_v[:, t, :], AC2[:, t, :]).then_inc(stored, 16)
            sp.wait_ge(stored, 16 * NT)

        @block.tensor
        def _(pe):
            pe.wait_ge(consts, 1)
            pe.wait_ge(band_in, 48)
            pe.matmul(PS[0:12, 6, 0:BAND], BANDT, BANDH[:], start=True, stop=True).then_inc(band_done, 1)
            def turn(src, j, bank):
                for t in range(NT):
                    last = pe.transpose(PS[:, bank, t * P:(t + 1) * P], src[:, t, j:D:C], ID[:])
                last.then_inc(turned, 1)

            pe.wait_ge(xn_ready, NT)
            for j in range(6):
                turn(XN, j, j)
            for v in range(2):
                pe.wait_ge(summed, v + 1)
                for j in range(C):
                    mm = pe.matmul(PS[:, 7, C * v + j:C * v + j + 1], COL[v][:, j:D:C], ONES[:, 0:1],
                                   start=True, stop=True)
            mm.then_inc(totals, 1)
            for j in range(6, C):
                pe.wait_ge(kept, j - 5)
                turn(XN, j, j % 6)
            pe.wait_ge(kept, C)

            def project(job):
                n = JOBS.index(job)
                kind, what = job
                if n >= 2:
                    before = JOBS[n - 2]
                    pe.wait_ge(q_kept if before[0] == "qk" else v_kept, kept_by(before))
                col = Q_COLS[what] if kind == "qk" else what[0]
                w = WIN[col // PIECE]
                col %= PIECE
                pe.wait_ge(win_in[WIN.index(w)], 16)
                if kind == "qk":
                    for k in range(C):
                        mm = pe.matmul(PS[:, 6 + n % 2, :], w[:, k, col:col + P], HT[:, k, :],
                                       start=(k == 0), stop=(k == C - 1))
                else:
                    _, width, _, t0, tiles = what
                    for t in range(tiles):
                        for k in range(C):
                            mm = pe.matmul(PS[:, 6 + n % 2, t * width:(t + 1) * width],
                                           HT[:, k, (t0 + t) * P:(t0 + t + 1) * P], w[:, k, col:col + width],
                                           start=(k == 0), stop=(k == C - 1))
                mm.then_inc(proj_done, 1)

            for job in FIRST_JOBS:
                project(job)

            def row_total(r):
                pe.wait_ge(summed, r + 3)
                if r >= 1:
                    pe.wait_ge(rows_kept, r)
                for h in range(2):
                    mm = pe.matmul(PS[:, 6 + h, :], ONES[:], ROW[ROWS[r][0]][:, h * 512:(h + 1) * 512],
                                   start=True, stop=True)
                mm.then_inc(totals, 1)

            def q_k(kind, h):
                p0 = 64 * (h % 2)
                if kind == "sb":
                    return QKT[p0:p0 + 64, h // 2, :], QKT[p0:p0 + 64, 2 + h // 2, :]
                if kind == "mb":
                    return QKT[p0:p0 + 64, 9 + h // 2, :], QKT[p0:p0 + 64, 11 + h // 2, :]
                k = QKT[p0:p0 + 64, 8, :] if h // 4 == h % 2 else KSW[p0:p0 + 64, :]
                if h // 4 != h % 2:
                    pe.wait_ge(swap_in, 32)
                return QKT[p0:p0 + 64, 4 + h // 2, :], k

            def scores(u):
                kind, h = UNITS[u]
                q, k = q_k(kind, h)
                blocks = {"sb": (h // 2, 2 + h // 2), "sw": (4 + h // 2, 8), "mb": (9 + h // 2, 11 + h // 2)}[kind]
                pe.wait_ge(q_kept, max(kept_by(("qk", blk)) for blk in blocks))
                if u >= 2:
                    pe.wait_ge(set_free, u - 1)
                for t in range(NT):
                    if kind == "sb":
                        mm = pe.matmul(stick(u, t), k[:, t * P:(t + 1) * P], q[:, t * P:T], start=(t != 3), stop=True,
                                       skip_group_check=True)
                    else:
                        lo = max(t - 1, 0) * P if kind == "sw" else 0
                        o = BANKS * (u % 2) + (SW_AT if kind == "sw" else MB_AT)[t]
                        mm = pe.matmul(PSF[:, o:o + (t + 1) * P - lo], q[:, t * P:(t + 1) * P], k[:, lo:(t + 1) * P],
                                       start=True, stop=True)
                mm.then_inc(scores_done, 1)

            def middle(u):
                kind, h = UNITS[u]
                if kind == "sb":
                    pe.wait_ge(drop_masked, nth(u, "sb"))
                    drop = UB2[u % 2][:].rearrange("p (t n) -> p t n", t=NT)
                    for kt in range(NT):
                        for jt in range(kt, NT):
                            mm = pe.matmul(stick(u, kt, jt), (NTRI if jt == kt else NONE_)[:],
                                           drop[:, jt, jt * P:T], start=False, stop=(jt == NT - 1),
                                           skip_group_check=True)
                    mm.then_inc(sums_done, 1)
                else:
                    pe.wait_ge(probs_scaled, nth(u, "sw", "mb"))
                    wide = 256 if kind == "sw" else T
                    probs = UB1[u % 2][:, 0:NT * wide].rearrange("p (t n) -> p t n", t=NT)
                    n = BANKS * (u % 2)
                    for kt in range(NT):
                        for qt in queries(kind, kt):
                            o = (kt - qt + 1) * P if kind == "sw" else kt * P
                            mm = pe.transpose(PSF[:, n:n + P], probs[:, qt, o:o + P], ID[:])
                            n += P
                    mm.then_inc(probs_turned, 1)

            def values(u):
                kind, h = UNITS[u]
                vo = {"sb": h * HD, "sw": 256 + (h // 4) * HD, "mb": 384 + h * HD}[kind]
                pe.wait_ge(v_kept, {"sb": kept_by(V_SB[1]), "sw": kept_by(V_SW), "mb": kept_by(V_MB[1])}[kind])
                if kind == "sb":
                    pe.wait_ge(stick_masked, nth(u, "sb"))
                else:
                    pe.wait_ge(pt_kept, nth(u, "sw", "mb"))
                p0, bank = 64 * (h % 2), 3 * (u % 2)
                for kt in range(NT):
                    n = len(queries(kind, kt)) * P
                    o = kt * T + kt * P if kind == "sb" else turned_at(kind, kt)
                    src = (UB1 if kind == "sb" else UB2)[u % 2][:, o:o + n]
                    mm = pe.matmul(PS[p0:p0 + 64, bank, kt * P:kt * P + n], V[:, kt, vo:vo + HD], src,
                                   start=(kt == 0), stop=(kt == NT - 1), skip_group_check=True)
                mm.then_inc(pv_done, 1)

            def group_sum(g, bank):
                chunks = GROUPS[g][0]
                pe.wait_ge(group_sq, max(SQUARES.index(ch) for ch in chunks) + 1)
                for ch in chunks:
                    mm = pe.matmul(PS[:, bank, :], ONES[:], SQ[:, ch, :], start=(ch == chunks[0]), stop=(ch == chunks[-1]))
                mm.then_inc(group_sums, 1)

            scores(0)
            for u in range(len(UNITS)):
                if u + 1 < len(UNITS):
                    scores(u + 1)
                jobs = UNIT_JOBS[u]
                if jobs:
                    project(jobs[0])
                middle(u)
                if len(jobs) > 1:
                    project(jobs[1])
                if 11 <= u < 15:
                    row_total(u - 11)
                if u == 15:
                    pe.wait_ge(rows_kept, 4)
                    group_sum(0, 6)
                    group_sum(1, 7)
                values(u)
            pe.wait_ge(wout_in, 16)
            order = [ch for chunks, _ in GROUPS for ch in chunks]

            def turn_tile(t):
                pe.wait_ge(xn_ready, NT + t + 1)
                if t >= 1:
                    pe.wait_ge(kept, 2 * C + t)
                for j in range(C):
                    mm = pe.transpose(PS[:, 6 + j // 4, (j % 4) * P:(j % 4 + 1) * P], XN2[:, t, j:D:C], ID[:])
                mm.then_inc(turned, 1)

            def logits(t):
                pe.wait_ge(kept, 2 * C + t + 1)
                for k in range(C):
                    mm = pe.matmul(PS[:, 5, t * E:(t + 1) * E], H2T[:, k, t * P:(t + 1) * P], WR[:, k, :],
                                   start=(k == 0), stop=(k == C - 1))
                if t == NT - 1:
                    mm.then_inc(logits_done, 1)

            for t in range(NT):
                if t >= 3:
                    pe.wait_ge(wout_kept, t - 2)
                for n, k in enumerate(order):
                    if t == 0 and n == 1:
                        group_sum(2, 0)
                    if t == 0:
                        pe.wait_ge(kept, C + n + 1)
                    for h in range(2):
                        mm = pe.matmul(PS[:, 2 * ((t + 1) % 3) + h, :], MT[:, k, t * P:(t + 1) * P],
                                       WOUT[:, k, h * 512:(h + 1) * 512], start=(n == 0), stop=(n == C - 1))
                mm.then_inc(wout_done, 1)
                if t >= 1:
                    turn_tile(t - 1)
            pe.wait_ge(wr_in, 32)
            for t in range(NT - 1):
                logits(t)
            turn_tile(NT - 1)
            logits(NT - 1)
            pe.wait_ge(ones_kept, 1)
            pe.wait_ge(mask_ready, 1)
            for t in range(NT):
                for s in range(t + 1):
                    mm = pe.matmul(PS[:, 7, t * E:(t + 1) * E], (SLTR if s == t else ONESR)[:], MASK[:, s, :],
                                   start=(s == 0), stop=(s == t))
            for s in range(NT):
                mm = pe.matmul(PS[:, 7, P:P + E], ONESR[:], MASK[:, s, :], start=(s == 0), stop=(s == NT - 1))
            mm.then_inc(ranks_done, 1)

            pe.wait_ge(slots_placed, 1)
            for n in range(NT * TOPK):
                mm = pe.matmul(PS[:, 6, 0:96], SLOTS[:, n, :], WHO[:, n].rearrange("p a i -> p (a i)"),
                               start=(n == 0), stop=(n == NT * TOPK - 1))
            mm.then_inc(slots_ready, 1)

            def turn_rows(n):
                pe.wait_ge(gathered, n * 16)
                for j in range(C):
                    mm = pe.transpose(PS[:, j // 4, (j % 4) * P:(j % 4 + 1) * P], XG[:, j:D:C], ID[:])
                mm.then_inc(rows_turned, 1)

            def chunk(i, k, xh, xl, banks, js, first, last):
                pe.wait_ge(lo_done, i * CHUNKS + (k + 7))
                b = (4 + k) % 3
                for a, j in enumerate(js):
                    for g in range(2):
                        o = (2 * a + g) * 512
                        for n, (xs, ws) in enumerate(((xh, WH), (xl, WH), (xh, WL))):
                            mm = pe.matmul(PS[:, banks + g, :], xs[:, j, :], ws[:, b, o:o + 512],
                                           start=(first and a == 0 and n == 0),
                                           stop=(last and a == 1 and n == 2), skip_group_check=True)
                mm.then_inc(pe_chunk, 1)

            def turn_act(h, n):
                pe.wait_ge(act_ready, n)
                for r in range(4):
                    mm = pe.transpose(PS[:, 2 + 2 * h, r * P:(r + 1) * P], AC[:, h, r:512:4], ID[:])
                mm.then_inc(act_turned, 1)

            def gate_up(i, k0, h, n, turned_half=None):
                for q in range(4):
                    if q == 3 and turned_half is not None:
                        turn_act(*turned_half)
                    chunk(i, k0 + q, XH, XL, 2 + 2 * h, (2 * q, 2 * q + 1), q == 0, False)
                for g in range(2):
                    o = g * D + h * 512
                    mm = pe.matmul(PS[:, 2 + 2 * h + g, :], SEL[:], BR[:, o:o + 512], start=False, stop=True,
                                   skip_group_check=True)
                mm.then_inc(gu_done, 1)

            def down(i, k0, h):
                pe.wait_ge(al_ready, i * 2 + (h + 1))
                if h == 0:
                    pe.wait_ge(y_kept, i + 1)
                    for g in range(2):
                        o = 2 * D + g * 512
                        mm = pe.matmul(PS[:, 6 + g, :], SEL[:], BR[:, o:o + 512], start=True, stop=False,
                                       skip_group_check=True)
                    mm.then_inc(sel_used, 1)
                for q in range(2):
                    chunk(i, k0 + q, AH[:, h], AL[:, h], 6, (2 * q, 2 * q + 1), False, h == 1 and q == 1)

            pe.wait_ge(bias_split, 1)
            pe.wait_ge(tables_ready, 1)
            last_tile = pe.value_load(LAST[0:1, 0:1], min_val=15, max_val=MAX_TILES - 1)
            turn_rows(1)
            pe.wait_ge(xl_ready, 1)
            pe.wait_ge(sel_ready, 1)
            gate_up(0, -4, 0, 1)
            with pe.Fori(0, last_tile) as i:
                gate_up(i, 0, 1, i * 2 + 2, (0, i * 2 + 1))
                turn_rows(i + 2)
                down(i, 4, 0)
                turn_act(1, i * 2 + 2)
                pe.wait_ge(xl_ready, i + 2)
                pe.wait_ge(sel_ready, i + 2)
                gate_up(i, 6, 0, i * 2 + 3)
                down(i, 10, 1)
            i = last_tile
            gate_up(i, 0, 1, i * 2 + 2, (0, i * 2 + 1))
            down(i, 4, 0)
            turn_act(1, i * 2 + 2)
            down(i, 6, 1)

        @block.scalar
        def _(act):
            done = [0]

            def step(ins):
                done[0] += 1
                ins.then_inc(act_step, 1)
                act.wait_ge(act_step, done[0])

            act.dma_start(BANDH[:], onehot).then_inc(band_in, 16)
            act.dma_start(BANDT, table).then_inc(band_in, 16)
            act.dma_start(BANDM[:], masks).then_inc(band_in, 16)
            act.wait_ge(c_in, 32)
            act.activation(sg, cT, ACT.Sigmoid).then_inc(roots, 1)

            def norm_sums(src, n, junk):
                for t in range(NT):
                    last = act.activation(junk[:, t, :], src[:, t, :], ACT.Square, accum_out=ss[:, t:t + 1])
                last.then_inc(squares, 1)
                act.wait_ge(dve_mean, n)
                act.activation(rs, rs, ACT.Sqrt).then_inc(roots, 1)

            act.wait_ge(x_in, 16)
            norm_sums(X, 1, XN)
            act.wait_ge(band_kept, 1)
            act.dma_start(band_dram, BANDS[:].unsqueeze(1).broadcast_to([12, P, BAND])).then_inc(band_out, 16)
            def keep(job):
                n = JOBS.index(job)
                if job[0] == "v":
                    _, width, o, t0, tiles = job[1]
                    act.wait_ge(proj_done, n + 1)
                    act.activation(V[:, t0:t0 + tiles, o:o + width],
                                   PS[:, 6 + n % 2, 0:tiles * width].rearrange("p (t n) -> p t n", t=tiles),
                                   ACT.Copy).then_inc(v_kept, 1)

            for job in FIRST_JOBS:
                keep(job)
            act.wait_ge(misc_in, 48)

            def first(u):
                kind, h = UNITS[u]
                s = u % 2
                a, b = UB1[s], UB2[s]
                if kind == "sb":
                    act.wait_ge(scores_done, u + 1)
                    av = a[:].rearrange("p (t n) -> p t n", t=NT)
                    for t in range(NT):
                        last = act.activation(av[:, t, t * P:T], stick(u, t), ACT.Abs)
                    step(last)
                    for t in range(NT):
                        last = act.activation(av[:, t, t * P:T], av[:, t, t * P:T], ACT.Exp, scale=-1.0)
                    step(last)
                    for t in range(NT):
                        last = act.activation(av[:, t, t * P:T], av[:, t, t * P:T], ACT.Ln, bias=1.0)
                    last.then_inc(logs_ready, 1)
                else:
                    act.wait_ge(max_ready, nth(u, "sw", "mb"))
                    wide = 256 if kind == "sw" else T
                    av = a[:, 0:NT * wide].rearrange("p (t n) -> p t n", t=NT)
                    for t in range(NT):
                        lo, hi = ((0 if t else P), 256) if kind == "sw" else (0, (t + 1) * P)
                        last = act.activation(av[:, t, lo:hi], av[:, t, lo:hi], ACT.Exp, bias=negm[s][:, t:t + 1],
                                              accum_out=den[s][:, t:t + 1])
                    if kind == "sw":
                        last = act.activation(esink[s], negm[s], ACT.Exp, bias=sinkb[:, h:h + 1])
                    last.then_inc(probs_ready, 1)

            def second(u):
                kind, h = UNITS[u]
                s = u % 2
                a, b = UB1[s], UB2[s]
                if kind == "sb":
                    act.wait_ge(sums_done, nth(u, "sb"))
                    av = a[:].rearrange("p (t n) -> p t n", t=NT)
                    for t in range(NT):
                        last = act.activation(av[:, t, t * P:T], stick(u, t), ACT.Exp)
                    last.then_inc(stick_ready, 1)
                else:
                    act.wait_ge(probs_turned, nth(u, "sw", "mb"))
                    n = 7 if kind == "sw" else 10
                    act.activation(b[:, 0:n * P], PSF[:, BANKS * s:BANKS * s + n * P], ACT.Copy).then_inc(pt_kept, 1)

            def square(ch):
                act.activation(SQ[:, ch, :], MT[:, ch, :], ACT.Square).then_inc(group_sq, 1)

            first(0)
            for u in range(len(UNITS)):
                for job in UNIT_JOBS[u]:
                    keep(job)
                if u in SQUARED:
                    act.wait_ge(set_free, u)
                    for ch in SQUARED[u]:
                        square(ch)
                if u + 1 < len(UNITS) and UNITS[u + 1][0] == "sb":
                    first(u + 1)
                second(u)
                if u + 1 < len(UNITS) and UNITS[u + 1][0] != "sb":
                    first(u + 1)
            for g in range(3):
                if g == 2:
                    act.wait_ge(set_free, len(UNITS))
                    square(5)
                act.wait_ge(group_mean, g + 1)
                act.activation(RSG[:, g, :], RSG[:, g, :], ACT.Sqrt).then_inc(group_roots, 1)
            act.wait_ge(bias_split, 1)
            act.activation(SLTR[:], SLT[:], ACT.Copy)
            act.activation(ONESR[:], ONES[:], ACT.Copy).then_inc(ones_kept, 1)
            for t in range(NT):
                act.wait_ge(wout_kept, t + 1)
                act.activation(XN2[:, t, :], XB[:, t, :], ACT.Square, accum_out=ss[:, t:t + 1]).then_inc(squares, 1)
                act.wait_ge(dve_mean, 2 + t)
                act.activation(rs[:, t:t + 1], rs[:, t:t + 1], ACT.Sqrt).then_inc(roots, 1)
            act.wait_ge(max_ready, SOFT_UNITS + 1)
            act.activation(EXPJ, LM, ACT.Exp).then_inc(probs_ready, 1)

            act.wait_ge(routed, 1)
            last_tile = act.value_load(LAST[0:1, 0:1], min_val=15, max_val=MAX_TILES - 1)
            act.wait_ge(h2_out, 16 * NT)

            act.sem_inc(y_kept, 1)
            act.sem_inc(y_free, 1)

            def hi(i, k):
                slot, b = (4 + k) % RING, (4 + k) % 3
                act.wait_ge(ring_in[slot], i * 32 + 16 * ((4 + k) // RING + 1))
                if not (isinstance(i, int) and 4 + CHUNKS * i + k < 3):
                    act.wait_ge(pe_chunk, i * CHUNKS + (k + 2))
                act.activation(WH[:, b, :], RINGB[:, slot, :], ACT.Copy).then_inc(hi_done, 1)

            def sig(n):
                act.wait_ge(gate_ready, n)
                act.activation(SG[:], GC[:], ACT.Sigmoid, scale=ALPHA).then_inc(sig_ready, 1)

            def keep_turned(h, n):
                act.wait_ge(act_turned, n)
                act.activation(AH[:, h].rearrange("p r m -> p (r m)"), PS[:, 2 + 2 * h, :], ACT.Copy
                               ).then_inc(ah_ready, 1)

            def keep_gathered(n):
                act.wait_ge(rows_turned, n)
                act.activation(XH[:].rearrange("p j m -> p (j m)"), PSF[:, 0:D], ACT.Copy).then_inc(xh_ready, 1)

            def keep_y(i, k):
                act.wait_ge(pe_chunk, i * CHUNKS + (k + 5))
                act.wait_ge(y_free, i + 1)
                act.activation(Y[:], PSF[:, 6 * 512:8 * 512], ACT.Copy).then_inc(y_kept, 1)

            for k in range(-4, -1):
                hi(0, k)
            keep_gathered(1)
            for k in range(-1, 1):
                hi(0, k)
            sig(1)
            for k in range(1, 3):
                hi(0, k)
            with act.Fori(0, last_tile) as i:
                hi(i, 3)
                hi(i, 4)
                hi(i, 5)
                keep_turned(0, i * 2 + 1)
                sig(i * 2 + 2)
                hi(i, 6)
                keep_gathered(i + 2)
                hi(i, 7)
                hi(i, 8)
                keep_turned(1, i * 2 + 2)
                hi(i, 9)
                hi(i, 10)
                hi(i, 11)
                sig(i * 2 + 3)
                hi(i, 12)
                hi(i, 13)
                hi(i, 14)
                keep_y(i, 11)
            i = last_tile
            hi(i, 3)
            hi(i, 4)
            hi(i, 5)
            keep_turned(0, i * 2 + 1)
            sig(i * 2 + 2)
            hi(i, 6)
            keep_turned(1, i * 2 + 2)
            hi(i, 7)
            keep_y(i, 7)
            def weigh(t):
                act.wait_ge(rows_in[t], 16)
                act.activation(AC2[:, t, :], GR[:, t, 0, :], ACT.Copy, scale=WJ[:, t, 0:1]).then_inc(first_ready, 1)

            weigh(0)
            for t in range(NT):
                if t + 1 < NT:
                    weigh(t + 1)
                act.wait_ge(sum_ready, t + 1)
                act.activation(FJ[:, t, :], AC2[:, t, :], ACT.Square,
                               accum_out=ss[:, t:t + 1]).then_inc(squares, 1)
                act.wait_ge(dve_mean, 2 + NT + t)
                act.activation(rs[:, t:t + 1], rs[:, t:t + 1], ACT.Sqrt).then_inc(roots, 1)

        @block.vector
        def _(v):
            done = [0]

            def step(ins):
                done[0] += 1
                ins.then_inc(dve_step, 1)
                v.wait_ge(dve_step, done[0])

            v.wait_ge(roots, 1)
            v.tensor_tensor(cS, cT, sg, ALU.mult).then_inc(c_silu, 1)

            v.wait_ge(band_done, 1)
            v.wait_ge(band_in, 48)
            v.tensor_tensor(BANDS[:], PS[0:12, 6, 0:BAND], BANDM[:], ALU.add).then_inc(band_kept, 1)
            def rows_normed(n_sq, n_mean, n_root, src, dst):
                v.wait_ge(squares, n_sq)
                v.tensor_scalar(rs, ss, 1.0 / D, EPS, ALU.mult, ALU.add).then_inc(dve_mean, 1)
                v.wait_ge(roots, n_root)
                step(v.reciprocal(rs, rs))
                for t in range(NT):
                    v.tensor_scalar(dst[:, t, :], src[:, t, :], rs[:, t:t + 1], None, ALU.mult).then_inc(xn_ready, 1)

            rows_normed(1, 1, 2, X, XN)

            def add_chunk(n):
                m = n - 4
                vec, part, width = (n // 2, n % 2, 512) if n < 4 else (2 + m // 4, m % 4, 256)
                buf = SUMS[vec][1][:, part * width:(part + 1) * width]
                w = (MB if n < 4 else MB2)[:, n % 2]
                v.wait_ge((mod_in if n < 4 else row_in)[n % 2], 16 * ((n if n < 4 else m) // 2 + 1))
                v.wait_ge(mod_bias, 16 * len(SUMS))
                v.wait_ge(c_silu, 1)
                for k in range(C):
                    last = v.scalar_tensor_tensor(out=buf, in0=w[:, k, :], scalar=cS[:, k:k + 1], in1=buf,
                                                  op0=ALU.mult, op1=ALU.add)
                    if k < C - 1:
                        step(last)
                last.then_inc(mod_used, 1)
                if (part + 1) * width == D:
                    v.wait_ge(mod_used, n + 1)
                    v.sem_inc(summed, 1)

            for n in range(4):
                add_chunk(n)
            v.wait_ge(totals, 1)
            v.tensor_copy(SH1, PS[:, 7, C:2 * C])
            step(v.scalar_tensor_tensor(out=G1, in0=PS[:, 7, 0:C], scalar=1.0, in1=gmixc, op0=ALU.add, op1=ALU.mult))
            v.wait_ge(band_out, 16)
            for j in range(C):
                v.wait_ge(turned, j + 1)
                v.tensor_scalar(HT[:, j, :], PS[:, j % 6, :], G1[:, j:j + 1], SH1[:, j:j + 1], ALU.mult, ALU.add
                                ).then_inc(kept, 1)
            def keep(job):
                n = JOBS.index(job)
                kind, blk = job
                if kind == "qk":
                    v.wait_ge(proj_done, n + 1)
                    q = blk in (0, 1, 4, 5, 6, 7, 9, 10)
                    v.tensor_scalar(QKT[:, blk, :], PS[:, 6 + n % 2, :], HD ** -0.5 if q else 1.0, None, ALU.mult
                                    ).then_inc(q_kept, 1)

            def keep_row(r):
                name = ROWS[r][0]
                v.wait_ge(totals, r + 2)
                v.tensor_scalar(ROW[name][:], PSF[:, 6 * 512:8 * 512], 1.0 if name == "sc2" else 0.0, None, ALU.add
                                ).then_inc(rows_kept, 1)

            for job in FIRST_JOBS:
                keep(job)
            v.wait_ge(band_in, 64)
            v.wait_ge(misc_in, 48)

            def first(u):
                kind, h = UNITS[u]
                s = u % 2
                c0 = BANKS * s
                a, b = UB1[s], UB2[s]
                if kind == "sb":
                    v.wait_ge(logs_ready, nth(u, "sb"))
                    av = a[:].rearrange("p (t n) -> p t n", t=NT)
                    bv = b[:].rearrange("p (t n) -> p t n", t=NT)
                    for t in range(NT):
                        last = v.scalar_tensor_tensor(out=bv[:, t, t * P:T], in0=stick(u, t), scalar=0.0,
                                                      in1=av[:, t, t * P:T], op0=ALU.max, op1=ALU.add)
                    last.then_inc(drop_ready, 1)
                    return
                v.wait_ge(scores_done, u + 1)
                if kind == "sw":
                    av = a[:, 0:NT * 256].rearrange("p (t n) -> p t n", t=NT)
                    o = c0 + SW_AT[0]
                    v.tensor_tensor(av[:, 0, P:256], PSF[:, o:o + P], BT[:, h, P:256], ALU.add)
                    step(v.tensor_tensor(av[:, 1:NT, :], PSF[:, c0:c0 + 768].rearrange("p (t n) -> p t n", t=NT - 1),
                                         BT[:, h, :].unsqueeze(1).broadcast_to([P, NT - 1, 256]), ALU.add))
                    v.tensor_reduce(mx[s][:, 0:1], av[:, 0, P:256], AX, ALU.max)
                    step(v.tensor_reduce(mx[s][:, 1:NT], av[:, 1:NT, :], AX, ALU.max))
                    v.tensor_scalar(negm[s], mx[s], sinkb[:, h:h + 1], -1.0, ALU.max, ALU.mult).then_inc(max_ready, 1)
                else:
                    av = a[:].rearrange("p (t n) -> p t n", t=NT)
                    for t in range(NT):
                        lo = max(t - 1, 0) * P
                        o = c0 + MB_AT[t]
                        last = v.tensor_tensor(av[:, t, lo:(t + 1) * P], PSF[:, o + lo:o + (t + 1) * P],
                                               BT[:, 8 + h, (0 if t else P):256], ALU.add)
                        if t >= 2:
                            last = v.tensor_scalar(av[:, t, 0:lo], PSF[:, o:o + lo], farb[:, h:h + 1], None, ALU.add)
                    step(last)
                    for t in range(NT):
                        last = v.tensor_reduce(mx[s][:, t:t + 1], av[:, t, 0:(t + 1) * P], AX, ALU.max)
                    step(last)
                    v.tensor_scalar(negm[s], mx[s], -1.0, None, ALU.mult).then_inc(max_ready, 1)

            def scale(u):
                kind, h = UNITS[u]
                s = u % 2
                if kind == "sb":
                    return
                v.wait_ge(probs_ready, nth(u, "sw", "mb"))
                if kind == "sw":
                    step(v.tensor_tensor(den[s], den[s], esink[s], ALU.add))
                step(v.reciprocal(rden[s], den[s]))
                wide = 256 if kind == "sw" else T
                av = UB1[s][:, 0:NT * wide].rearrange("p (t n) -> p t n", t=NT)
                for t in range(NT):
                    lo, hi = ((0 if t else P), 256) if kind == "sw" else (0, (t + 1) * P)
                    last = v.tensor_scalar(av[:, t, lo:hi], av[:, t, lo:hi], rden[s][:, t:t + 1], None, ALU.mult)
                last.then_inc(probs_scaled, 1)

            def mean_squares(g):
                v.wait_ge(group_sums, g + 1)
                v.tensor_scalar(RSG[:, g, :], PS[:, (6, 7, 0)[g], :], 1.0 / GROUPS[g][1], EPS, ALU.mult, ALU.add
                                ).then_inc(group_mean, 1)

            def group_norm(g):
                v.wait_ge(group_roots, g + 1)
                step(v.reciprocal(RSG[:, g, :], RSG[:, g, :]))
                for ch in GROUPS[g][0]:
                    v.scalar_tensor_tensor(out=MT[:, ch, :], in0=MT[:, ch, :], scalar=ggrc[:, ch:ch + 1],
                                           in1=RSG[:, g, :], op0=ALU.mult, op1=ALU.mult).then_inc(kept, 1)

            def last_of(u):
                kind, h = UNITS[u]
                p0 = 64 * (h % 2)
                v.wait_ge(pv_done, u + 1)
                v.tensor_copy(MT[p0:p0 + 64, chunk_of(kind, h), :], PS[p0:p0 + 64, 3 * (u % 2), :]).then_inc(set_free, 1)

            first(0)
            for u in range(len(UNITS)):
                scale(u)
                if u + 1 < len(UNITS):
                    first(u + 1)
                for job in UNIT_JOBS[u][0:1]:
                    keep(job)
                if 3 <= u < 11:
                    add_chunk(4 + 2 * (u - 3))
                    add_chunk(5 + 2 * (u - 3))
                for job in UNIT_JOBS[u][1:]:
                    keep(job)
                if 11 <= u < 15:
                    keep_row(u - 11)
                if u == 15:
                    mean_squares(0)
                    mean_squares(1)
                last_of(u)
            group_norm(0)
            group_norm(1)
            mean_squares(2)
            group_norm(2)
            v.wait_ge(bias_in, 64)
            step(v.tensor_scalar(BW[:, D:2 * D], BW[:, D:2 * D], 1.0, None, ALU.add))
            v.tensor_copy(BR[0:32, :], BW[0:32, :])
            step(v.tensor_copy(BHT[32:64, :], BW[32:64, :]))
            v.tensor_tensor(BR[32:64, :], BW[32:64, :], BHT[32:64, :].bitcast(F32), ALU.subtract).then_inc(bias_split, 1)
            v.wait_ge(x_back, 16)
            v.wait_ge(g_ffn_in, 16)
            step(v.tensor_tensor(ROW["sc2"][:], ROW["sc2"][:], GFFN[:], ALU.mult))
            for t in range(NT):
                v.wait_ge(wout_done, t + 1)
                b0 = 2 * ((t + 1) % 3)
                step(v.tensor_tensor(TMP[t % 2][:], PSF[:, b0 * 512:b0 * 512 + D], ROW["gt1"][:], ALU.mult))
                v.tensor_tensor(XB[:, t, :], XB[:, t, :], TMP[t % 2][:], ALU.add).then_inc(wout_kept, 1)
                v.wait_ge(squares, 2 + t)
                v.tensor_scalar(rs[:, t:t + 1], ss[:, t:t + 1], 1.0 / D, EPS, ALU.mult, ALU.add).then_inc(dve_mean, 1)
                v.wait_ge(roots, 3 + t)
                step(v.reciprocal(rs[:, t:t + 1], rs[:, t:t + 1]))
                step(v.scalar_tensor_tensor(out=XN2[:, t, :], in0=XB[:, t, :], scalar=rs[:, t:t + 1],
                                            in1=ROW["sc2"][:], op0=ALU.mult, op1=ALU.mult))
                v.tensor_tensor(XN2[:, t, :], XN2[:, t, :], ROW["sh2"][:], ALU.add).then_inc(xn_ready, 1)
                v.wait_ge(turned, C + t + 1)
                v.tensor_copy(H2T[:, :, t * P:(t + 1) * P],
                              PSF[:, 6 * 512:8 * 512].rearrange("p (j m) -> p j m", j=C)).then_inc(kept, 1)
            v.wait_ge(logits_done, 1)
            step(v.tensor_tensor(L, PS[:, 5, 0:P].rearrange("p (t e) -> p t e", t=NT),
                                 BRT[:].unsqueeze(1).broadcast_to([P, NT, E]), ALU.add))
            for t in range(NT):
                last = v.max(M8[:, t, :], L[:, t, :])
            step(last)
            for t in range(NT):
                last = v.max_index(I8[:, t, :], M8[:, t, :], L[:, t, :])
            step(last)
            v.tensor_tensor(LM, M8, M8[:, :, 0:1].broadcast_to([P, NT, 8]), ALU.subtract).then_inc(max_ready, 1)
            step(v.tensor_copy(IF, I8))
            v.wait_ge(iotas, 1)
            step(v.tensor_tensor(OH, IF[:, :, 0:TOPK].unsqueeze(3).broadcast_to([P, NT, TOPK, E]),
                                 IOTAE.unsqueeze(1).unsqueeze(1).broadcast_to([P, NT, TOPK, E]), ALU.is_equal))
            step(v.tensor_tensor(MK2, OH[:, :, 0, :], OH[:, :, 1, :], ALU.add))
            step(v.tensor_tensor(MK3, OH[:, :, 2, :], OH[:, :, 3, :], ALU.add))
            v.tensor_tensor(MASK[:], MK2, MK3, ALU.add).then_inc(mask_ready, 1)
            v.wait_ge(probs_ready, SOFT_UNITS + 1)
            step(v.tensor_reduce(SUM4, EXPJ[:, :, 0:TOPK], AX, ALU.add))
            step(v.reciprocal(SUM4, SUM4))
            v.tensor_tensor(WJ[:], EXPJ, SUM4.unsqueeze(2).broadcast_to([P, NT, 8]), ALU.mult)
            v.wait_ge(ranks_done, 1)
            step(v.tensor_copy(CNT, PS[:, 7, P:P + E]))
            step(v.tensor_scalar(TL, CNT, 0.0, None, ALU.is_gt))
            for full in range(1, NT):
                step(v.scalar_tensor_tensor(out=TL, in0=CNT, scalar=float(full * P), in1=TL, op0=ALU.is_gt, op1=ALU.add))
            step(v.tensor_scalar(TL[:, 0:1], TL[:, 0:1], 1.0, None, ALU.max))
            step(v.tensor_copy(TEND[0], TL))
            k, n = 0, 1
            while n < E:
                v.tensor_copy(TEND[1 - k][:, 0:n], TEND[k][:, 0:n])
                step(v.tensor_tensor(TEND[1 - k][:, n:E], TEND[k][:, n:E], TEND[k][:, 0:E - n], ALU.add))
                k, n = 1 - k, 2 * n
            tend = TEND[k]
            step(v.tensor_tensor(TSTART, tend, TL, ALU.subtract))
            step(v.scalar_tensor_tensor(out=SLOT, in0=TSTART.unsqueeze(1).broadcast_to([P, NT, E]), scalar=float(P),
                                        in1=PS[:, 7, 0:P].rearrange("p (t e) -> p t e", t=NT),
                                        op0=ALU.mult, op1=ALU.add))
            step(v.tensor_tensor(OH, OH, SLOT.unsqueeze(2).broadcast_to([P, NT, TOPK, E]), ALU.mult))
            step(v.tensor_reduce(SJ, OH, AX, ALU.add))
            NC = NT * TOPK
            sjf = SJ.rearrange("p t j -> p (t j)")
            step(v.tensor_tensor(PAST[:], sjf.unsqueeze(2).broadcast_to([P, NC, 48]),
                                 TILEV[:].unsqueeze(1).broadcast_to([P, NC, 48]), ALU.is_ge))
            step(v.tensor_reduce(TA[:], PAST[:], AX, ALU.add))
            step(v.scalar_tensor_tensor(out=MA[:], in0=TA[:], scalar=float(-P), in1=sjf, op0=ALU.mult, op1=ALU.add))
            v.tensor_tensor(INT[:], TA[:].unsqueeze(2).broadcast_to([P, NC, 48]),
                            IOTA[:, 0:48].unsqueeze(1).broadcast_to([P, NC, 48]), ALU.is_equal)
            for n in range(NC):
                last = v.tensor_scalar(SLOTS[:, n, :], IOTA[:], MA[:, n:n + 1], None, ALU.is_equal)
            step(last)
            v.tensor_tensor(WHO[:, :, 0, :], INT[:], TOKV[:].unsqueeze(2).broadcast_to([P, NC, 48]), ALU.mult)
            v.tensor_tensor(WHO[:, :, 1, :], INT[:], ROWV[:].unsqueeze(2).broadcast_to([P, NC, 48]), ALU.mult
                            ).then_inc(slots_placed, 1)
            step(v.tensor_tensor(TT, IOTA48.unsqueeze(2).broadcast_to([1, 48, E]), tend[0:1].unsqueeze(1).broadcast_to([1, 48, E]), ALU.is_ge))
            step(v.tensor_reduce(TE, TT, AX, ALU.add))
            v.tensor_scalar(TILE_E[:], TE, float(E - 1), None, ALU.min)
            v.tensor_scalar(LAST[0:1, 0:1], tend[0:1, E - 1:E], -1.0, None, ALU.add).then_inc(routed, 1)
            v.wait_ge(slots_ready, 1)
            step(v.tensor_scalar(EMPTY[:], PS[:, 6, 48:96], 0.0, float(2 * T * TOPK), ALU.is_equal, ALU.mult))
            v.tensor_tensor(TOKF[:, 0, :], PS[:, 6, 0:48], EMPTY[:], ALU.add)
            v.scalar_tensor_tensor(out=TOKF[:, 1, :], in0=PS[:, 6, 48:96], scalar=-1.0, in1=EMPTY[:],
                                   op0=ALU.add, op1=ALU.add).then_inc(tables_ready, 1)

            last_tile = v.value_load(LAST[0:1, 0:1], min_val=15, max_val=MAX_TILES - 1)
            v.sem_inc(lo_done, 2)

            def lo(i, k):
                slot, b = (4 + k) % RING, (4 + k) % 3
                v.wait_ge(hi_done, i * CHUNKS + (4 + k + 1))
                v.tensor_tensor(WL[:, b, :], RINGB[:, slot, :], WH[:, b, :].bitcast(F32), ALU.subtract
                                ).then_inc(lo_done, 1)

            def clip(h, n, first_=False):
                v.wait_ge(gu_done, n)
                if not first_:
                    v.wait_ge(act_ready, n - 1)
                b = 2 + 2 * h
                v.tensor_scalar(GC[:], PS[:, b, :], LIMIT, None, ALU.min).then_inc(gate_ready, 1)
                v.tensor_scalar(UC[:], PS[:, b + 1, :], LIMIT + 1.0, 1.0 - LIMIT, ALU.min, ALU.max).then_inc(up_ready, 1)

            def keep_turned(h, n):
                v.wait_ge(ah_ready, n)
                v.tensor_tensor(AL[:, h].rearrange("p r m -> p (r m)"), PS[:, 2 + 2 * h, :],
                                AH[:, h].rearrange("p r m -> p (r m)").bitcast(F32), ALU.subtract).then_inc(al_ready, 1)

            def keep_gathered(n):
                v.wait_ge(xh_ready, n)
                v.tensor_tensor(XL[:].rearrange("p j m -> p (j m)"), PSF[:, 0:D],
                                XH[:].rearrange("p j m -> p (j m)").bitcast(F32), ALU.subtract).then_inc(xl_ready, 1)

            for k in range(-4, -1):
                lo(0, k)
            keep_gathered(1)
            for k in range(-1, 1):
                lo(0, k)
            clip(0, 1, True)
            for k in range(1, 3):
                lo(0, k)
            with v.Fori(0, last_tile) as i:
                lo(i, 3)
                lo(i, 4)
                lo(i, 5)
                keep_turned(0, i * 2 + 1)
                clip(1, i * 2 + 2)
                lo(i, 6)
                keep_gathered(i + 2)
                lo(i, 7)
                lo(i, 8)
                keep_turned(1, i * 2 + 2)
                lo(i, 9)
                lo(i, 10)
                lo(i, 11)
                clip(0, i * 2 + 3)
                lo(i, 12)
                lo(i, 13)
                lo(i, 14)
            i = last_tile
            lo(i, 3)
            lo(i, 4)
            lo(i, 5)
            keep_turned(0, i * 2 + 1)
            clip(1, i * 2 + 2)
            lo(i, 6)
            keep_turned(1, i * 2 + 2)
            lo(i, 7)
            v.wait_ge(misc_in, 64)
            def finish(t):
                v.wait_ge(squares, 2 + NT + t)
                v.tensor_scalar(rs[:, t:t + 1], ss[:, t:t + 1], 1.0 / D, EPS, ALU.mult, ALU.add).then_inc(dve_mean, 1)
                v.wait_ge(roots, 3 + NT + t)
                step(v.reciprocal(rs[:, t:t + 1], rs[:, t:t + 1]))
                v.scalar_tensor_tensor(out=AC2[:, t, :], in0=AC2[:, t, :], scalar=rs[:, t:t + 1], in1=GF[:],
                                       op0=ALU.mult, op1=ALU.mult).then_inc(final_ready, 1)

            for t in range(NT):
                v.wait_ge(rows_in[t], 16)
                v.wait_ge(first_ready, t + 1)
                for j in range(1, TOPK):
                    step(v.scalar_tensor_tensor(out=AC2[:, t, :], in0=GR[:, t, j, :], scalar=WJ[:, t, j:j + 1],
                                                in1=AC2[:, t, :], op0=ALU.mult, op1=ALU.add))
                v.tensor_tensor(AC2[:, t, :], AC2[:, t, :], ROW["gt2"][:], ALU.mult).then_inc(gated_sum, 1)
                if t >= 1:
                    finish(t - 1)
            finish(NT - 1)

        @block.gpsimd
        def _(g):
            done = [0]

            def step(ins):
                done[0] += 1
                ins.then_inc(pool_step, 1)
                g.wait_ge(pool_step, done[0])

            for _, buf in SUMS:
                last = g.memset(buf[:], 0.0)
            last.then_inc(zeroed, 1)
            for m, val in ((ID, 0.0), (NTRI, -1.0), (NONE_, -1.0), (ONES, 1.0), (SLT, 1.0)):
                last = g.memset(m[:], val)
            step(last)
            g.affine_select(out=ID[:], in_=ID[:], compare_op=ALU.not_equal, fill=1.0, base=0,
                            pattern=[[-1, P]], channel_multiplier=1)
            g.affine_select(out=NTRI[:], in_=NTRI[:], compare_op=ALU.is_ge, fill=0.0, base=0,
                            pattern=[[-1, P]], channel_multiplier=1)
            g.affine_select(out=SLT[:], in_=SLT[:], compare_op=ALU.is_gt, fill=0.0, base=0,
                            pattern=[[1, P]], channel_multiplier=-1).then_inc(consts, 1)

            def keep_past(buf):
                ap = bass.AP(buf[:].tensor, 0, [[2048, P], [T + P, NT], [1, P]])
                return g.affine_select(out=ap, in_=ap, compare_op=ALU.is_gt, fill=0.0, base=0,
                                       pattern=[[0, NT], [1, P]], channel_multiplier=-1)

            def first(u):
                if UNITS[u][0] == "sb":
                    g.wait_ge(drop_ready, nth(u, "sb"))
                    keep_past(UB2[u % 2]).then_inc(drop_masked, 1)

            def second(u):
                if UNITS[u][0] == "sb":
                    g.wait_ge(stick_ready, nth(u, "sb"))
                    keep_past(UB1[u % 2]).then_inc(stick_masked, 1)

            first(0)
            for u in range(len(UNITS)):
                if u + 1 < len(UNITS):
                    first(u + 1)
                second(u)
            g.wait_ge(set_free, len(UNITS))
            g.iota(IOTAE, pattern=[[1, E]], base=0, channel_multiplier=0, allow_small_or_imprecise_dtypes=True)
            g.iota(IOTA48, pattern=[[1, 48]], base=0, channel_multiplier=0, allow_small_or_imprecise_dtypes=True)
            g.iota(IOTA[:], pattern=[[1, P]], base=0, channel_multiplier=0, allow_small_or_imprecise_dtypes=True)
            step(g.memset(ID2[:], 0.0))
            for half in range(2):
                step(g.affine_select(out=ID2[:], in_=ID2[:], compare_op=ALU.not_equal, fill=1.0, base=-32 * half,
                                     pattern=[[-1, E]], channel_multiplier=1))
            g.iota(TOKV[:], pattern=[[P, NT], [0, TOPK]], base=0, channel_multiplier=1,
                   allow_small_or_imprecise_dtypes=True)
            g.iota(ROWV[:], pattern=[[P * TOPK, NT], [1, TOPK]], base=1, channel_multiplier=TOPK,
                   allow_small_or_imprecise_dtypes=True)
            g.iota(TILEV[:], pattern=[[P, 48]], base=P, channel_multiplier=0,
                   allow_small_or_imprecise_dtypes=True).then_inc(iotas, 1)
            g.wait_ge(routed, 1)
            last_tile = g.value_load(LAST[0:1, 0:1], min_val=15, max_val=MAX_TILES - 1)

            def gather(i, n):
                if n is not None:
                    g.tensor_copy(TOKC[:, 0:1], TOKF[:, 0, bass.ds(i, 1)]).then_inc(idx_step, 1)
                    g.wait_ge(h2_out, 16 * NT)
                    g.wait_ge(idx_step, n)
                g.indirect_dma_start(XG[:], None, h2_dram,
                                     bass.IndirectOffsetOnAxis(ap=TOKC[:, 0:1], axis=0),
                                     bounds_check=T - 1, oob_is_err=False).then_inc(gathered, 16)

            def scatter(i):
                g.wait_ge(y_kept, i + 2)
                g.tensor_copy(ROWC[:, 0:1], TOKF[:, 1, bass.ds(i, 1)]).then_inc(row_step, 1)
                g.wait_ge(h2_out, 16 * NT)
                g.wait_ge(row_step, i + 2)
                g.indirect_dma_start(ys, bass.IndirectOffsetOnAxis(ap=ROWC[:, 0:1], axis=0), Y[:], None,
                                     bounds_check=T * TOPK - 1, oob_is_err=False).then_inc(y_stored, 16)

            def selector(e):
                g.tensor_copy(SEL[:], ID2[:, bass.ds(e, 1)].broadcast_to([64, P])).then_inc(sel_ready, 1)

            def gated(h, n):
                g.wait_ge(up_ready, n)
                g.wait_ge(gate_ready, n)
                g.tensor_tensor(UC[:], UC[:], GC[:], ALU.mult).then_inc(gated_up, 1)
                g.wait_ge(gated_up, n)
                g.wait_ge(sig_ready, n)
                g.tensor_tensor(AC[:, h], UC[:], SG[:], ALU.mult).then_inc(act_ready, 1)

            e = g.value_load(TILE_E[0:1, 0:1], min_val=0, max_val=E - 1)
            selector(e)
            g.wait_ge(bias_split, 1)
            step(g.memset(XG[:], 0.0))
            g.wait_ge(tables_ready, 1)
            g.sem_inc(row_step, 1)
            step(g.tensor_copy(TOKC[:, 0:1], TOKF[:, 0, 0:1]))
            g.wait_ge(h2_out, 16 * NT)
            gather(0, None)
            g.wait_ge(rows_turned, 1)
            gather(1, 1)
            gated(0, 1)
            with g.Fori(0, last_tile) as i:
                e = g.value_load(TILE_E[0:1, bass.ds(i + 1, 1)], min_val=0, max_val=E - 1)
                g.wait_ge(sel_used, i + 1)
                selector(e)
                g.wait_ge(rows_turned, i + 2)
                gather(i + 2, i + 2)
                gated(1, i * 2 + 2)
                gated(0, i * 2 + 3)
                scatter(i)
                g.wait_ge(y_stored, i * 16 + 16)
                g.sem_inc(y_free, 1)
            i = last_tile
            gated(1, i * 2 + 2)
            scatter(i)
            g.wait_ge(gathered, last_tile * 16 + 32)
            for t in range(NT):
                g.wait_ge(gated_sum, t + 1)
                g.tensor_tensor(AC2[:, t, :], AC2[:, t, :], XB[:, t, :], ALU.add).then_inc(sum_ready, 1)
    return nc


_INS = ["x", "c", "w_in", "w_out", "g_norm_mix", "g_norm_ffn", "g_group", "w_mod", "b_mod", "swa_sinks", "rel_bias",
        "w_router", "b_router", "w_gate_up", "b_gate_up", "w_down", "b_down", "g_final"]


def kernel(**inputs):
    import concourse.bacc as bacc
    from concourse.bass_utils import run_bass_kernel_spmd

    onehot, masks = dist_tables()
    nc = bacc.Bacc("TRN2", target_bir_lowering=False, num_devices=1)
    arrays, args = {}, []
    given = {n: inputs[n] for n in _INS}
    given["onehot"], given["masks"] = onehot, masks
    for name, a in given.items():
        a = np.ascontiguousarray(a)
        arrays[f"in_{name}"] = a
        args.append(nc.dram_tensor(f"in_{name}", a.shape, mybir.dt.from_np(a.dtype), kind="ExternalInput").ap())
    out = nc.dram_tensor("out_dram", (1, T, D), F32, kind="ExternalOutput").ap()
    build(nc, *args, out)
    r = run_bass_kernel_spmd(nc, [arrays], core_ids=[0])
    return r.results[0]["out_dram"]
```
